# Optimizing a Trainium2 kernel written in Bass

```python
import jax, jax.numpy as jnp
from jax import lax
import numpy as np

D_MODEL = 1024
BATCH = 1
SEQ = 1024
DEPTH = 2
DEC_BATCH = 8
DEC_SEQ = 16
PAST_LEN = 512

CHUNK = 64
N_A_LAYERS = DEPTH // 2
N_B_LAYERS = DEPTH - N_A_LAYERS
A_HEADS = 8
A_DQK = D_MODEL // 16
A_DV = D_MODEL // A_HEADS
A_QK_WIDTH = A_HEADS * A_DQK
A_V_WIDTH = A_HEADS * A_DV
A_IN_WIDTH = 2 * A_QK_WIDTH + 2 * A_V_WIDTH + 2 * A_HEADS
GATE_CAP = 15.0
B_HEADS = 16
B_HD = D_MODEL // B_HEADS
Q_BLOCK = 128
KVF_WIDTH = 2 * D_MODEL + B_HEADS
D_FF = ((8 * D_MODEL // 3 + 255) // 256) * 256
EPS = 1e-6

kernel_name = "yoco_mlstm_fox_stream_step"

def rms_norm(x, gain):
    xf = x.astype(jnp.float32)
    y = xf * lax.rsqrt(jnp.mean(xf * xf, axis=-1, keepdims=True) + EPS)
    return (y * gain.astype(jnp.float32)).astype(x.dtype)

def soft_cap(z):
    return GATE_CAP * jnp.tanh(z / GATE_CAP)

def swiglu(xn, w_gu, w_down):
    gate, up = jnp.split(xn @ w_gu, [D_FF], axis=-1)
    return (jax.nn.silu(gate) * up) @ w_down

def mlstm_chunk(carry, blk):
    c, n, m = carry
    q, k, v, li, lf = blk
    L = q.shape[2]
    b = jnp.cumsum(lf, axis=-1)
    causal = jnp.tril(jnp.ones((L, L), dtype=bool))
    dmat = jnp.where(causal, b[..., :, None] - b[..., None, :] + li[..., None, :], -jnp.inf)
    inter = b + m[..., None]
    m_t = jnp.maximum(inter, jnp.max(dmat, axis=-1))
    g = jnp.exp(inter - m_t)
    s = jnp.einsum('bhtd,bhsd->bhts', q, k) * jnp.exp(dmat - m_t[..., None])
    num = g[..., None] * jnp.einsum('bhvd,bhtd->bhtv', c, q) + jnp.einsum('bhts,bhsv->bhtv', s, v)
    den = g * jnp.einsum('bhd,bhtd->bht', n, q) + jnp.sum(s, axis=-1)
    h = num / jnp.maximum(jnp.abs(den), jnp.exp(-m_t))[..., None]
    b_last = b[..., -1]
    w_log = b_last[..., None] - b + li
    m_new = jnp.maximum(b_last + m, jnp.max(w_log, axis=-1))
    g_c = jnp.exp(b_last + m - m_new)
    ws = jnp.exp(w_log - m_new[..., None])
    c_new = g_c[..., None, None] * c + jnp.einsum('bhsv,bhsd->bhvd', ws[..., None] * v, k)
    n_new = g_c[..., None] * n + jnp.einsum('bhs,bhsd->bhd', ws, k)
    return (c_new, n_new, m_new), h

def mlstm_mixer(xn, w_in, b_i, b_f, g_head, w_out, c0, n0, m0):
    f32 = jnp.float32
    bsz, t, _ = xn.shape
    q, k, v, o, ig, fg = jnp.split(xn @ w_in, [A_QK_WIDTH, 2 * A_QK_WIDTH, 2 * A_QK_WIDTH + A_V_WIDTH,
                                              2 * A_QK_WIDTH + 2 * A_V_WIDTH,
                                              2 * A_QK_WIDTH + 2 * A_V_WIDTH + A_HEADS], axis=-1)
    L = min(t, CHUNK)
    nc = t // L

    def to_chunks(z, d):
        return z.astype(f32).reshape(bsz, nc, L, A_HEADS, d).transpose(1, 0, 3, 2, 4)

    def gate_chunks(z):
        return z.reshape(bsz, nc, L, A_HEADS).transpose(1, 0, 3, 2)

    qc = to_chunks(q, A_DQK)
    kc = to_chunks(k, A_DQK) * (A_DQK ** -0.5)
    vc = to_chunks(v, A_DV)
    li = gate_chunks(soft_cap(ig.astype(f32) + b_i.astype(f32)))
    lf = gate_chunks(jax.nn.log_sigmoid(soft_cap(fg.astype(f32) + b_f.astype(f32))))
    (c, n, m), h = lax.scan(mlstm_chunk, (c0.astype(f32), n0.astype(f32), m0.astype(f32)),
                            (qc, kc, vc, li, lf))
    h = h.transpose(1, 0, 3, 2, 4).reshape(bsz, t, A_HEADS, A_DV)
    h = h * lax.rsqrt(jnp.mean(h * h, axis=-1, keepdims=True) + EPS)
    h = h.reshape(bsz, t, A_V_WIDTH) * g_head.astype(f32)
    h = (h * jax.nn.sigmoid(o.astype(f32))).astype(xn.dtype)
    return h @ w_out, c, n, m

def shared_kv(s, g_kv, w_kvf, b_f, g_k):
    bsz, t, _ = s.shape
    k, v, f = jnp.split(rms_norm(s, g_kv) @ w_kvf, [D_MODEL, 2 * D_MODEL], axis=-1)
    k = rms_norm(k.reshape(bsz, t, B_HEADS, B_HD), g_k)
    v = v.reshape(bsz, t, B_HEADS, B_HD)
    logf = jax.nn.log_sigmoid(f.astype(jnp.float32) + b_f.astype(jnp.float32)).astype(s.dtype)
    return k, v, logf

def fox_attend(q, k, v, cum_q, cum_k, q_pos):
    s = jnp.einsum('bqhd,bkhd->bhqk', q, k).astype(jnp.float32) * (B_HD ** -0.5)
    s = s + cum_q.transpose(0, 2, 1)[..., :, None] - cum_k.transpose(0, 2, 1)[..., None, :]
    mask = q_pos[:, None] >= jnp.arange(k.shape[1])[None, :]
    p = jax.nn.softmax(jnp.where(mask, s, -jnp.inf), axis=-1)
    return jnp.einsum('bhqk,bkhd->bqhd', p.astype(v.dtype), v)

def fox_mixer(xn, w_qg, g_q, w_o, k_all, v_all, logf_all):
    bsz, t, _ = xn.shape
    n_past = k_all.shape[1] - t
    q, g = jnp.split(xn @ w_qg, [D_MODEL], axis=-1)
    q = rms_norm(q.reshape(bsz, t, B_HEADS, B_HD), g_q)
    cum = jnp.cumsum(logf_all.astype(jnp.float32), axis=1)
    qb = min(t, Q_BLOCK)
    nb = t // qb

    def block(i):
        start = i * qb
        qi = lax.dynamic_slice_in_dim(q, start, qb, axis=1)
        ci = lax.dynamic_slice_in_dim(cum, n_past + start, qb, axis=1)
        pos = n_past + start + jnp.arange(qb)
        return fox_attend(qi, k_all, v_all, ci, cum, pos)

    o = lax.map(block, jnp.arange(nb))
    o = o.transpose(1, 0, 2, 3, 4).reshape(bsz, t, D_MODEL)
    o = (o.astype(jnp.float32) * jax.nn.sigmoid(g.astype(jnp.float32))).astype(xn.dtype)
    return o @ w_o

def trunk(x, c0, n0, m0, past_k, past_v, past_logf, params):
    (g_mix, g_ffn, w_in_a, b_i_a, b_f_a, g_head_a, w_out_a, g_kv, w_kvf, b_f_b, g_k,
     w_qg_b, g_q_b, w_o_b, w_gu, w_down) = params
    cs, ns, ms = [], [], []
    k_new = v_new = logf_new = None
    k_all = v_all = logf_all = None
    for layer in range(DEPTH):
        h = rms_norm(x, g_mix[layer])
        if layer < N_A_LAYERS:
            y, c, n, m = mlstm_mixer(h, w_in_a[layer], b_i_a[layer], b_f_a[layer], g_head_a[layer],
                                     w_out_a[layer], c0[:, layer], n0[:, layer], m0[:, layer])
            cs.append(c)
            ns.append(n)
            ms.append(m)
        else:
            if layer == N_A_LAYERS:
                k_new, v_new, logf_new = shared_kv(x, g_kv, w_kvf, b_f_b, g_k)
                k_all = jnp.concatenate([past_k.astype(k_new.dtype), k_new], axis=1)
                v_all = jnp.concatenate([past_v.astype(v_new.dtype), v_new], axis=1)
                logf_all = jnp.concatenate([past_logf.astype(logf_new.dtype), logf_new], axis=1)
            j = layer - N_A_LAYERS
            y = fox_mixer(h, w_qg_b[j], g_q_b[j], w_o_b[j], k_all, v_all, logf_all)
        x = x + y
        x = x + swiglu(rms_norm(x, g_ffn[layer]), w_gu[layer], w_down[layer])
    dt = x.dtype
    c_out = jnp.stack(cs, axis=1).astype(dt)
    n_out = jnp.stack(ns, axis=1).astype(dt)
    m_out = jnp.stack(ms, axis=1).astype(dt)
    return x, k_new, v_new, logf_new, c_out, n_out, m_out

def setup_inputs(seed: int = 0) -> dict:
    key = jax.random.key(seed)
    ks = jax.random.split(key, 24)
    f32 = jnp.float32

    def nrm(k, shape, scale=1.0):
        return scale * jax.random.normal(k, shape, f32)

    def w(k, shape, fan_in):
        return jax.random.normal(k, shape, f32) * fan_in ** -0.5

    def gain(k, shape):
        return 1.0 + 0.05 * jax.random.normal(k, shape, f32)

    return dict(
        x_prompt=nrm(ks[0], (BATCH, SEQ, D_MODEL)),
        x_sample=nrm(ks[1], (DEC_BATCH, DEC_SEQ, D_MODEL)),
        cache_k=nrm(ks[2], (DEC_BATCH, PAST_LEN, B_HEADS, B_HD)),
        cache_v=nrm(ks[3], (DEC_BATCH, PAST_LEN, B_HEADS, B_HD)),
        cache_logf=jax.nn.log_sigmoid(jax.random.uniform(ks[4], (DEC_BATCH, PAST_LEN, B_HEADS), f32, 1.0, 4.0)),
        state_c=nrm(ks[5], (DEC_BATCH, N_A_LAYERS, A_HEADS, A_DV, A_DQK), 0.3),
        state_n=nrm(ks[6], (DEC_BATCH, N_A_LAYERS, A_HEADS, A_DQK), 0.3),
        state_m=jax.random.uniform(ks[7], (DEC_BATCH, N_A_LAYERS, A_HEADS), f32, -1.0, 1.0),
        g_mix=gain(ks[8], (DEPTH, D_MODEL)),
        g_ffn=gain(ks[9], (DEPTH, D_MODEL)),
        w_in_a=w(ks[10], (N_A_LAYERS, D_MODEL, A_IN_WIDTH), D_MODEL),
        b_i_a=nrm(ks[11], (N_A_LAYERS, A_HEADS), 0.1),
        b_f_a=jax.random.uniform(ks[12], (N_A_LAYERS, A_HEADS), f32, 3.0, 6.0),
        g_head_a=gain(ks[13], (N_A_LAYERS, A_V_WIDTH)),
        w_out_a=w(ks[14], (N_A_LAYERS, A_V_WIDTH, D_MODEL), A_V_WIDTH),
        g_kv=gain(ks[15], (D_MODEL,)),
        w_kvf=w(ks[16], (D_MODEL, KVF_WIDTH), D_MODEL),
        b_f_b=jax.random.uniform(ks[17], (B_HEADS,), f32, 1.0, 4.0),
        g_k=gain(ks[18], (B_HD,)),
        w_qg_b=w(ks[19], (N_B_LAYERS, D_MODEL, 2 * D_MODEL), D_MODEL),
        g_q_b=gain(ks[20], (N_B_LAYERS, B_HD)),
        w_o_b=w(ks[21], (N_B_LAYERS, D_MODEL, D_MODEL), D_MODEL),
        w_gu=w(ks[22], (DEPTH, D_MODEL, 2 * D_FF), D_MODEL),
        w_down=w(ks[23], (DEPTH, D_FF, D_MODEL), D_FF),
    )

def reference(x_prompt, x_sample, cache_k, cache_v, cache_logf, state_c, state_n, state_m,
              g_mix, g_ffn, w_in_a, b_i_a, b_f_a, g_head_a, w_out_a, g_kv, w_kvf, b_f_b, g_k,
              w_qg_b, g_q_b, w_o_b, w_gu, w_down):
    params = (g_mix, g_ffn, w_in_a, b_i_a, b_f_a, g_head_a, w_out_a, g_kv, w_kvf, b_f_b, g_k,
              w_qg_b, g_q_b, w_o_b, w_gu, w_down)
    bsz = x_prompt.shape[0]
    dt = x_prompt.dtype
    c0 = jnp.zeros((bsz, N_A_LAYERS, A_HEADS, A_DV, A_DQK), jnp.float32)
    n0 = jnp.zeros((bsz, N_A_LAYERS, A_HEADS, A_DQK), jnp.float32)
    m0 = jnp.zeros((bsz, N_A_LAYERS, A_HEADS), jnp.float32)
    empty_kv = jnp.zeros((bsz, 0, B_HEADS, B_HD), dt)
    empty_f = jnp.zeros((bsz, 0, B_HEADS), dt)
    y_prompt, k_p, v_p, logf_p, c_p, n_p, m_p = trunk(x_prompt, c0, n0, m0, empty_kv, empty_kv, empty_f, params)
    y_sample, k_s, v_s, logf_s, c_s, n_s, m_s = trunk(x_sample, state_c, state_n, state_m,
                                                      cache_k, cache_v, cache_logf, params)
    return (y_prompt, y_sample, k_p, v_p, logf_p, c_p, n_p, m_p, k_s, v_s, logf_s, c_s, n_s, m_s)


_drawn_inputs = setup_inputs


def setup_inputs(seed=0):
    import zlib

    import numpy as np

    out = dict(_drawn_inputs(seed))
    spreads = {}
    factors = {'cache_logf': 4.176, 'g_q_b': 8.0}
    for name, (base, spread) in spreads.items():
        noise = np.random.default_rng([zlib.crc32(name.encode()), seed]).standard_normal(out[name].shape)
        drawn = base * np.exp(spread * noise) if base else spread * noise
        out[name] = __import__('jax').numpy.asarray(drawn.astype(out[name].dtype))
    for name, factor in factors.items():
        out[name] = (out[name] * factor).astype(out[name].dtype)
    return out
```

```python
import concourse.bass as bass
from concourse import mybir
from contextlib import ExitStack, contextmanager

fp32 = mybir.dt.float32
fp32r = mybir.dt.float32r
ACT = mybir.ActivationFunctionType
ALU = mybir.AluOpType
AX = mybir.AxisListType

P = 128
D = 1024
SEQ = 1024
DEC_BATCH, DEC_SEQ, PAST = 8, 16, 512
T_ALL = SEQ + DEC_BATCH * DEC_SEQ
NT = T_ALL // P
NP = SEQ // P
KC = D // P
CB = 512
THIRD = T_ALL // 3
A_H, A_QK, A_V = 8, 64, 128
A_PAIRS = A_H // 2
B_H, B_HD = 16, 64
B_PAIRS = B_H // 2
D_FF = 2816
FG = 2
FFN_GROUPS = D_FF // (FG * P)
EPS = 1e-6
CAP = 15.0
NEG = -1e30
A_Q0, A_K0, A_V0, A_O0 = 0, 512, 1024, 2048
PAST_T = PAST // P
DK = PAST + DEC_SEQ


def below(i, n):
    return isinstance(i, int) and i < n


def wait(engine, sem, count):
    if not isinstance(count, int):
        engine.wait_ge(sem, 1)
    engine.wait_ge(sem, count)


def settle(engine, sem):
    engine.sem_inc(sem, 1)


def round_high(pool, g, out, in_):
    ones = g.one[:, :].rearrange("p (a b) -> p a b", a=1).to_broadcast((P, *in_.shape[1:]))
    return pool.tensor_tensor(out, in_, ones, ALU.mult)


class Chain:

    def __init__(self, engine, sem):
        self.engine, self.sem, self.n, self.base = engine, sem, 0, 0

    def link(self, ins):
        self.n += 1
        ins.then_inc(self.sem, 1)
        self.engine.wait_ge(self.sem, self.base + self.n)


def run(engine, count, body, chain=None):
    start = chain.n if chain else 0
    body(0)
    if count > 1:
        with engine.Fori(1, count) as i:
            if chain:
                per = chain.n - start
                chain.base, chain.n = start + i * per, 0
            body(i)
            if chain:
                assert chain.n == per
        if chain:
            chain.base, chain.n = 0, start + count * per


class Scope:

    def __init__(self, nc, tag):
        self.nc, self.tag, self.ctx, self.sems = nc, tag, ExitStack(), []

    def __enter__(self):
        return self

    def __exit__(self, *a):
        if a[0] is not None:
            return
        if self.sems:
            self.nc.clear_and_free_semaphores(self.sems)
            self.nc.all_engine_barrier()
        self.ctx.close()

    def sb(self, name, shape, dt=fp32):
        return self.ctx.enter_context(self.nc.sbuf_tensor(f"{self.tag}_{name}", shape, dt))

    def ps(self, name, shape):
        cols = 1
        for n in shape[1:]:
            cols *= n
        banks = -(-cols // CB)
        whole = self.ctx.enter_context(self.nc.psum_tensor(f"{self.tag}_{name}", [P, banks * CB], fp32))
        letters = "abc"[:len(shape) - 1]
        sizes = {k: n for k, n in zip(letters, shape[1:])}
        return whole[:, 0:cols].rearrange(f"p ({' '.join(letters)}) -> p {' '.join(letters)}", **sizes)

    def sem(self, name):
        self.sems.append(self.nc.alloc_semaphore(f"{self.tag}_{name}"))
        return self.sems[-1]


def spread(ap, n):
    return ap.rearrange("p (h o) -> p h o", o=1).to_broadcast((ap.shape[0], ap.shape[1], n))


def repeat(ap, n):
    return ap.rearrange("p (o d) -> p o d", o=1).to_broadcast((ap.shape[0], n, ap.shape[1]))


def f32(ap):
    return ap.bitcast(fp32)


def setup(nc, g, x_prompt, x_sample):
    with Scope(nc, "setup") as s:
        x_loaded, made, filled = s.sem("x_loaded"), s.sem("made"), s.sem("filled")
        with nc.Block() as block:

            @block.sync
            def _(sp):
                sp.dma_start(g.x[:, 0:NP, :], x_prompt.rearrange("(t p) d -> p t d", p=P)).then_inc(x_loaded, 16)
                sp.dma_start(g.x[:, NP, :], x_sample).then_inc(x_loaded, 16)
                wait(sp, x_loaded, 32)

            @block.gpsimd
            def _(pool):
                pool.memset(g.one[:, :], 1.0).then_inc(filled, 1)
                pool.memset(g.ident[:, :], 0.0).then_inc(filled, 1)
                pool.memset(g.mask_kq[:, :, :], 0.0).then_inc(filled, 1)
                pool.memset(g.mask_qk[:, :], 0.0).then_inc(filled, 1)
                wait(pool, filled, 4)
                pool.affine_select(out=g.ident[:, :], in_=g.ident[:, :], compare_op=ALU.not_equal, fill=1.0,
                                   base=0, pattern=[[-1, P]], channel_multiplier=1).then_inc(made, 1)
                pool.affine_select(out=g.mask_kq[:, :, :], in_=g.mask_kq[:, :, :], compare_op=ALU.is_ge, fill=NEG,
                                   base=0, pattern=[[0, 2], [1, P]], channel_multiplier=-1).then_inc(made, 1)
                pool.affine_select(out=g.mask_qk[:, :], in_=g.mask_qk[:, :], compare_op=ALU.is_ge, fill=NEG,
                                   base=0, pattern=[[-1, P]], channel_multiplier=1).then_inc(made, 1)
                wait(pool, made, 3)


def build_xt(nc, g, xth, xtl, tag, kind, a=None, b=None, gain_row=None):
    SLOTS = 3
    GROUPS = NT // SLOTS
    HV = "p (h v) -> p h v"
    with Scope(nc, tag) as s:
        tok = s.sb("tok", [P, SLOTS, D])
        gain_loaded, tile_made = s.sem("gain_loaded"), s.sem("tile_made")
        transposed, high_done, low_done = s.sem("transposed"), s.sem("high_done"), s.sem("low_done")
        square_done, mean_done, root_done, chain_sem = s.sem("square"), s.sem("mean"), s.sem("root"), s.sem("chain")
        a_loaded = [s.sem(f"a_loaded{i}") for i in range(SLOTS)]
        b_loaded = [s.sem(f"b_loaded{i}") for i in range(SLOTS)]
        psum = [s.ps(f"xt{i}", [P, CB]) for i in range(2 * SLOTS)]
        if kind != "gated":
            gain, junk = s.sb("gain", [P, D]), s.sb("junk", [P, D])
        if kind == "norm":
            ss, rms = s.sb("ss", [P, NT]), s.sb("rms", [P, NT])
        else:
            a_in, b_in = s.sb("a_in", [P, SLOTS, D]), s.sb("b_in", [P, SLOTS, D])
            ss, rms = s.sb("ss", [P, A_H]), s.sb("rms", [P, A_H])
        with nc.Block() as block:

            @block.sync
            def _(sp):
                if kind != "gated":
                    sp.dma_start(gain[:, :], gain_row.to_broadcast((P, D))).then_inc(gain_loaded, 16)
                if kind != "norm":
                    def load(i):
                        for k in range(SLOTS):
                            t = i * SLOTS + k
                            if not below(i, 1):
                                wait(sp, tile_made, t - SLOTS + 1)
                            sp.dma_start(a_in[:, k, :], a[t]).then_inc(a_loaded[k], 16)
                            sp.dma_start(b_in[:, k, :], b[t]).then_inc(b_loaded[k], 16)

                    run(sp, GROUPS, load)
                    for k in range(SLOTS):
                        wait(sp, a_loaded[k], 16 * GROUPS)
                        wait(sp, b_loaded[k], 16 * GROUPS)
                if kind != "gated":
                    wait(sp, gain_loaded, 16)

            @block.scalar
            def _(act):
                if kind == "norm":
                    for t in range(NT):
                        if t:
                            act.wait_ge(square_done, t)
                        act.activation(junk[:, :], g.x[:, t, :], ACT.Square, accum_out=ss[:, t:t + 1]).then_inc(square_done, 1)
                    act.wait_ge(mean_done, 1)
                    act.activation(rms[:, :], ss[:, :], ACT.Sqrt).then_inc(root_done, 1)

                def high_parts(i):
                    for k in range(SLOTS):
                        t = i * SLOTS + k
                        if kind == "mlstm":
                            act.wait_ge(a_loaded[k], i * 16 + 16)
                            if not below(t, 1):
                                act.wait_ge(mean_done, t)
                            act.activation(junk[:, :], a_in[:, k, :], ACT.Square).then_inc(square_done, 1)
                            act.wait_ge(mean_done, t + 1)
                            act.activation(rms[:, :], ss[:, :], ACT.Sqrt).then_inc(root_done, 1)
                        for q in range(2):
                            act.wait_ge(transposed, 2 * t + q + 1)
                            act.activation(xth[:, 4 * q:4 * q + 4, bass.ds(t * P, P)],
                                           psum[2 * k + q][:, :].rearrange("p (c n) -> p c n", n=P), ACT.Copy).then_inc(high_done, 1)

                run(act, GROUPS, high_parts)

            @block.vector
            def _(dve):
                c = Chain(dve, chain_sem)
                if kind == "norm":
                    dve.wait_ge(square_done, NT)
                    dve.tensor_scalar(ss[:, :], ss[:, :], 1.0 / D, EPS, ALU.mult, ALU.add).then_inc(mean_done, 1)
                    dve.wait_ge(root_done, 1)
                    c.link(dve.reciprocal(rms[:, :], rms[:, :]))
                if kind != "gated":
                    dve.wait_ge(gain_loaded, 16)

                def make(i, k):
                    t = i * SLOTS + k
                    if not below(i, 1):
                        dve.wait_ge(transposed, 2 * (t - SLOTS) + 2)
                    if kind == "norm":
                        dve.scalar_tensor_tensor(tok[:, k, :], g.x[:, t, :], rms[:, bass.ds(t, 1)], gain[:, :],
                                                 ALU.mult, ALU.mult).then_inc(tile_made, 1)
                        return
                    dve.wait_ge(a_loaded[k], i * 16 + 16)
                    dve.wait_ge(b_loaded[k], i * 16 + 16)
                    if kind == "gated":
                        dve.tensor_tensor(tok[:, k, :], a_in[:, k, :], b_in[:, k, :], ALU.mult).then_inc(tile_made, 1)
                        return
                    dve.wait_ge(square_done, t + 1)
                    c.link(dve.tensor_reduce(ss[:, :], junk[:, :].rearrange(HV, v=A_V), axis=AX.X, op=ALU.add))
                    dve.tensor_scalar(ss[:, :], ss[:, :], 1.0 / A_V, EPS, ALU.mult, ALU.add).then_inc(mean_done, 1)
                    dve.wait_ge(root_done, t + 1)
                    c.link(dve.reciprocal(rms[:, :], rms[:, :]))
                    c.link(dve.tensor_tensor(tok[:, k, :].rearrange(HV, v=A_V), a_in[:, k, :].rearrange(HV, v=A_V),
                                             spread(rms[:, :], A_V), ALU.mult))
                    c.link(dve.tensor_tensor(tok[:, k, :], tok[:, k, :], gain[:, :], ALU.mult))
                    dve.tensor_tensor(tok[:, k, :], tok[:, k, :], b_in[:, k, :], ALU.mult).then_inc(tile_made, 1)

                def low(i, k):
                    t = i * SLOTS + k
                    for q in range(2):
                        dve.wait_ge(high_done, 2 * t + q + 1)
                        xs = bass.ds(t * P, P)
                        dve.tensor_tensor(xtl[:, 4 * q:4 * q + 4, xs], psum[2 * k + q][:, :].rearrange("p (c n) -> p c n", n=P),
                                          f32(xth[:, 4 * q:4 * q + 4, xs]), ALU.subtract).then_inc(low_done, 1)

                if kind == "norm":
                    for k in range(SLOTS):
                        make(0, k)
                    with dve.Fori(1, GROUPS) as i:
                        for k in range(SLOTS):
                            low(i - 1, k)
                            make(i, k)
                    for k in range(SLOTS):
                        low(GROUPS - 1, k)
                else:
                    def make_and_split(i):
                        for k in range(SLOTS):
                            make(i, k)
                            low(i, k)

                    run(dve, GROUPS, make_and_split, c)

            @block.tensor
            def _(pe):
                def tiles(i):
                    for k in range(SLOTS):
                        t = i * SLOTS + k
                        pe.wait_ge(tile_made, t + 1)
                        for q in range(2):
                            if not below(i, 1):
                                pe.wait_ge(low_done, 2 * (t - SLOTS) + q + 1)
                            for n in range(4):
                                ins = pe.transpose(psum[2 * k + q][:, n * P:(n + 1) * P],
                                                   tok[:, k, (4 * q + n) * P:(4 * q + n + 1) * P], g.ident[:, :])
                            ins.then_inc(transposed, 1)

                run(pe, GROUPS, tiles)


def linear(nc, g, xth, xtl, tag, w, segments, gates=None):
    BANKS = 3
    wv = w.rearrange("(k p) n -> p k n", p=P)
    HK = KC // 2
    nb = sum(n for _, n, _, _ in segments)
    with Scope(nc, tag) as s:
        raw = s.sb("raw", [P, 2, HK, CB])
        wh, wl = s.sb("wh", [P, 2, KC, CB], fp32r), s.sb("wl", [P, 2, KC, CB], fp32r)
        stage = s.sb("stage", [P, BANKS, CB])
        normed = [m for _, _, m, _ in segments if isinstance(m, tuple)]
        loaded = [s.sem(f"w_loaded{i}") for i in range(2)]
        w_split, high_sem = s.sem("w_split"), s.sem("w_high")
        psum_ready, stage_ready = s.sem("psum_ready"), s.sem("stage_ready")
        psum_used = [s.sem(f"psum_used{i}") for i in range(len(segments))]
        stored = [s.sem(f"stored{i}") for i in range(BANKS)]
        psum = [s.ps(f"y{i}", [P, CB]) for i in range(BANKS)]
        if normed:
            gain_small, gain = s.sb("gain_small", [P, B_HD]), s.sb("gain", [P, B_HD])
            squares, ss, rms = s.sb("squares", [P, CB]), s.sb("ss", [P, A_H]), s.sb("rms", [P, A_H])
            gain_loaded, square_done, mean_done, root_done = s.sem("gain_loaded"), s.sem("square"), s.sem("mean"), s.sem("root")
        chain_sem = s.sem("chain")
        if gates:
            g_col, g_n, g_dst = gates
            g_raw = s.sb("g_raw", [P, KC, g_n])
            gh, gl = s.sb("gh", [P, KC, P], fp32r), s.sb("gl", [P, KC, P], fp32r)
            g_out = stage[0:g_n, :, :].rearrange("p a n -> p (a n)")
            g_loaded, g_split, g_ready, g_copied, g_stored = (s.sem(n) for n in ("g_loaded", "g_split", "g_ready", "g_copied", "g_stored"))
            g_psum = [s.ps(f"g{i}", [P, THIRD]) for i in range(3)]

        def each_segment(engine, body, chain=None, when=lambda m: True):
            b0 = 0
            for n, (col0, blocks, mode, target) in enumerate(segments):
                if when(mode):
                    start = chain.n if chain else 0
                    pairs = blocks // 2
                    run(engine, pairs, lambda i: body(n, i, b0), chain)
                b0 += blocks

        with nc.Block() as block:

            @block.sync
            def _(sp):
                if normed:
                    sp.dma_start(gain_small[:, :], normed[0][1].to_broadcast((P, B_HD))).then_inc(gain_loaded, 16)

                def load(n, i, b0):
                    for par in range(2):
                        b = b0 + 2 * i + par
                        col = segments[n][0] + (2 * i + par) * CB
                        for h in range(2):
                            if not below(b, 1):
                                wait(sp, w_split, 2 * b + h - 1)
                            sp.dma_start(raw[:, h], wv[:, h * HK:(h + 1) * HK, bass.ds(col, CB)]).then_inc(loaded[h], 16)

                each_segment(sp, load)
                if gates:
                    sp.dma_start(g_raw[:, :, :], wv[:, :, g_col:g_col + g_n]).then_inc(g_loaded, 16)
                    wait(sp, g_copied, 3)
                    sp.dma_start(g_dst, g_out[:, 0:T_ALL]).then_inc(g_stored, 16)
                    wait(sp, g_stored, 16)

            @block.gpsimd
            def _(pool):
                if gates:
                    pool.memset(f32(gh[:, :, :]), 0.0).then_inc(g_split, 1)
                    pool.memset(f32(gl[:, :, :]), 0.0).then_inc(g_split, 1)

                def split(n, i, b0):
                    for par in range(2):
                        b = b0 + 2 * i + par
                        for h in range(2):
                            wait(pool, loaded[h], b * 16 + 16)
                            if not below(b, 2):
                                wait(pool, psum_ready, (b - 1) * NT)
                            ks = slice(h * HK, (h + 1) * HK)
                            round_high(pool, g, wh[:, par, ks], raw[:, h]).then_inc(high_sem, 1)
                            wait(pool, high_sem, 2 * b + h + 1)
                            pool.tensor_tensor(wl[:, par, ks], raw[:, h], f32(wh[:, par, ks]), ALU.subtract).then_inc(w_split, 1)

                each_segment(pool, split)
                if gates:
                    wait(pool, g_loaded, 16)
                    wait(pool, g_split, 2)
                    pool.tensor_copy(gh[:, :, 0:g_n], g_raw[:, :, :]).then_inc(g_split, 1)
                    wait(pool, g_split, 3)
                    pool.tensor_tensor(gl[:, :, 0:g_n], g_raw[:, :, :], f32(gh[:, :, 0:g_n]), ALU.subtract).then_inc(g_split, 1)

            @block.tensor
            def _(pe):
                def products(n, i, b0):
                    for par in range(2):
                        b = b0 + 2 * i + par
                        for t in range(NT):
                            bank = t % BANKS
                            if t < BANKS and b0 == 0 and par == 0 and below(i, 1):
                                pass
                            elif t < BANKS and par == 0 and below(i, 1):
                                pe.wait_ge(psum_used[n - 1], NT * segments[n - 1][1] - BANKS + t + 1)
                            else:
                                pe.wait_ge(psum_used[n], (b - b0) * NT + t - BANKS + 1)
                            for k in range(KC):
                                if t == 0 and k % HK == 0:
                                    pe.wait_ge(w_split, 2 * b + k // HK + 1)
                                xs = slice(t * P, (t + 1) * P)
                                pe.matmul(psum[bank][:, :], xth[:, k, xs], wh[:, par, k], start=(k == 0), stop=False)
                                pe.matmul(psum[bank][:, :], xth[:, k, xs], wl[:, par, k], start=False, stop=False)
                                ins = pe.matmul(psum[bank][:, :], xtl[:, k, xs], wh[:, par, k], start=False, stop=(k == KC - 1))
                            ins.then_inc(psum_ready, 1)

                each_segment(pe, products)
                if gates:
                    pe.wait_ge(g_split, 4)
                    for j in range(3):
                        xs = slice(j * THIRD, (j + 1) * THIRD)
                        for k in range(KC):
                            pe.matmul(g_psum[j][:, :], gh[:, k], xth[:, k, xs], start=(k == 0), stop=False)
                            pe.matmul(g_psum[j][:, :], gl[:, k], xth[:, k, xs], start=False, stop=False)
                            ins = pe.matmul(g_psum[j][:, :], gh[:, k], xtl[:, k, xs], start=False, stop=(k == KC - 1))
                        ins.then_inc(g_ready, 1)

            @block.scalar
            def _(act):
                def evacuate(n, i, b0):
                    _, _, mode, target = segments[n]
                    for par in range(2):
                        bl = 2 * i + par
                        for t in range(NT):
                            bank = t % BANKS
                            u = (b0 + bl) * NT + t
                            act.wait_ge(psum_ready, u + 1)
                            if isinstance(mode, tuple):
                                if t or not below(bl, 1):
                                    act.wait_ge(mean_done, bl * NT + t)
                                act.activation(squares[:, :], psum[bank][:, :], ACT.Square).then_inc(square_done, 1)
                                act.wait_ge(mean_done, bl * NT + t + 1)
                                act.activation(rms[:, :], ss[:, :], ACT.Sqrt).then_inc(root_done, 1)
                                act.wait_ge(psum_used[n], bl * NT + t + 1)
                            else:
                                if not below(u, BANKS):
                                    act.wait_ge(stored[bank], store_count(b0 + bl, t))
                                act.activation(stage[:, bank, :], psum[bank][:, :],
                                               ACT.Sigmoid if mode == "sigmoid" else ACT.Copy).then_inc(psum_used[n], 1)
                                act.wait_ge(psum_used[n], bl * NT + t + 1)
                            act.dma_start(target(bl, t), stage[:, bank, :]).then_inc(stored[bank], 16)

                def store_count(b, t):
                    return (b * (NT // BANKS) + t // BANKS) * 16

                each_segment(act, evacuate, when=lambda m: m != "residual")
                if segments[0][2] != "residual":
                    for k in range(BANKS):
                        act.wait_ge(stored[k], nb * (NT // BANKS) * 16)
                if gates:
                    for j in range(3):
                        act.wait_ge(g_ready, j + 1)
                        act.activation(g_out[:, j * THIRD:(j + 1) * THIRD], g_psum[j][0:g_n, :], ACT.Copy).then_inc(g_copied, 1)

            @block.vector
            def _(dve):
                c = Chain(dve, chain_sem)
                if normed:
                    dve.wait_ge(gain_loaded, 16)
                    c.link(dve.tensor_scalar(gain[:, :], gain_small[:, :], normed[0][2], None, ALU.mult))

                def evacuate(n, i, b0):
                    col0, _, mode, _ = segments[n]
                    for par in range(2):
                        bl = 2 * i + par
                        for t in range(NT):
                            bank = t % BANKS
                            dve.wait_ge(psum_ready, (b0 + bl) * NT + t + 1)
                            if mode == "residual":
                                xs = g.x[:, t, bass.ds(bl * CB, CB)]
                                dve.tensor_tensor(xs, psum[bank][:, :], xs, ALU.add).then_inc(psum_used[n], 1)
                                continue
                            dve.wait_ge(square_done, bl * NT + t + 1)
                            c.link(dve.tensor_reduce(ss[:, :], squares[:, :].rearrange("p (h d) -> p h d", d=B_HD), axis=AX.X, op=ALU.add))
                            dve.tensor_scalar(ss[:, :], ss[:, :], 1.0 / B_HD, EPS, ALU.mult, ALU.add).then_inc(mean_done, 1)
                            dve.wait_ge(root_done, bl * NT + t + 1)
                            c.link(dve.reciprocal(rms[:, :], rms[:, :]))
                            if not (b0 == 0 and t < BANKS and below(bl, 1)):
                                dve.wait_ge(stored[bank], ((b0 + bl) * (NT // BANKS) + t // BANKS) * 16)
                            sv = stage[:, bank, :].rearrange("p (h d) -> p h d", d=B_HD)
                            c.link(dve.tensor_tensor(sv, psum[bank][:, :].rearrange("p (h d) -> p h d", d=B_HD), spread(rms[:, :], B_HD), ALU.mult))
                            dve.tensor_tensor(sv, sv, repeat(gain[:, :], A_H), ALU.mult).then_inc(psum_used[n], 1)

                each_segment(dve, evacuate, c, when=lambda m: m == "residual" or isinstance(m, tuple))


def ffn(nc, g, xth, xtl, tag, w_gu, w_down):
    FW = FG * P
    guv = w_gu.rearrange("(k p) n -> p k n", p=P)
    dv = w_down.rearrange("(f p) n -> p f n", p=P)
    G = FFN_GROUPS
    with Scope(nc, tag) as s:
        raw_a, raw_b = s.sb("raw_a", [P, KC * FW]), s.sb("raw_b", [P, KC, FW])
        raw_gate = raw_a[:, :].rearrange("p (k n) -> p k n", k=KC)
        raw_down = raw_a[:, :].rearrange("p (f n) -> p f n", f=FG)
        gh, gl = s.sb("gate_h", [P, FG, KC, P], fp32r), s.sb("gate_l", [P, FG, KC, P], fp32r)
        uh, ul = s.sb("up_h", [P, FG, KC, P], fp32r), s.sb("up_l", [P, FG, KC, P], fp32r)
        dh, dl = s.sb("down_h", [P, FG, D], fp32r), s.sb("down_l", [P, FG, D], fp32r)
        hid = s.sb("hid", [P, T_ALL])
        hh, hl = s.sb("hid_h", [P, FG, T_ALL], fp32r), s.sb("hid_l", [P, FG, T_ALL], fp32r)
        names = ("gate_loaded", "up_loaded", "down_loaded", "gate_split", "up_split", "down_split", "split_high",
                 "gate_ready", "up_ready", "silu_done", "prod_done", "hid_high", "hid_low", "down_ready", "added")
        (gate_loaded, up_loaded, down_loaded, gate_split, up_split, down_split, split_high,
         gate_ready, up_ready, silu_done, prod_done, hid_high, hid_low, down_ready, added) = (s.sem(n) for n in names)
        gp = [s.ps(f"gate{j}", [P, THIRD]) for j in range(3)]
        up = [s.ps(f"up{j}", [P, THIRD]) for j in range(3)]
        yp = [s.ps(f"y{j}", [P, CB]) for j in range(2)]
        thirds = [slice(j * THIRD, (j + 1) * THIRD) for j in range(3)]
        NY = NT * (D // CB)

        with nc.Block() as block:

            @block.sync
            def _(sp):
                def load(n):
                    first = below(n, 1)
                    if not first:
                        wait(sp, down_split, n)
                    sp.dma_start(raw_gate, guv[:, :, bass.ds(n * FW, FW)]).then_inc(gate_loaded, 16)
                    if not first:
                        wait(sp, up_split, n * FG)
                    sp.dma_start(raw_b[:, :, :], guv[:, :, bass.ds(D_FF + n * FW, FW)]).then_inc(up_loaded, 16)
                    wait(sp, gate_split, n * FG + FG)
                    sp.dma_start(raw_down, dv[:, bass.ds(n * FG, FG), :]).then_inc(down_loaded, 16)

                run(sp, G, load)
                wait(sp, down_loaded, 16 * G)

            @block.gpsimd
            def _(pool):
                def split(n):
                    first = below(n, 1)
                    for f in range(FG):
                        fs = slice(f * P, (f + 1) * P)
                        for part, (raw, h, l, loaded, ready, done) in enumerate((
                                (raw_gate, gh, gl, gate_loaded, gate_ready, gate_split),
                                (raw_b, uh, ul, up_loaded, up_ready, up_split))):
                            wait(pool, loaded, n * 16 + 16)
                            if not first:
                                wait(pool, ready, ((n - 1) * FG + f) * 3 + 3)
                            round_high(pool, g, h[:, f], raw[:, :, fs]).then_inc(split_high, 1)
                            wait(pool, split_high, n * (2 * FG + 1) + 2 * f + part + 1)
                            pool.tensor_tensor(l[:, f], raw[:, :, fs], f32(h[:, f]), ALU.subtract).then_inc(done, 1)
                    wait(pool, down_loaded, n * 16 + 16)
                    if not first:
                        wait(pool, down_ready, n * NY)
                    round_high(pool, g, dh[:, :, :], raw_down).then_inc(split_high, 1)
                    wait(pool, split_high, n * (2 * FG + 1) + 2 * FG + 1)
                    pool.tensor_tensor(dl[:, :, :], raw_down, f32(dh[:, :, :]), ALU.subtract).then_inc(down_split, 1)

                run(pool, G, split)

            @block.tensor
            def _(pe):
                def hidden(n, f, banks, h, l, split, freed, ready):
                    pe.wait_ge(split, n * FG + f + 1)
                    for j in range(3):
                        if f or not below(n, 1):
                            pe.wait_ge(freed, (n * FG + f - 1) * 3 + j + 1)
                        for k in range(KC):
                            pe.matmul(banks[j][:, :], h[:, f, k], xth[:, k, thirds[j]], start=(k == 0), stop=False)
                            pe.matmul(banks[j][:, :], l[:, f, k], xth[:, k, thirds[j]], start=False, stop=False)
                            ins = pe.matmul(banks[j][:, :], h[:, f, k], xtl[:, k, thirds[j]], start=False, stop=(k == KC - 1))
                        ins.then_inc(ready, 1)

                def gate(n, f):
                    hidden(n, f, gp, gh, gl, gate_split, silu_done, gate_ready)

                def upward(n, f):
                    hidden(n, f, up, uh, ul, up_split, prod_done, up_ready)

                def down(n):
                    pe.wait_ge(down_split, n + 1)
                    pe.wait_ge(hid_low, (n + 1) * FG * 3)
                    for t in range(NT):
                        ts = slice(t * P, (t + 1) * P)
                        for c in range(2):
                            cs = slice(c * CB, (c + 1) * CB)
                            if t or not below(n, 1):
                                pe.wait_ge(added, n * NY + 2 * t + c - 1)
                            for f in range(FG):
                                pe.matmul(yp[c][:, :], hh[:, f, ts], dh[:, f, cs], start=(f == 0), stop=False)
                                pe.matmul(yp[c][:, :], hh[:, f, ts], dl[:, f, cs], start=False, stop=False)
                                ins = pe.matmul(yp[c][:, :], hl[:, f, ts], dh[:, f, cs], start=False, stop=(f == FG - 1))
                            ins.then_inc(down_ready, 1)

                def group(n):
                    upward(n, 0)
                    for f in range(1, FG):
                        gate(n, f)
                        upward(n, f)
                    gate(n + 1, 0)
                    down(n)

                gate(0, 0)
                run(pe, G - 1, group)
                upward(G - 1, 0)
                for f in range(1, FG):
                    gate(G - 1, f)
                    upward(G - 1, f)
                down(G - 1)

            @block.scalar
            def _(act):
                def silu(n, f):
                    for j in range(3):
                        act.wait_ge(gate_ready, (n * FG + f) * 3 + j + 1)
                        if f or not below(n, 1):
                            act.wait_ge(hid_low, (n * FG + f - 1) * 3 + j + 1)
                        act.activation(hid[:, thirds[j]], gp[j][:, :], ACT.Silu).then_inc(silu_done, 1)

                def high(n, f):
                    for j in range(3):
                        act.wait_ge(prod_done, (n * FG + f) * 3 + j + 1)
                        if not below(n, 1):
                            act.wait_ge(down_ready, n * NY)
                        act.activation(hh[:, f, thirds[j]], hid[:, thirds[j]], ACT.Copy).then_inc(hid_high, 1)

                def group(n):
                    high(n, 0)
                    for f in range(1, FG):
                        silu(n, f)
                        high(n, f)
                    silu(n + 1, 0)

                silu(0, 0)
                run(act, G - 1, group)
                high(G - 1, 0)
                for f in range(1, FG):
                    silu(G - 1, f)
                    high(G - 1, f)

            @block.vector
            def _(dve):
                def group(n):
                    for f in range(FG):
                        for j in range(3):
                            dve.wait_ge(up_ready, (n * FG + f) * 3 + j + 1)
                            dve.wait_ge(silu_done, (n * FG + f) * 3 + j + 1)
                            dve.tensor_tensor(hid[:, thirds[j]], up[j][:, :], hid[:, thirds[j]], ALU.mult).then_inc(prod_done, 1)
                        for j in range(3):
                            dve.wait_ge(hid_high, (n * FG + f) * 3 + j + 1)
                            dve.tensor_tensor(hl[:, f, thirds[j]], hid[:, thirds[j]], f32(hh[:, f, thirds[j]]), ALU.subtract).then_inc(hid_low, 1)
                    for t in range(NT):
                        for c in range(2):
                            dve.wait_ge(down_ready, n * NY + 2 * t + c + 1)
                            xs = g.x[:, t, c * CB:(c + 1) * CB]
                            dve.tensor_tensor(xs, yp[c][:, :], xs, ALU.add).then_inc(added, 1)

                run(dve, G, group)


def log_sigmoid_act(act, u, w, ready_exp, exp_done, ready_ln, ln_done):
    act.wait_ge(*ready_exp)
    act.activation(u, u, ACT.Exp, scale=-1.0).then_inc(exp_done, 1)
    act.wait_ge(*ready_ln)
    act.activation(w[1], w[0], ACT.Ln).then_inc(ln_done, 1)


def log_sigmoid_dve(dve, c, z, u, w, lw, abs_done, exp_done, sum_done, ln_done):
    dve.scalar_tensor_tensor(u, z, -1.0, z, ALU.mult, ALU.max).then_inc(abs_done, 1)
    dve.wait_ge(exp_done, 1)
    dve.tensor_scalar(w, u, 1.0, None, ALU.add).then_inc(sum_done, 1)
    dve.wait_ge(sum_done, 1)
    c.link(dve.scalar_tensor_tensor(u, w, 1.0, u, ALU.subtract, ALU.subtract))
    dve.wait_ge(ln_done, 1)
    c.link(dve.reciprocal(w, w))
    c.link(dve.tensor_tensor(u, u, w, ALU.mult))
    c.link(dve.tensor_tensor(lw, lw, u, ALU.subtract))
    c.link(dve.scalar_tensor_tensor(z, z, 0.0, lw, ALU.min, ALU.subtract))


KIND_A, KIND_G, KIND_W, KIND_E = range(4)


def mlstm_gates(nc, g, gates_d, b_i, b_f, state_m, m_prompt, m_sample):
    NG = NP + DEC_BATCH
    with Scope(nc, "mgates") as s:
        li, lf, u, w, lw = (s.sb(n, [A_H, T_ALL]) for n in ("li", "lf", "u", "w", "lw"))
        b, m, reset = s.sb("b", [A_H, T_ALL]), s.sb("m", [A_H, T_ALL]), s.sb("reset", [A_H, T_ALL])
        gg, ws, en, A = s.sb("gg", [A_H, T_ALL]), s.sb("ws", [A_H, T_ALL]), s.sb("en", [A_H, T_ALL]), s.sb("A", [A_H, T_ALL])
        bi, bf, bi15, bf15 = (s.sb(n, [A_H, 1]) for n in ("bi", "bf", "bi15", "bf15"))
        m0, mprev, bend, gend = s.sb("m0", [A_H, DEC_BATCH]), s.sb("mprev", [A_H, NG]), s.sb("bend", [A_H, NG]), s.sb("gend", [A_H, NG])
        diag, gcs = s.sb("diag", [A_H, A_H, DEC_BATCH]), s.sb("gcs", [DEC_BATCH, A_H])
        loaded = s.sem("loaded")
        chain_sem, scaled, tanh_done, abs_done, exp_done, sum_done, ln_done = (s.sem(n) for n in (
            "chain", "scaled", "tanh", "abs", "exp", "sum", "ln"))
        arg_done, exps_done, A_done, filled, made, turned, out_sem, gend_done = (s.sem(n) for n in (
            "arg", "exps", "A", "filled", "made", "turned", "out", "gend"))
        copied = s.sem("copied")
        tp = s.ps("tok", [P, NT, 4, A_H])
        sp_ = s.ps("small", [P, CB])

        def groups(ap):
            return (ap[:, 0:SEQ].rearrange("h (c t) -> h c t", t=P),
                    ap[:, SEQ:T_ALL].rearrange("h (c t) -> h c t", t=DEC_SEQ))

        with nc.Block() as block:

            @block.sync
            def _(sp):
                sp.dma_start(li[:, :], gates_d[0:A_H, :]).then_inc(loaded, 16)
                sp.dma_start(lf[:, :], gates_d[A_H:2 * A_H, :]).then_inc(loaded, 16)
                sp.dma_start(bi[:, :], b_i.rearrange("o h -> h o")).then_inc(loaded, 16)
                sp.dma_start(bf[:, :], b_f.rearrange("o h -> h o")).then_inc(loaded, 16)
                sp.dma_start(m0[:, :], state_m.rearrange("s o h -> h (s o)"), allow_slow_non_contiguous=True).then_inc(loaded, 16)
                wait(sp, gend_done, 1)
                sp.dma_start(m_prompt.rearrange("a o h -> h (a o)"), m[:, SEQ - 1:SEQ]).then_inc(out_sem, 16)
                sp.dma_start(m_sample.rearrange("s o h -> h (s o)"), groups(m)[1][:, :, DEC_SEQ - 1], allow_slow_non_contiguous=True).then_inc(out_sem, 16)
                wait(sp, out_sem, 32)

            @block.gpsimd
            def _(pool):
                pool.memset(g.sel[:, :, :], 0.0).then_inc(filled, 1)
                pool.memset(g.pair_sel[:, :, :, :], 0.0).then_inc(filled, 1)
                pool.memset(g.own[:, :], 1.0).then_inc(filled, 1)
                pool.memset(g.ones8[:, :], 1.0).then_inc(filled, 1)
                pool.memset(reset[:, :], 1.0).then_inc(filled, 1)
                wait(pool, filled, 5)
                pool.affine_select(out=g.sel[:, :, :], in_=g.sel[:, :, :], compare_op=ALU.not_equal, fill=1.0,
                                   base=0, pattern=[[-1, A_H], [0, P]], channel_multiplier=1).then_inc(made, 1)
                pool.affine_select(out=g.pair_sel[:, :, :, :], in_=g.pair_sel[:, :, :, :], compare_op=ALU.not_equal, fill=1.0,
                                   base=0, pattern=[[-2, A_PAIRS], [-1, 2], [0, A_QK]], channel_multiplier=1).then_inc(made, 1)
                pool.affine_select(out=g.own[:, :], in_=g.own[:, :], compare_op=ALU.is_ge, fill=0.0,
                                   base=0, pattern=[[-DEC_SEQ, DEC_BATCH]], channel_multiplier=1).then_inc(made, 1)
                wait(pool, made, 3)
                pool.affine_select(out=g.own[:, :], in_=g.own[:, :], compare_op=ALU.is_ge, fill=0.0,
                                   base=DEC_SEQ - 1, pattern=[[DEC_SEQ, DEC_BATCH]], channel_multiplier=-1).then_inc(made, 1)
                mk = g.mask_dec[:, :, :].rearrange("p e (c t) -> p e c t", t=DEC_SEQ)
                pool.affine_select(out=mk, in_=g.mask_kq[:, :, :].rearrange("p e (c t) -> p e c t", t=DEC_SEQ), compare_op=ALU.is_ge, fill=NEG,
                                   base=0, pattern=[[0, 2], [-DEC_SEQ, DEC_BATCH], [0, DEC_SEQ]], channel_multiplier=1).then_inc(made, 1)
                for view in groups(reset):
                    pool.memset(view[:, :, 0:1], 0.0).then_inc(made, 1)
                wait(pool, made, 7)

            @block.scalar
            def _(act):
                act.wait_ge(scaled, 2)
                act.activation(li[:, :], li[:, :], ACT.Tanh, bias=bi15[:, :], scale=1.0 / CAP).then_inc(tanh_done, 1)
                act.activation(lf[:, :], lf[:, :], ACT.Tanh, bias=bf15[:, :], scale=1.0 / CAP).then_inc(tanh_done, 1)
                log_sigmoid_act(act, u[:, :], (w[:, :], lw[:, :]), (abs_done, 1), exp_done, (sum_done, 1), ln_done)
                act.wait_ge(arg_done, 3)
                act.activation(gg[:, :], gg[:, :], ACT.Exp).then_inc(exps_done, 1)
                act.activation(ws[:, :], ws[:, :], ACT.Exp).then_inc(exps_done, 1)
                act.activation(en[:, :], m[:, :], ACT.Exp, scale=-1.0).then_inc(exps_done, 1)

            @block.vector
            def _(dve):
                c = Chain(dve, chain_sem)
                dve.wait_ge(loaded, 80)
                dve.tensor_scalar(bi15[:, :], bi[:, :], 1.0 / CAP, None, ALU.mult).then_inc(scaled, 1)
                dve.tensor_scalar(bf15[:, :], bf[:, :], 1.0 / CAP, None, ALU.mult).then_inc(scaled, 1)
                dve.wait_ge(tanh_done, 2)
                c.link(dve.tensor_scalar(li[:, :], li[:, :], CAP, None, ALU.mult))
                c.link(dve.tensor_scalar(lf[:, :], lf[:, :], CAP, None, ALU.mult))
                log_sigmoid_dve(dve, c, lf[:, :], u[:, :], w[:, :], lw[:, :], abs_done, exp_done, sum_done, ln_done)
                dve.wait_ge(made, 7)
                c.link(dve.tensor_tensor_scan(b[:, :], reset[:, :], lf[:, :], 0.0, ALU.mult, ALU.add))
                c.link(dve.tensor_tensor_scan(m[:, 0:SEQ], lf[:, 0:SEQ], li[:, 0:SEQ], 0.0, ALU.add, ALU.max))
                for k in range(DEC_BATCH):
                    ks = slice(SEQ + k * DEC_SEQ, SEQ + (k + 1) * DEC_SEQ)
                    c.link(dve.tensor_tensor_scan(m[:, ks], lf[:, ks], li[:, ks], m0[:, k:k + 1], ALU.add, ALU.max))
                c.link(dve.memset(mprev[:, 0:1], 0.0))
                c.link(dve.tensor_copy(mprev[:, 1:NP], groups(m)[0][:, 0:NP - 1, P - 1]))
                c.link(dve.tensor_copy(mprev[:, NP:NG], m0[:, :]))
                c.link(dve.tensor_tensor(g.B[:, :], b[:, :], m[:, :], ALU.subtract))
                dve.tensor_tensor(A[:, :], li[:, :], b[:, :], ALU.subtract).then_inc(A_done, 1)
                dve.wait_ge(A_done, 1)
                for part, (lo, hi, n, last) in enumerate(((0, NP, P, P - 1), (NP, NG, DEC_SEQ, DEC_SEQ - 1))):
                    c.link(dve.tensor_copy(bend[:, lo:hi], groups(g.B)[part][:, :, last]))
                for part, (lo, hi, n, last) in enumerate(((0, NP, P, P - 1), (NP, NG, DEC_SEQ, DEC_SEQ - 1))):
                    c.link(dve.tensor_tensor(groups(gg)[part], groups(g.B)[part], spread(mprev[:, lo:hi], n), ALU.add))
                    dve.tensor_tensor(groups(ws)[part], groups(A)[part], spread(bend[:, lo:hi], n), ALU.add).then_inc(arg_done, 1)
                dve.wait_ge(arg_done, 2)
                dve.sem_inc(arg_done, 1)
                dve.wait_ge(exps_done, 3)
                c.link(dve.tensor_copy(gend[:, 0:NP], groups(gg)[0][:, :, P - 1]))
                c.link(dve.tensor_copy(gend[:, NP:NG], groups(gg)[1][:, :, DEC_SEQ - 1]))
                c.link(dve.tensor_tensor(diag[:, :, :], spread(g.ident[0:A_H, 0:A_H], DEC_BATCH), repeat(gend[:, NP:NG], A_H), ALU.mult))
                dve.sem_inc(gend_done, 1)
                dve.wait_ge(turned, 2)
                dve.tensor_copy(g.tok[:, :, :, :], tp[:, :, :, :]).then_inc(copied, 1)
                dve.tensor_copy(g.gc_pair[:, :, :], sp_[:, 0:A_PAIRS * NP].rearrange("p (j c) -> p j c", j=A_PAIRS)).then_inc(copied, 1)
                dve.tensor_copy(g.gc_dec[:, :, :], sp_[:, 64:128].rearrange("p (h c) -> p h c", h=A_H)).then_inc(copied, 1)
                dve.tensor_copy(g.gc_s[:, :], sp_[0:DEC_BATCH, 128:128 + A_H]).then_inc(copied, 1)

            @block.tensor
            def _(pe):
                pe.wait_ge(A_done, 1)
                pe.wait_ge(exps_done, 3)
                for t in range(NT):
                    for kind, row in ((KIND_A, A), (KIND_G, gg), (KIND_W, ws), (KIND_E, en)):
                        ins = pe.transpose(tp[:, t, kind, :], row[:, t * P:(t + 1) * P], g.ident[0:A_H, 0:A_H])
                ins.then_inc(turned, 1)
                pe.wait_ge(gend_done, 1)
                pe.wait_ge(made, 7)
                for j in range(A_PAIRS):
                    pe.matmul(sp_[:, j * NP:(j + 1) * NP], g.pair_sel[:, j].rearrange("k e d -> k (e d)"), gend[:, 0:NP], start=True, stop=True)
                pe.matmul(sp_[:, 64:128], g.ones8[:, :], diag[:, :, :].rearrange("k h c -> k (h c)"), start=True, stop=True)
                pe.transpose(sp_[0:DEC_BATCH, 128:128 + A_H], gend[:, NP:NG], g.ident[0:A_H, 0:A_H]).then_inc(turned, 1)


def mlstm(nc, g, qkvo, h_d, running, c_out, n_out, state_c=None, state_n=None):
    tag = "mrun" if running else "mprompt"
    N_C = 1 if running else NP
    V1 = A_V + 1
    NPAIR = DEC_BATCH // 2
    with Scope(nc, tag) as s:
        qk, v1 = s.sb("qk", [P, 2 * A_H * A_QK]), s.sb("v1", [P, A_H, V1])
        k8, wsv = s.sb("k8", [P, A_H * A_QK]), s.sb("wsv", [P, A_H, V1])
        qt, kt = s.sb("qt", [P, A_PAIRS, P]), s.sb("kt", [P, A_PAIRS, P])
        tokc, gcc = s.sb("tokc", [P, 4, A_H]), s.sb("gcc", [P, A_PAIRS])
        arg, st = s.sb("arg", [P, 2, 2, P]), s.sb("st", [P, 2, 2, P])
        ig, num = s.sb("ig", [P, 2, 2, V1]), s.sb("num", [P, A_H, V1])
        den, hout = s.sb("den", [P, A_H]), s.sb("hout", [P, A_H, A_V])
        names = ("qk_loaded", "v_loaded", "ones", "tok_done", "k8_done", "wsv_done", "turned", "t_copied", "bias_ready",
                 "arg_done", "exp_done", "score_ready", "st_done", "num_ready", "inter_ready", "ig_done", "num_done",
                 "state_ready", "state_done", "h_done", "stored", "chain")
        (qk_loaded, v_loaded, ones, tok_done, k8_done, wsv_done, turned, t_copied, bias_ready,
         arg_done, exp_done, score_ready, st_done, num_ready, inter_ready, ig_done, num_done,
         state_ready, state_done, h_done, stored, chain_sem) = (s.sem(n) for n in names)
        psc, pi = s.ps("scores", [P, 2, CB]), s.ps("inter", [P, 2, CB])
        pb, pn, pc, pt = s.ps("bias", [P, 2, P]), s.ps("num_p", [P, 2, V1]), s.ps("state", [P, CB]), s.ps("turn", [P, 4, P])
        final_t, final_c, final_s, final_n = (s.sem(n) for n in ("final_t", "final_c", "final_s", "final_n"))
        if running:
            cold, c0t = s.sb("cold", [P, A_H, DEC_BATCH, A_QK]), s.sb("c0t", [P, NPAIR, A_H, V1])
            nload, nold = s.sb("nload", [NPAIR * A_H, P]), s.sb("nold", [DEC_BATCH, A_H * A_QK])
            qm, km = s.sb("qm", [P, 2, DEC_BATCH, A_QK]), s.sb("km", [P, 2, DEC_BATCH, A_QK])
            qmt, wsk, ccur = s.sb("qmt", [P, 2, NPAIR, P]), s.sb("wsk", [P, A_H, A_QK]), s.sb("ccur", [P, 2, DEC_BATCH, A_QK])
            c_loaded, n_loaded, c0_turned, c0_copied, qm_done, qm_turned, qm_copied = (s.sem(n) for n in (
                "c_loaded", "n_loaded", "c0_turned", "c0_copied", "qm_done", "qm_turned", "qm_copied"))
            decayed, km_done, wsk_done, c_ready, c_done, n_ready, n_done = (s.sem(n) for n in (
                "decayed", "km_done", "wsk_done", "c_ready", "c_done", "n_ready", "n_done"))
            mask = g.mask_dec
        else:
            ct = s.sb("ct", [P, A_PAIRS, V1])
            cfin, nfin = s.sb("cfin", [P, A_PAIRS, P]), s.sb("nfin", [A_PAIRS, P])
            mask = g.mask_kq

        def tile(i):
            return NT - 1 if running else i

        with nc.Block() as block:

            @block.sync
            def _(sp):
                if running:
                    for j in range(NPAIR):
                        sp.dma_start(nload[j * A_H:(j + 1) * A_H, :].rearrange("h (s d) -> h s d", s=2),
                                     state_n[2 * j:2 * j + 2, 0].rearrange("s h d -> h s d")).then_inc(n_loaded, 16)
                    sp.dma_start(nold[:, :], state_n.rearrange("s o h d -> s (o h d)")).then_inc(n_loaded, 16)
                    for h in range(A_H):
                        sp.dma_start(cold[:, h], state_c[:, 0, h].rearrange("s v d -> v s d")).then_inc(c_loaded, 16)

                def load(i):
                    t = tile(i)
                    if not below(i, 1):
                        wait(sp, t_copied, 2 * i)
                        wait(sp, k8_done, i)
                    sp.dma_start(qk[:, :], qkvo[t, :, 0:A_V0]).then_inc(qk_loaded, 16)
                    if not below(i, 1):
                        wait(sp, wsv_done, i)
                        wait(sp, num_ready, i * A_PAIRS)
                    sp.dma_start(v1[:, :, 0:A_V], qkvo[t, :, A_V0:A_O0].rearrange("t (h v) -> t h v", v=A_V)).then_inc(v_loaded, 16)

                run(sp, N_C, load)
                if not running:
                    wait(sp, final_c, 5)
                    for j in range(A_PAIRS):
                        sp.dma_start(c_out[0, 0, 2 * j:2 * j + 2].rearrange("h v d -> v h d"),
                                     cfin[:, j, :].rearrange("v (h d) -> v h d", h=2)).then_inc(final_s, 16)
                    sp.dma_start(n_out.rearrange("a b (j h) d -> (a b j) (h d)", j=A_PAIRS), nfin[:, :]).then_inc(final_s, 16)
                    wait(sp, final_s, 16 * (A_PAIRS + 1))
                else:
                    for h in range(A_H):
                        wait(sp, c_done, h + 1)
                        sp.dma_start(c_out[:, 0, h].rearrange("s v d -> v s d"), cold[:, h]).then_inc(final_s, 16)
                    wait(sp, n_done, 1)
                    sp.dma_start(n_out.rearrange("s o h d -> s (o h d)"), nold[:, :]).then_inc(final_s, 16)
                    wait(sp, final_s, 16 * (A_H + 1))

            @block.gpsimd
            def _(pool):
                pool.memset(v1[:, :, A_V:V1], 1.0).then_inc(ones, 1)
                if not running:
                    pool.memset(ct[:, :, :], 0.0).then_inc(ones, 1)
                else:
                    pool.sem_inc(ones, 1)

                def weigh(i):
                    wait(pool, qk_loaded, i * 16 + 16)
                    if not below(i, 1):
                        wait(pool, state_ready, i * A_PAIRS)
                    wait(pool, v_loaded, i * 16 + 16)
                    wait(pool, tok_done, i + 1)
                    wait(pool, ones, 2)
                    pool.tensor_tensor(wsv[:, :, :], v1[:, :, :], spread(tokc[:, KIND_W, :], V1), ALU.mult).then_inc(wsv_done, 1)
                    pool.tensor_scalar(k8[:, :], qk[:, A_K0:A_V0], A_QK ** -0.5, None, ALU.mult).then_inc(k8_done, 1)

                run(pool, N_C, weigh)
                if running:
                    wait(pool, k8_done, 1)
                    k8v = k8[:, :].rearrange("p (h d) -> p h d", d=A_QK)
                    pool.tensor_tensor(wsk[:, :, :], k8v, spread(tokc[:, KIND_W, :], A_QK), ALU.mult).then_inc(wsk_done, 1)
                    for h in range(A_H):
                        if h >= 2:
                            wait(pool, c_ready, h - 1)
                        pool.tensor_tensor(km[:, h % 2], repeat(k8v[:, h, :], DEC_BATCH), spread(g.own[:, :], A_QK), ALU.mult).then_inc(km_done, 1)

            @block.tensor
            def _(pe):
                if running:
                    for h in range(A_H):
                        pe.wait_ge(c_loaded, 16 * A_H)
                        if h:
                            pe.wait_ge(c0_copied, h)
                        for j in range(NPAIR):
                            ins = pe.transpose(pt[:, j, :], cold[:, h, 2 * j:2 * j + 2, :].rearrange("v s d -> v (s d)"), g.ident[:, :])
                        ins.then_inc(c0_turned, 1)
                    pe.wait_ge(c0_copied, A_H)
                    pe.wait_ge(n_loaded, 16 * (NPAIR + 1))
                    pe.transpose(pt[:, 0, 0:NPAIR * A_H], nload[:, :], g.ident[0:NPAIR * A_H, 0:NPAIR * A_H]).then_inc(c0_turned, 1)
                    pe.wait_ge(c0_copied, A_H + 1)

                def head_pair(i, j):
                    return i * A_PAIRS + j

                def bias(i, j):
                    u = head_pair(i, j)
                    if not below(u, 1):
                        pe.wait_ge(arg_done, u)
                    cols = bass.ds(tile(i) * P, P)
                    pe.matmul(pb[:, :, :], g.ident[:, :], mask[:, :, :], start=True, stop=False)
                    for e in range(2):
                        ins = pe.matmul(pb[:, e, :], g.sel[:, 2 * j + e, :], g.B[:, cols], start=False, stop=(e == 1))
                    ins.then_inc(bias_ready, 1)

                def scores(i, j):
                    u = head_pair(i, j)
                    if not below(u, 1):
                        pe.wait_ge(st_done, u)
                    for e in range(2):
                        es = slice(e * A_QK, (e + 1) * A_QK)
                        ins = pe.matmul(psc[:, e, 0:P], kt[es, j, :], qt[es, j, :], start=True, stop=True)
                    ins.then_inc(score_ready, 1)

                def chunk(i):
                    pe.wait_ge(qk_loaded, i * 16 + 16)
                    for part in range(2):
                        if part or not below(i, 1):
                            pe.wait_ge(t_copied, 2 * i + part)
                        for n in range(A_PAIRS):
                            ins = pe.transpose(pt[:, n, :], qk[:, (part * A_PAIRS + n) * P:(part * A_PAIRS + n + 1) * P], g.ident[:, :])
                        ins.then_inc(turned, 1)
                    pe.wait_ge(t_copied, 2 * i + 2)
                    bias(i, 0)
                    scores(i, 0)
                    for j in range(A_PAIRS):
                        u = head_pair(i, j)
                        slot = j % 2
                        if j + 1 < A_PAIRS:
                            bias(i, j + 1)
                            scores(i, j + 1)
                        pe.wait_ge(st_done, u + 1)
                        pe.wait_ge(v_loaded, i * 16 + 16)
                        pe.wait_ge(ones, 2)
                        if not below(u, 1):
                            pe.wait_ge(num_done, u)
                        for e in range(2):
                            ins = pe.matmul(pn[:, e, :], st[:, slot, e, :], v1[:, 2 * j + e, :], start=True, stop=True)
                        ins.then_inc(num_ready, 1)
                        if not below(u, 1):
                            pe.wait_ge(ig_done, 2 * u)
                        if running:
                            for e in range(2):
                                h = 2 * j + e
                                pe.wait_ge(qm_done, h + 1)
                                if h >= 1:
                                    pe.wait_ge(qm_copied, h)
                                for n in range(NPAIR):
                                    ins = pe.transpose(pt[:, n, :], qm[:, e, 2 * n:2 * n + 2, :].rearrange("t s d -> t (s d)"), g.ident[:, :])
                                ins.then_inc(qm_turned, 1)
                                pe.wait_ge(qm_copied, h + 1)
                                for n in range(NPAIR):
                                    ins = pe.matmul(pi[:, e, 0:V1], qmt[:, e, n, :], c0t[:, n, h, :], start=(n == 0), stop=(n == NPAIR - 1))
                            ins.then_inc(inter_ready, 1)
                        else:
                            if not below(i, 1):
                                pe.wait_ge(state_done, u - A_PAIRS + 1)
                            for e in range(2):
                                es = slice(e * A_QK, (e + 1) * A_QK)
                                ins = pe.matmul(pi[:, e, 0:V1], qt[es, j, :], ct[es, j, :], start=True, stop=True)
                            ins.then_inc(inter_ready, 1)
                            pe.wait_ge(k8_done, i + 1)
                            pe.wait_ge(wsv_done, i + 1)
                            if not below(u, 1):
                                pe.wait_ge(state_done, u)
                            for e in range(2):
                                h = 2 * j + e
                                ins = pe.matmul(pc[e * A_QK:(e + 1) * A_QK, 0:V1], k8[:, h * A_QK:(h + 1) * A_QK], wsv[:, h, :], start=True, stop=True)
                            ins.then_inc(state_ready, 1)

                run(pe, N_C, chunk)
                if not running:
                    pe.wait_ge(state_done, N_C * A_PAIRS)
                    for j in range(A_PAIRS):
                        ins = pe.transpose(pt[:, j, :], ct[:, j, 0:A_V], g.ident[:, :])
                    ins.then_inc(final_t, 1)
                    pe.wait_ge(final_c, 4)
                    pe.transpose(pt[0:A_PAIRS, 0, :], ct[:, :, A_V:V1].rearrange("p j o -> p (j o)"), g.ident[:, :]).then_inc(final_t, 1)
                else:
                    pe.wait_ge(wsk_done, 1)
                    pe.matmul(pc[0:DEC_BATCH, :], g.own[:, :], wsk[:, :, :].rearrange("p h d -> p (h d)"), start=True, stop=True).then_inc(n_ready, 1)
                    for h in range(A_H):
                        bank = pt[:, :, :].rearrange("p a b -> p (a b)") if h % 2 == 0 else pc[:, :]
                        if h == 1:
                            pe.wait_ge(n_done, 1)
                        if h >= 2:
                            pe.wait_ge(c_done, h - 1)
                        pe.wait_ge(km_done, h + 1)
                        pe.wait_ge(wsv_done, 1)
                        pe.matmul(bank, wsv[:, h, 0:A_V], km[:, h % 2].rearrange("p s d -> p (s d)"), start=True, stop=True).then_inc(c_ready, 1)

            @block.scalar
            def _(act):
                if running:
                    for h in range(A_H):
                        act.wait_ge(c0_turned, h + 1)
                        act.activation(c0t[:, :, h, 0:A_V], pt[:, :, :], ACT.Copy).then_inc(c0_copied, 1)
                    act.wait_ge(c0_turned, A_H + 1)
                    act.activation(c0t[:, :, :, A_V:V1].rearrange("p n h o -> p (n h o)"), pt[:, 0, 0:NPAIR * A_H], ACT.Copy).then_inc(c0_copied, 1)

                def exponent(i, j):
                    u = i * A_PAIRS + j
                    act.wait_ge(arg_done, u + 1)
                    act.activation(arg[:, j % 2], arg[:, j % 2], ACT.Exp).then_inc(exp_done, 1)

                def chunk(i):
                    for part, (dst, scale) in enumerate(((qt, 1.0), (kt, A_QK ** -0.5))):
                        act.wait_ge(turned, 2 * i + part + 1)
                        act.activation(dst[:, :, :], pt[:, :, :], ACT.Copy, scale=scale).then_inc(t_copied, 1)
                    exponent(i, 0)
                    for j in range(A_PAIRS):
                        u = i * A_PAIRS + j
                        if j + 1 < A_PAIRS:
                            exponent(i, j + 1)
                        if running:
                            for e in range(2):
                                act.wait_ge(qm_turned, 2 * j + e + 1)
                                act.activation(qmt[:, e], pt[:, :, :], ACT.Copy).then_inc(qm_copied, 1)
                        act.wait_ge(inter_ready, u + 1)
                        act.wait_ge(tok_done, i + 1)
                        if not below(u, 2):
                            act.wait_ge(num_done, u - 1)
                        for e in range(2):
                            act.activation(ig[:, j % 2, e, :], pi[:, e, 0:V1], ACT.Copy,
                                           scale=tokc[:, KIND_G, 2 * j + e:2 * j + e + 1]).then_inc(ig_done, 1)
                    act.wait_ge(h_done, i + 1)
                    act.dma_start(h_d[tile(i)], hout[:, :, :].rearrange("t h v -> t (h v)")).then_inc(stored, 16)

                run(act, N_C, chunk)
                act.wait_ge(stored, 16 * N_C)
                if not running:
                    for n in range(1):
                        act.wait_ge(final_t, 1)
                        for j in range(A_PAIRS):
                            act.activation(cfin[:, j, :], pt[:, j, :], ACT.Copy).then_inc(final_c, 1)
                        act.wait_ge(final_t, 2)
                        act.activation(nfin[:, :], pt[0:A_PAIRS, 0, :], ACT.Copy).then_inc(final_c, 1)

            @block.vector
            def _(dve):
                c = Chain(dve, chain_sem)
                if running:
                    for h in range(2):
                        dve.wait_ge(qk_loaded, 16)
                        dve.tensor_tensor(qm[:, h % 2], repeat(qk[:, h * A_QK:(h + 1) * A_QK], DEC_BATCH), spread(g.own[:, :], A_QK), ALU.mult).then_inc(qm_done, 1)

                def argument(i, j):
                    u = i * A_PAIRS + j
                    dve.wait_ge(bias_ready, u + 1)
                    dve.tensor_tensor(arg[:, j % 2], pb[:, :, :], spread(tokc[:, KIND_A, 2 * j:2 * j + 2], P), ALU.add).then_inc(arg_done, 1)

                def chunk(i):
                    dve.tensor_copy(tokc[:, :, :], g.tok[:, tile(i)]).then_inc(tok_done, 1)
                    if not running:
                        c.link(dve.tensor_copy(gcc[:, :], g.gc_pair[:, :, i]))
                    dve.wait_ge(tok_done, i + 1)
                    argument(i, 0)
                    for j in range(A_PAIRS):
                        u = i * A_PAIRS + j
                        if j + 1 < A_PAIRS:
                            argument(i, j + 1)
                        dve.wait_ge(exp_done, u + 1)
                        dve.wait_ge(score_ready, u + 1)
                        dve.tensor_tensor(st[:, j % 2], psc[:, :, 0:P], arg[:, j % 2], ALU.mult).then_inc(st_done, 1)
                        if running and j + 1 < A_PAIRS:
                            for e in range(2):
                                h = 2 * j + 2 + e
                                dve.wait_ge(qm_turned, h - 1)
                                dve.tensor_tensor(qm[:, e], repeat(qk[:, h * A_QK:(h + 1) * A_QK], DEC_BATCH), spread(g.own[:, :], A_QK), ALU.mult).then_inc(qm_done, 1)
                        dve.wait_ge(num_ready, u + 1)
                        dve.wait_ge(ig_done, 2 * u + 2)
                        dve.tensor_tensor(num[:, 2 * j:2 * j + 2, :], pn[:, :, :], ig[:, j % 2], ALU.add).then_inc(num_done, 1)
                        if not running:
                            dve.wait_ge(state_ready, u + 1)
                            dve.wait_ge(ones, 2)
                            dve.scalar_tensor_tensor(ct[:, j, :], ct[:, j, :], gcc[:, j:j + 1], pc[:, 0:V1], ALU.mult, ALU.add).then_inc(state_done, 1)
                    dve.wait_ge(num_done, i * A_PAIRS + A_PAIRS)
                    c.link(dve.scalar_tensor_tensor(den[:, :], num[:, :, A_V], -1.0, num[:, :, A_V], ALU.mult, ALU.max))
                    c.link(dve.tensor_tensor(den[:, :], den[:, :], tokc[:, KIND_E, :], ALU.max))
                    c.link(dve.reciprocal(den[:, :], den[:, :]))
                    if not below(i, 1):
                        dve.wait_ge(stored, 16 * i)
                    dve.tensor_tensor(hout[:, :, :], num[:, :, 0:A_V], spread(den[:, :], A_V), ALU.mult).then_inc(h_done, 1)

                run(dve, N_C, chunk, c)
                if running:
                    dve.wait_ge(n_loaded, 16 * (NPAIR + 1))
                    nv = nold[:, :].rearrange("s (h d) -> s h d", h=A_H)
                    c.link(dve.tensor_tensor(nv, nv, spread(g.gc_s[:, :], A_QK), ALU.mult))
                    dve.wait_ge(n_ready, 1)
                    dve.tensor_tensor(nold[:, :], pc[0:DEC_BATCH, :], nold[:, :], ALU.add).then_inc(n_done, 1)
                    dve.wait_ge(c0_turned, A_H + 1)
                    for h in range(A_H):
                        bank = pt[:, :, :].rearrange("p a b -> p (a b)") if h % 2 == 0 else pc[:, :]
                        c.link(dve.tensor_tensor(cold[:, h], cold[:, h], spread(g.gc_dec[:, h, :], A_QK), ALU.mult))
                        dve.wait_ge(c_ready, h + 1)
                        cv = cold[:, h].rearrange("v s d -> v (s d)")
                        dve.tensor_tensor(cv, bank, cv, ALU.add).then_inc(c_done, 1)


def fox_gates(nc, g, gates_d, b_f, cache_logf, logf_prompt, logf_sample, ncp_d, ncd_d):
    with Scope(nc, "fgates") as s:
        lf, u, w, lw, ones = (s.sb(n, [B_H, T_ALL]) for n in ("lf", "u", "w", "lw", "ones"))
        bias, cached = s.sb("bias", [B_H, 1]), s.sb("cached", [P, DEC_BATCH, PAST_T, B_H])
        lall, ncd, ncp = s.sb("lall", [B_H, DEC_BATCH, DK]), s.sb("ncd", [B_H, DEC_BATCH, DK]), s.sb("ncp", [B_H, SEQ])
        out, wide = s.sb("out", [P, NT, B_H]), s.sb("wide", [P, DEC_BATCH, DEC_SEQ])
        loaded, filled, made, own_made, abs_done, exp_done, sum_done, ln_done, lf_done, out_turned, out_copied, turned, copied, cum_done, stored, chain_sem, wide_made = (
            s.sem(n) for n in ("loaded", "filled", "made", "own_made", "abs", "exp", "sum", "ln", "lf_done", "out_turned", "out_copied",
                               "turned", "copied", "cum_done", "stored", "chain", "wide"))
        banks = [s.ps(f"turn{i}", [P, CB]) for i in range(2)]
        outp = s.ps("outp", [P, NT, B_H])
        with nc.Block() as block:

            @block.sync
            def _(sp):
                sp.dma_start(lf[:, :], gates_d).then_inc(loaded, 16)
                sp.dma_start(bias[:, :], b_f.rearrange("(h o) -> h o", o=1)).then_inc(loaded, 16)
                for k in range(DEC_BATCH):
                    sp.dma_start(cached[:, k], cache_logf[k].rearrange("(t p) h -> p t h", p=P)).then_inc(loaded, 16)
                sp.wait_ge(out_copied, 1)
                sp.dma_start(logf_prompt[0].rearrange("(t p) h -> p t h", p=P), out[:, 0:NP, :]).then_inc(stored, 16)
                sp.dma_start(logf_sample.rearrange("s t h -> (s t) h"), out[:, NP, :]).then_inc(stored, 16)
                sp.wait_ge(cum_done, 1)
                sp.dma_start(ncp_d, ncp[:, :]).then_inc(stored, 16)
                for k in range(DEC_BATCH):
                    sp.wait_ge(cum_done, 2 + k)
                    sp.dma_start(ncd_d[k], ncd[:, k:k + 1, :].to_broadcast((B_H, DEC_SEQ, DK))).then_inc(stored, 16)
                sp.wait_ge(stored, 16 * (3 + DEC_BATCH))

            @block.gpsimd
            def _(pool):
                pool.memset(ones[:, :], 1.0).then_inc(filled, 1)
                pool.memset(g.own[:, :], 1.0).then_inc(filled, 1)
                pool.memset(wide[:, :, :], 0.0).then_inc(filled, 1)
                pool.wait_ge(filled, 3)
                pool.affine_select(out=g.own[:, :], in_=g.own[:, :], compare_op=ALU.is_ge, fill=0.0,
                                   base=0, pattern=[[-DEC_SEQ, DEC_BATCH]], channel_multiplier=1).then_inc(own_made, 1)
                pool.wait_ge(own_made, 1)
                pool.affine_select(out=g.own[:, :], in_=g.own[:, :], compare_op=ALU.is_ge, fill=0.0,
                                   base=DEC_SEQ - 1, pattern=[[DEC_SEQ, DEC_BATCH]], channel_multiplier=-1).then_inc(own_made, 1)
                pool.affine_select(out=wide[:, :, :], in_=wide[:, :, :], compare_op=ALU.is_ge, fill=NEG,
                                   base=0, pattern=[[-DEC_SEQ, DEC_BATCH], [-1, DEC_SEQ]], channel_multiplier=1).then_inc(made, 1)

            @block.scalar
            def _(act):
                log_sigmoid_act(act, u[:, :], (w[:, :], lw[:, :]), (abs_done, 1), exp_done, (sum_done, 1), ln_done)
                for k in range(DEC_BATCH):
                    act.wait_ge(turned, k + 1)
                    act.activation(lall[:, k, 0:PAST], banks[k % 2][0:B_H, :], ACT.Copy).then_inc(copied, 1)

            @block.vector
            def _(dve):
                c = Chain(dve, chain_sem)
                dve.wait_ge(loaded, 16 * (2 + DEC_BATCH))
                c.link(dve.tensor_scalar(lf[:, :], lf[:, :], bias[:, :], None, ALU.add))
                log_sigmoid_dve(dve, c, lf[:, :], u[:, :], w[:, :], lw[:, :], abs_done, exp_done, sum_done, ln_done)
                dve.sem_inc(lf_done, 1)
                dve.wait_ge(filled, 3)
                dve.tensor_tensor_scan(ncp[:, :], ones[:, 0:SEQ], lf[:, 0:SEQ], 0.0, ALU.mult, ALU.subtract).then_inc(cum_done, 1)
                c.link(dve.tensor_copy(lall[:, :, PAST:DK], lf[:, SEQ:T_ALL].rearrange("h (s t) -> h s t", t=DEC_SEQ)))
                for k in range(DEC_BATCH):
                    dve.wait_ge(copied, k + 1)
                    dve.tensor_tensor_scan(ncd[:, k, :], ones[:, 0:DK], lall[:, k, :], 0.0, ALU.mult, ALU.subtract).then_inc(cum_done, 1)
                dve.wait_ge(out_turned, 1)
                dve.tensor_copy(out[:, :, :], outp[:, :, :]).then_inc(out_copied, 1)
                dve.wait_ge(own_made, 2)
                dve.wait_ge(made, 1)
                c.link(dve.tensor_reduce(g.parity[:, :], g.own[:, :].rearrange("p (c e) -> p e c", e=2), axis=AX.X, op=ALU.add))
                c.link(dve.tensor_tensor(wide[:, :, :], wide[:, :, :], spread(g.own[:, :], DEC_SEQ), ALU.mult))
                c.link(dve.tensor_reduce(g.mask_new[:, :], wide[:, :, :].rearrange("p c k -> p k c"), axis=AX.X, op=ALU.add))

            @block.tensor
            def _(pe):
                pe.wait_ge(loaded, 16 * (2 + DEC_BATCH))
                for k in range(DEC_BATCH):
                    if k >= 2:
                        pe.wait_ge(copied, k - 1)
                    for t in range(PAST_T):
                        ins = pe.transpose(banks[k % 2][0:B_H, t * P:(t + 1) * P], cached[:, k, t, :], g.ident[:, :])
                    ins.then_inc(turned, 1)
                pe.wait_ge(lf_done, 1)
                for t in range(NT):
                    ins = pe.transpose(outp[:, t, :], lf[:, t * P:(t + 1) * P], g.ident[0:B_H, 0:B_H])
                ins.then_inc(out_turned, 1)


def fox_prompt(nc, g, q_d, k_prompt, v_prompt, ncp_d, o_d):
    UNITS = 2 * NP
    CPP = P
    kv = k_prompt.rearrange("(t p) d -> p t d", p=P)
    vv = v_prompt.rearrange("(t p) d -> p t d", p=P)
    qv = q_d[0:NP].rearrange("t p d -> p t d")
    ov = o_d[0:NP].rearrange("t p d -> p t d")

    def groups(u):
        n = u // 2 + 1
        return [range(a, min(a + 4, n)) for a in range(0, n, 4)]

    IN_GROUPS = 4
    first_group, at = [], IN_GROUPS
    for u in range(UNITS):
        first_group.append(at)
        at += len(groups(u))
    PER_PAIR = at
    assert PER_PAIR % 2 == 0

    with Scope(nc, "fprompt") as s:
        kq = s.sb("kq", [P, 2, NP, CPP])
        v, ncum = s.sb("v", [P, NP, CPP]), s.sb("ncum", [P, 2, SEQ])
        kqt = s.sb("kqt", [P, 2, SEQ])
        prob, pt = s.sb("prob", [P, 2, SEQ]), s.sb("pt", [P, 2, NP, P])
        mx, rs, rinv = s.sb("mx", [P, 2]), s.sb("rs", [P, 2]), s.sb("rinv", [P, 2])
        o = s.sb("o", [P, NP, CPP])
        (k_loaded, q_loaded, v_loaded, nc_loaded, turned, copied, scores_ready, shifted, max_done, exp_done, pv_ready, o_done, stored, chain_sem) = (
            s.sem(n) for n in ("k_loaded", "q_loaded", "v_loaded", "nc_loaded", "turned", "copied", "scores_ready", "shifted", "max_done",
                               "exp_done", "pv_ready", "o_done", "stored", "chain"))
        settled = s.sem("settled")
        ps = [s.ps(f"scores{e}", [P, SEQ]) for e in range(2)]
        tb = [s.ps(f"turn{i}", [P, 4, P]) for i in range(2)]
        po = [s.ps(f"o_psum{e}", [P, B_HD]) for e in range(2)]

        with nc.Block() as block:

            @block.sync
            def _(sp):
                def load(j):
                    cols = bass.ds(j * CPP, CPP)
                    if not below(j, 1):
                        wait(sp, turned, (j - 1) * PER_PAIR + IN_GROUPS)
                    sp.dma_start(kq[:, 0], kv[:, :, cols]).then_inc(k_loaded, 16)
                    sp.dma_start(kq[:, 1], qv[:, :, cols]).then_inc(q_loaded, 16)
                    if not below(j, 1):
                        wait(sp, shifted, j * UNITS)
                    for e in range(2):
                        sp.dma_start(ncum[:, e, :], ncp_d[bass.ds(2 * j + e, 1), :].to_broadcast((P, SEQ))).then_inc(nc_loaded, 16)
                    if not below(j, 1):
                        wait(sp, pv_ready, j * UNITS)
                    sp.dma_start(v[:, :, :], vv[:, :, cols]).then_inc(v_loaded, 16)

                run(sp, B_PAIRS, load)
                sp.wait_ge(v_loaded, 16 * B_PAIRS)

            @block.gpsimd
            def _(pool):
                def store(j):
                    wait(pool, o_done, j * UNITS + UNITS)
                    pool.dma_start(ov[:, :, bass.ds(j * CPP, CPP)], o[:, :, :]).then_inc(stored, 16)

                run(pool, B_PAIRS, store)
                pool.wait_ge(stored, 16 * B_PAIRS)

            @block.tensor
            def _(pe):
                def bank_free(j, gi):
                    if gi >= 2 or not below(j, 1):
                        pe.wait_ge(copied, j * PER_PAIR + gi - 1)

                def scores(j, u):
                    i, e = u // 2, u % 2
                    if u >= 2 or not below(j, 1):
                        pe.wait_ge(shifted, j * UNITS + u - 1)
                    es = slice(e * B_HD, (e + 1) * B_HD)
                    width = (i + 1) * P
                    for a in range(0, width, CB):
                        b = min(a + CB, width)
                        pe.matmul(ps[e][:, a:b], kqt[es, 1, i * P:(i + 1) * P], kqt[es, 0, a:b], start=True, stop=(b < width))
                    pe.matmul(ps[e][:, width - P:width], g.ident[:, :], g.mask_qk[:, :], start=False, stop=True).then_inc(scores_ready, 1)

                def turn(j, u):
                    pe.wait_ge(exp_done, j * UNITS + u + 1)
                    for n, tiles in enumerate(groups(u)):
                        gi = first_group[u] + n
                        bank_free(j, gi)
                        for m, t in enumerate(tiles):
                            ins = pe.transpose(tb[gi % 2][:, m, :], prob[:, u % 2, t * P:(t + 1) * P], g.ident[:, :])
                        ins.then_inc(turned, 1)

                def weigh(j, u):
                    i, e = u // 2, u % 2
                    pe.wait_ge(copied, j * PER_PAIR + first_group[u] + len(groups(u)))
                    if u >= 2 or not below(j, 1):
                        pe.wait_ge(o_done, j * UNITS + u - 1)
                    if u == 0:
                        pe.wait_ge(v_loaded, j * 16 + 16)
                    for t in range(i + 1):
                        ins = pe.matmul(po[e][:, :], pt[:, u % 2, t, :], v[:, t, e * B_HD:(e + 1) * B_HD], start=(t == 0), stop=(t == i))
                    ins.then_inc(pv_ready, 1)

                def pair(j):
                    for part in range(2):
                        pe.wait_ge((k_loaded, q_loaded)[part], j * 16 + 16)
                        for h in range(2):
                            gi = 2 * part + h
                            bank_free(j, gi)
                            for m in range(4):
                                ins = pe.transpose(tb[gi % 2][:, m, :], kq[:, part, 4 * h + m, :], g.ident[:, :])
                            ins.then_inc(turned, 1)
                    pe.wait_ge(copied, j * PER_PAIR + IN_GROUPS)
                    scores(j, 0)
                    for u in range(UNITS):
                        if u + 1 < UNITS:
                            scores(j, u + 1)
                        turn(j, u)
                        if u:
                            weigh(j, u - 1)
                    weigh(j, UNITS - 1)

                run(pe, B_PAIRS, pair)

            @block.vector
            def _(dve):
                c = Chain(dve, chain_sem)

                def copy_group(j, gi, dst, n):
                    dve.wait_ge(turned, j * PER_PAIR + gi + 1)
                    dve.tensor_copy(dst, tb[gi % 2][:, 0:n, :]).then_inc(copied, 1)

                def shift(j, u):
                    e, width = u % 2, (u // 2 + 1) * P
                    dve.wait_ge(scores_ready, j * UNITS + u + 1)
                    if u == 0:
                        dve.wait_ge(nc_loaded, j * 32 + 32)
                    if u >= 2 or not below(j, 1):
                        former = first_group[u - 2] + len(groups(u - 2)) if u >= 2 else first_group[UNITS - 2 + u] + len(groups(UNITS - 2 + u)) - PER_PAIR
                        dve.wait_ge(turned, j * PER_PAIR + former)
                    settle(dve, settled)
                    dve.tensor_tensor_reduce(out=prob[:, e, 0:width], in0=ps[e][:, 0:width], in1=ncum[:, e, 0:width], scale=1.0, scalar=-3e38,
                                             op0=ALU.add, op1=ALU.max, accum_out=mx[:, e:e + 1]).then_inc(shifted, 1)
                    dve.wait_ge(shifted, j * UNITS + u + 1)
                    dve.tensor_scalar(mx[:, e:e + 1], mx[:, e:e + 1], -1.0, None, ALU.mult).then_inc(max_done, 1)

                def scale_out(j, u):
                    i, e = u // 2, u % 2
                    c.link(dve.reciprocal(rinv[:, e:e + 1], rs[:, e:e + 1]))
                    dve.wait_ge(pv_ready, j * UNITS + u + 1)
                    if u == 0 and not below(j, 1):
                        dve.wait_ge(stored, j * 16)
                    dve.tensor_scalar(o[:, i, e * B_HD:(e + 1) * B_HD], po[e][:, :], rinv[:, e:e + 1], None, ALU.mult).then_inc(o_done, 1)

                def pair(j):
                    for gi in range(IN_GROUPS):
                        part, h = gi // 2, gi % 2
                        if gi == 0 and not below(j, 1):
                            dve.wait_ge(scores_ready, j * UNITS)
                        copy_group(j, gi, kqt[:, part, h * CB:(h + 1) * CB].rearrange("p (t n) -> p t n", n=P), 4)
                    shift(j, 0)
                    for u in range(UNITS):
                        if u + 1 < UNITS:
                            shift(j, u + 1)
                        for n, tiles in enumerate(groups(u)):
                            if n == 0 and (u >= 2 or not below(j, 1)):
                                dve.wait_ge(pv_ready, j * UNITS + u - 1)
                            copy_group(j, first_group[u] + n, pt[:, u % 2, tiles[0]:tiles[-1] + 1, :], len(tiles))
                        if u:
                            scale_out(j, u - 1)
                    scale_out(j, UNITS - 1)

                run(dve, B_PAIRS, pair, c)

            @block.scalar
            def _(act):
                def pair(j):
                    for u in range(UNITS):
                        e, width = u % 2, (u // 2 + 1) * P
                        act.wait_ge(max_done, j * UNITS + u + 1)
                        if u >= 2 or not below(j, 1):
                            act.wait_ge(o_done, j * UNITS + u - 1)
                        act.activation(prob[:, e, 0:width], prob[:, e, 0:width], ACT.Exp, bias=mx[:, e:e + 1],
                                       accum_out=rs[:, e:e + 1]).then_inc(exp_done, 1)

                run(act, B_PAIRS, pair)


def fox_running(nc, g, q_d, cache_k, cache_v, k_sample, v_sample, ncd_d, half_d, o_d):
    HALVES = 2
    JH = B_PAIRS // HALVES
    NS = DEC_SEQ
    SLOTS = 2
    kc = cache_k.rearrange("s (t p) h d -> s p t (h d)", p=P)
    vc = cache_v.rearrange("s (t p) h d -> s p t (h d)", p=P)
    kn_d, vn_d = k_sample.rearrange("s t h d -> s t (h d)"), v_sample.rearrange("s t h d -> s t (h d)")
    qn_d = q_d[NT - 1].rearrange("(s t) d -> s t d", t=NS)
    with Scope(nc, "frun") as s:
        k, small = s.sb("k", [P, PAST_T, D]), s.sb("small", [NS, 2, D])
        v, vn, ncum = s.sb("v", [P, SLOTS, PAST_T, D]), s.sb("vn", [NS, SLOTS, D]), s.sb("ncum", [P, SLOTS, HALVES, DK])
        kt, ktn, qb = s.sb("kt", [P, B_PAIRS, PAST]), s.sb("ktn", [P, B_PAIRS, NS]), s.sb("qb", [P, B_PAIRS, 2 * NS])
        prob, pt, ptn = s.sb("prob", [P, HALVES, DK]), s.sb("pt", [P, HALVES, PAST_T, P]), s.sb("ptn", [NS, HALVES, P])
        mx, rs, rinv, sel = s.sb("mx", [P, 2]), s.sb("rs", [P, 2]), s.sb("rinv", [P, 2]), s.sb("sel", [P, 2, 2])
        o = s.sb("o", [P, HALVES, B_HD])
        names = ("k_loaded", "kn_loaded", "qn_loaded", "turned", "copied", "small_turned", "kn_copied", "qn_copied", "filled", "scores_ready",
                 "shifted", "max_done", "exp_done", "p_turned", "p_copied", "pv_ready", "o_done", "chain", "moved")
        (k_loaded, kn_loaded, qn_loaded, turned, copied, small_turned, kn_copied, qn_copied, filled, scores_ready,
         shifted, max_done, exp_done, p_turned, p_copied, pv_ready, o_done, chain_sem, moved) = (s.sem(n) for n in names)
        v_loaded, vn_loaded, nc_loaded = ([s.sem(f"{n}{i}") for i in range(SLOTS)] for n in ("v_loaded", "vn_loaded", "nc_loaded"))
        stored = [s.sem(f"stored{i}") for i in range(HALVES)]
        settled, pe_settled = s.sem("settled"), s.sem("pe_settled")
        ps = s.ps("scores", [P, 2 * CB])
        tb = [s.ps(f"turn{i}", [P, 4, P]) for i in range(2)]
        tp = [s.ps(f"pturn{i}", [P, 4, P]) for i in range(2)]
        small_p, po = s.ps("small_p", [P, CB]), s.ps("o_psum", [P, P])

        with nc.Block() as block:

            @block.sync
            def _(sp):
                def load(i2):
                    for slot in range(SLOTS):
                        i = SLOTS * i2 + slot
                        if not below(i, 1):
                            wait(sp, turned, i * B_PAIRS)
                        sp.dma_start(k[:, :, :], kc[i]).then_inc(k_loaded, 16)
                        if not below(i, 1):
                            wait(sp, small_turned, 2 * i)
                        sp.dma_start(small[:, 0], kn_d[i]).then_inc(kn_loaded, 16)
                        sp.dma_start(small[:, 1], qn_d[i]).then_inc(qn_loaded, 16)
                        if not below(i, SLOTS):
                            wait(sp, pv_ready, (i - 1) * HALVES)
                        sp.dma_start(v[:, slot], vc[i]).then_inc(v_loaded[slot], 16)
                        sp.dma_start(vn[:, slot], vn_d[i]).then_inc(vn_loaded[slot], 16)
                        for e in range(HALVES):
                            sp.dma_start(ncum[:, slot, e, :], ncd_d[i, 8 * e:8 * e + 8].rearrange("h q k -> (h q) k")).then_inc(nc_loaded[slot], 16)

                run(sp, DEC_BATCH // SLOTS, load)
                for e in range(HALVES):
                    sp.wait_ge(stored[e], 16 * DEC_BATCH)
                for i in range(DEC_BATCH):
                    sp.dma_start(o_d[NT - 1, i * NS:(i + 1) * NS, :].rearrange("q (h d) -> h q d", d=B_HD),
                                 half_d[i].rearrange("e (h q) d -> (e h) q d", q=NS)).then_inc(moved, 16)
                sp.wait_ge(moved, 16 * DEC_BATCH)

            @block.gpsimd
            def _(pool):
                pool.memset(qb[:, :, :], 0.0).then_inc(filled, 1)

                def store(i):
                    for e in range(HALVES):
                        wait(pool, o_done, i * HALVES + e + 1)
                        pool.dma_start(half_d[i, e], o[:, e, :]).then_inc(stored[e], 16)

                run(pool, DEC_BATCH, store)

            @block.tensor
            def _(pe):
                def stream(i, slot):
                    first = below(i, 1)
                    pe.wait_ge(k_loaded, i * 16 + 16)
                    for j in range(B_PAIRS):
                        if j >= 2 or not first:
                            pe.wait_ge(copied, i * B_PAIRS + j - 1)
                        for t in range(PAST_T):
                            ins = pe.transpose(tb[j % 2][:, t, :], k[:, t, j * P:(j + 1) * P], g.ident[:, :])
                        ins.then_inc(turned, 1)
                    for part, (loaded, used) in enumerate(((kn_loaded, qn_copied), (qn_loaded, kn_copied))):
                        pe.wait_ge(loaded, i * 16 + 16)
                        if part or not first:
                            pe.wait_ge(used, i + part)
                        settle(pe, pe_settled)
                        for j in range(B_PAIRS):
                            ins = pe.transpose(small_p[:, j * NS:(j + 1) * NS], small[:, part, j * P:(j + 1) * P], g.ident[0:NS, 0:NS])
                        ins.then_inc(small_turned, 1)
                    pe.wait_ge(copied, i * B_PAIRS + B_PAIRS)
                    pe.wait_ge(kn_copied, i + 1)
                    pe.wait_ge(qn_copied, i + 1)

                    def scores(e):
                        u = i * HALVES + e
                        if not below(u, 1):
                            pe.wait_ge(shifted, u)
                        for n in range(JH):
                            pe.matmul(ps[32 * n:32 * n + 32, 0:PAST], qb[:, JH * e + n, :], kt[:, JH * e + n, :], start=True, stop=True)
                        for n in range(JH):
                            rows = slice(32 * n, 32 * n + 32)
                            pe.matmul(ps[rows, CB:CB + NS], qb[:, JH * e + n, :], ktn[:, JH * e + n, :], start=True, stop=False)
                            ins = pe.matmul(ps[rows, CB:CB + NS], g.ident[:, rows], g.mask_new[:, :], start=False, stop=True)
                        ins.then_inc(scores_ready, 1)

                    def turn_and_weigh(e):
                        u = i * HALVES + e
                        pe.wait_ge(exp_done, u + 1)
                        if not below(u, 1):
                            pe.wait_ge(p_copied, 2 * u)
                        for t in range(PAST_T):
                            ins = pe.transpose(tp[0][:, t, :], prob[:, e, t * P:(t + 1) * P], g.ident[:, :])
                        ins.then_inc(p_turned, 1)
                        pe.transpose(tp[1][0:NS, 0, :], prob[:, e, PAST:DK], g.ident[:, :]).then_inc(p_turned, 1)
                        pe.wait_ge(p_copied, 2 * u + 2)
                        if not below(u, 1):
                            pe.wait_ge(o_done, u)
                        if e == 0:
                            pe.wait_ge(v_loaded[slot], (i - slot) * 8 + 16)
                            pe.wait_ge(vn_loaded[slot], (i - slot) * 8 + 16)
                        for n in range(JH):
                            rows, cols = slice(32 * n, 32 * n + 32), slice((JH * e + n) * P, (JH * e + n + 1) * P)
                            for t in range(PAST_T):
                                pe.matmul(po[rows, :], pt[:, e, t, rows], v[:, slot, t, cols], start=(t == 0), stop=False)
                            ins = pe.matmul(po[rows, :], ptn[:, e, rows], vn[:, slot, cols], start=False, stop=True)
                        ins.then_inc(pv_ready, 1)

                    scores(0)
                    scores(1)
                    turn_and_weigh(0)
                    turn_and_weigh(1)

                run(pe, DEC_BATCH // SLOTS, lambda i2: [stream(SLOTS * i2 + slot, slot) for slot in range(SLOTS)])

            @block.scalar
            def _(act):
                def stream(i, slot):
                    for j in range(B_PAIRS):
                        act.wait_ge(turned, i * B_PAIRS + j + 1)
                        if j == 0 and not below(i, 1):
                            act.wait_ge(scores_ready, i * HALVES)
                        act.activation(kt[:, j, :], tb[j % 2][:, :, :].rearrange("p t n -> p (t n)"), ACT.Copy).then_inc(copied, 1)
                    act.wait_ge(small_turned, 2 * i + 1)
                    act.activation(ktn[:, :, :], small_p[:, 0:B_PAIRS * NS].rearrange("p (j n) -> p j n", n=NS), ACT.Copy).then_inc(kn_copied, 1)
                    for e in range(HALVES):
                        u = i * HALVES + e
                        act.wait_ge(max_done, u + 1)
                        if not below(u, HALVES):
                            act.wait_ge(o_done, u - 1)
                        act.activation(prob[:, e, :], prob[:, e, :], ACT.Exp, bias=mx[:, e:e + 1], accum_out=rs[:, e:e + 1]).then_inc(exp_done, 1)

                run(act, DEC_BATCH // SLOTS, lambda i2: [stream(SLOTS * i2 + slot, slot) for slot in range(SLOTS)])

            @block.vector
            def _(dve):
                c = Chain(dve, chain_sem)

                def stream(i, slot):
                    dve.wait_ge(small_turned, 2 * i + 2)
                    dve.wait_ge(filled, 1)
                    for half in range(2):
                        rows = slice(half * B_HD, (half + 1) * B_HD)
                        ins = dve.tensor_copy(qb[rows, :, half * NS:(half + 1) * NS], small_p[rows, 0:B_PAIRS * NS].rearrange("p (j n) -> p j n", n=NS))
                        if half == 0:
                            c.link(ins)
                    ins.then_inc(qn_copied, 1)
                    for e in range(HALVES):
                        u = i * HALVES + e
                        dve.wait_ge(scores_ready, u + 1)
                        dve.wait_ge(nc_loaded[slot], (i - slot) * 16 + 32)
                        if not below(u, HALVES):
                            dve.wait_ge(p_turned, 2 * u - 2)
                        settle(dve, settled)
                        dve.tensor_tensor_reduce(out=prob[:, e, :], in0=ps[:, 0:DK], in1=ncum[:, slot, e, :], scale=1.0, scalar=-3e38,
                                                 op0=ALU.add, op1=ALU.max, accum_out=mx[:, e:e + 1]).then_inc(shifted, 1)
                        dve.wait_ge(shifted, u + 1)
                        dve.tensor_scalar(mx[:, e:e + 1], mx[:, e:e + 1], -1.0, None, ALU.mult).then_inc(max_done, 1)
                    for e in range(HALVES):
                        u = i * HALVES + e
                        dve.wait_ge(p_turned, 2 * u + 1)
                        dve.tensor_copy(pt[:, e], tp[0][:, :, :]).then_inc(p_copied, 1)
                        dve.wait_ge(p_turned, 2 * u + 2)
                        dve.tensor_copy(ptn[:, e], tp[1][0:NS, 0, :]).then_inc(p_copied, 1)
                        c.link(dve.reciprocal(rinv[:, e:e + 1], rs[:, e:e + 1]))
                        c.link(dve.tensor_scalar(sel[:, e, :], g.parity[:, :], rinv[:, e:e + 1], None, ALU.mult))
                        dve.wait_ge(pv_ready, u + 1)
                        if not below(i, 1):
                            dve.wait_ge(stored[e], i * 16)
                        c.link(dve.tensor_scalar(o[:, e, :], po[:, 0:B_HD], sel[:, e, 0:1], None, ALU.mult))
                        dve.scalar_tensor_tensor(o[:, e, :], po[:, B_HD:P], sel[:, e, 1:2], o[:, e, :], ALU.mult, ALU.add).then_inc(o_done, 1)

                run(dve, DEC_BATCH // SLOTS, lambda i2: [stream(SLOTS * i2 + slot, slot) for slot in range(SLOTS)], c)


def store_x(nc, g, y_prompt, y_sample):
    with Scope(nc, "out") as s:
        stored = s.sem("stored")
        with nc.Block() as block:

            @block.sync
            def _(sp):
                sp.dma_start(y_prompt.rearrange("(t p) d -> p t d", p=P), g.x[:, 0:NP, :]).then_inc(stored, 16)
                sp.dma_start(y_sample, g.x[:, NP, :]).then_inc(stored, 16)
                sp.wait_ge(stored, 32)


def build(nc, A, O):
    (y_prompt, y_sample, k_prompt, v_prompt, logf_prompt, c_prompt, n_prompt, m_prompt,
     k_sample, v_sample, logf_sample, c_sample, n_sample, m_sample) = O

    def scratch(name, shape):
        return nc.dram_tensor(name, shape, fp32, kind="Internal").ap()

    qkvo = scratch("qkvo", (NT, P, A_O0 + A_H * A_V))
    gates_d = scratch("mlstm_gates_rows", (2 * A_H, T_ALL))
    h_d = scratch("mlstm_h", (NT, P, D))
    fgates_d = scratch("fox_gates_rows", (B_H, T_ALL))
    q_d, sg_d, o_d = scratch("fox_q", (NT, P, D)), scratch("fox_out_gate", (NT, P, D)), scratch("fox_o", (NT, P, D))
    ncp_d = scratch("neg_cum_prompt", (B_H, SEQ))
    ncd_d = scratch("neg_cum_running", (DEC_BATCH, B_H, DEC_SEQ, DK))
    half_d = scratch("fox_o_running", (DEC_BATCH, 2, P, B_HD))

    class Globals:
        pass

    g = Globals()
    with Scope(nc, "g") as top:
        g.x = top.sb("x", [P, NT, D])
        g.ident = top.sb("ident", [P, P])
        g.one = top.sb("one", [P, 1])
        g.mask_kq, g.mask_qk = top.sb("mask_kq", [P, 2, P]), top.sb("mask_qk", [P, P])
        setup(nc, g, A["x_prompt"][0], A["x_sample"].rearrange("s t d -> (s t) d"))
        with Scope(nc, "A1") as s:
            xth, xtl = s.sb("xth", [P, KC, T_ALL], fp32r), s.sb("xtl", [P, KC, T_ALL], fp32r)
            build_xt(nc, g, xth, xtl, "xt_mix0", "norm", gain_row=A["g_mix"][0:1, :])
            linear(nc, g, xth, xtl, "w_in", A["w_in_a"][0],
                   [(0, 4, "store", lambda b, t: qkvo[t, :, bass.ds(b * CB, CB)]),
                    (A_O0, 2, "sigmoid", lambda b, t: qkvo[t, :, bass.ds(A_O0 + b * CB, CB)])],
                   gates=(A_O0 + A_H * A_V, 2 * A_H, gates_d))
        with Scope(nc, "A2") as s:
            g.sel, g.pair_sel = s.sb("sel", [A_H, A_H, P]), s.sb("pair_sel", [A_H, A_PAIRS, 2, A_QK])
            g.own, g.ones8 = s.sb("own", [P, DEC_BATCH]), s.sb("ones8", [A_H, P])
            g.mask_dec = s.sb("mask_dec", [P, 2, P])
            g.B, g.tok = s.sb("B", [A_H, T_ALL]), s.sb("tok", [P, NT, 4, A_H])
            g.gc_pair, g.gc_dec, g.gc_s = s.sb("gc_pair", [P, A_PAIRS, NP]), s.sb("gc_dec", [P, A_H, DEC_BATCH]), s.sb("gc_s", [DEC_BATCH, A_H])
            mlstm_gates(nc, g, gates_d, A["b_i_a"], A["b_f_a"], A["state_m"], m_prompt, m_sample)
            mlstm(nc, g, qkvo, h_d, False, c_prompt, n_prompt)
            mlstm(nc, g, qkvo, h_d, True, c_sample, n_sample, A["state_c"], A["state_n"])
        with Scope(nc, "A3") as s:
            xth, xtl = s.sb("xth", [P, KC, T_ALL], fp32r), s.sb("xtl", [P, KC, T_ALL], fp32r)
            build_xt(nc, g, xth, xtl, "xt_h", "mlstm", a=h_d, b=qkvo[:, :, A_O0:A_O0 + D], gain_row=A["g_head_a"])
            linear(nc, g, xth, xtl, "w_out", A["w_out_a"][0], [(0, 2, "residual", None)])
            build_xt(nc, g, xth, xtl, "xt_ffn0", "norm", gain_row=A["g_ffn"][0:1, :])
            ffn(nc, g, xth, xtl, "ffn0", A["w_gu"][0], A["w_down"][0])

            def rows(prompt, sample):
                pv, sv = prompt.rearrange("o (t p) h d -> (o t) p (h d)", p=P), sample.rearrange("s t h d -> (s t) (h d)")
                return lambda b, t: (pv[t] if t < NP else sv)[:, bass.ds(b * CB, CB)]

            build_xt(nc, g, xth, xtl, "xt_kv", "norm", gain_row=A["g_kv"].rearrange("(o d) -> o d", o=1))
            linear(nc, g, xth, xtl, "w_kvf", A["w_kvf"],
                   [(0, 2, ("norm", A["g_k"].rearrange("(o d) -> o d", o=1), 1.0), rows(k_prompt, k_sample)),
                    (D, 2, "store", rows(v_prompt, v_sample))], gates=(2 * D, B_H, fgates_d))
            build_xt(nc, g, xth, xtl, "xt_mix1", "norm", gain_row=A["g_mix"][1:2, :])
            linear(nc, g, xth, xtl, "w_qg", A["w_qg_b"][0],
                   [(0, 2, ("norm", A["g_q_b"], B_HD ** -0.5), lambda b, t: q_d[t, :, bass.ds(b * CB, CB)]),
                    (D, 2, "sigmoid", lambda b, t: sg_d[t, :, bass.ds(b * CB, CB)])])
        with Scope(nc, "B1") as s:
            g.own, g.parity, g.mask_new = s.sb("own", [P, DEC_BATCH]), s.sb("parity", [P, 2]), s.sb("mask_new", [P, DEC_SEQ])
            fox_gates(nc, g, fgates_d, A["b_f_b"], A["cache_logf"], logf_prompt, logf_sample, ncp_d, ncd_d)
            fox_prompt(nc, g, q_d, k_prompt.rearrange("o t h d -> (o t) (h d)"), v_prompt.rearrange("o t h d -> (o t) (h d)"), ncp_d, o_d)
            fox_running(nc, g, q_d, A["cache_k"], A["cache_v"], k_sample, v_sample, ncd_d, half_d, o_d)
        with Scope(nc, "B2") as s:
            xth, xtl = s.sb("xth", [P, KC, T_ALL], fp32r), s.sb("xtl", [P, KC, T_ALL], fp32r)
            build_xt(nc, g, xth, xtl, "xt_o", "gated", a=o_d, b=sg_d)
            linear(nc, g, xth, xtl, "w_o", A["w_o_b"][0], [(0, 2, "residual", None)])
            build_xt(nc, g, xth, xtl, "xt_ffn1", "norm", gain_row=A["g_ffn"][1:2, :])
            ffn(nc, g, xth, xtl, "ffn1", A["w_gu"][1], A["w_down"][1])
        store_x(nc, g, y_prompt[0], y_sample.rearrange("s t d -> (s t) d"))


_INS = ['x_prompt', 'x_sample', 'cache_k', 'cache_v', 'cache_logf', 'state_c', 'state_n', 'state_m', 'g_mix', 'g_ffn',
        'w_in_a', 'b_i_a', 'b_f_a', 'g_head_a', 'w_out_a', 'g_kv', 'w_kvf', 'b_f_b', 'g_k', 'w_qg_b', 'g_q_b', 'w_o_b',
        'w_gu', 'w_down']
_OUTS = [(1, SEQ, D), (DEC_BATCH, DEC_SEQ, D), (1, SEQ, B_H, B_HD), (1, SEQ, B_H, B_HD), (1, SEQ, B_H),
         (1, 1, A_H, A_V, A_QK), (1, 1, A_H, A_QK), (1, 1, A_H),
         (DEC_BATCH, DEC_SEQ, B_H, B_HD), (DEC_BATCH, DEC_SEQ, B_H, B_HD), (DEC_BATCH, DEC_SEQ, B_H),
         (DEC_BATCH, 1, A_H, A_V, A_QK), (DEC_BATCH, 1, A_H, A_QK), (DEC_BATCH, 1, A_H)]


def kernel(**inputs):
    import numpy as _np
    import concourse.bacc as _bacc
    from concourse import mybir as _mybir
    from concourse.bass_utils import run_bass_kernel_spmd as _run

    nc = _bacc.Bacc("TRN2", target_bir_lowering=False, num_devices=1)
    arrays, args = {}, {}
    for name in _INS:
        a = _np.ascontiguousarray(inputs[name])
        arrays[f"in_{name}_dram"] = a
        args[name] = nc.dram_tensor(f"in_{name}_dram", a.shape, _mybir.dt.from_np(a.dtype), kind="ExternalInput").ap()
    outs = [nc.dram_tensor(f"out_{i}_dram", shape, _mybir.dt.float32, kind="ExternalOutput").ap() for i, shape in enumerate(_OUTS)]
    build(nc, args, outs)
    r = _run(nc, [arrays], core_ids=[0])
    return tuple(r.results[0][f"out_{i}_dram"] for i in range(len(_OUTS)))
```

```python
import concourse.bass as bass
from concourse import mybir
from contextlib import ExitStack, contextmanager

fp32 = mybir.dt.float32
fp32r = mybir.dt.float32r
ACT = mybir.ActivationFunctionType
ALU = mybir.AluOpType
AX = mybir.AxisListType

P = 128
D = 1024
SEQ = 1024
DEC_BATCH, DEC_SEQ, PAST = 8, 16, 512
T_ALL = SEQ + DEC_BATCH * DEC_SEQ
NT = T_ALL // P
NP = SEQ // P
KC = D // P
CB = 512
THIRD = T_ALL // 3
A_H, A_QK, A_V = 8, 64, 128
A_PAIRS = A_H // 2
B_H, B_HD = 16, 64
B_PAIRS = B_H // 2
D_FF = 2816
FG = 2
FFN_GROUPS = D_FF // (FG * P)
EPS = 1e-6
CAP = 15.0
NEG = -1e30
A_Q0, A_K0, A_V0, A_O0 = 0, 512, 1024, 2048
PAST_T = PAST // P
DK = PAST + DEC_SEQ


def below(i, n):
    return isinstance(i, int) and i < n


def wait(engine, sem, count):
    if not isinstance(count, int):
        engine.wait_ge(sem, 1)
    engine.wait_ge(sem, count)


def settle(engine, sem):
    engine.sem_inc(sem, 1)


def round_high(pool, g, out, in_):
    ones = g.one[:, :].rearrange("p (a b) -> p a b", a=1).to_broadcast((P, *in_.shape[1:]))
    return pool.tensor_tensor(out, in_, ones, ALU.mult)


class Chain:

    def __init__(self, engine, sem):
        self.engine, self.sem, self.n, self.base = engine, sem, 0, 0

    def link(self, ins):
        self.n += 1
        ins.then_inc(self.sem, 1)
        self.engine.wait_ge(self.sem, self.base + self.n)


def run(engine, count, body, chain=None, peel_last=False):
    start = chain.n if chain else 0
    end = count - 1 if peel_last else count
    body(0)
    per = chain.n - start if chain else 0
    if end > 1:
        with engine.Fori(1, end) as i:
            if chain:
                chain.base, chain.n = start + i * per, 0
            body(i)
            if chain:
                assert chain.n == per
        if chain:
            chain.base, chain.n = 0, start + end * per
    if peel_last:
        body(count - 1)


class Scope:

    def __init__(self, nc, tag):
        self.nc, self.tag, self.ctx, self.sems = nc, tag, ExitStack(), []

    def __enter__(self):
        return self

    def __exit__(self, *a):
        if a[0] is not None:
            return
        if self.sems:
            self.nc.clear_and_free_semaphores(self.sems)
            self.nc.all_engine_barrier()
        self.ctx.close()

    def sb(self, name, shape, dt=fp32):
        return self.ctx.enter_context(self.nc.sbuf_tensor(f"{self.tag}_{name}", shape, dt))

    def brief(self, name, shape):
        with self.nc.sbuf_tensor(f"{self.tag}_{name}", shape, fp32) as tile:
            return tile

    def ps(self, name, shape):
        cols = 1
        for n in shape[1:]:
            cols *= n
        banks = -(-cols // CB)
        whole = self.ctx.enter_context(self.nc.psum_tensor(f"{self.tag}_{name}", [P, banks * CB], fp32))
        letters = "abc"[:len(shape) - 1]
        sizes = {k: n for k, n in zip(letters, shape[1:])}
        return whole[:, 0:cols].rearrange(f"p ({' '.join(letters)}) -> p {' '.join(letters)}", **sizes)

    def sem(self, name):
        self.sems.append(self.nc.alloc_semaphore(f"{self.tag}_{name}"))
        return self.sems[-1]


def spread(ap, n):
    return ap.rearrange("p (h o) -> p h o", o=1).to_broadcast((ap.shape[0], ap.shape[1], n))


def repeat(ap, n):
    return ap.rearrange("p (o d) -> p o d", o=1).to_broadcast((ap.shape[0], n, ap.shape[1]))


def f32(ap):
    return ap.bitcast(fp32)


def setup(nc, g, x_prompt, x_sample):
    with Scope(nc, "setup") as s:
        x_loaded, made, filled = s.sem("x_loaded"), s.sem("made"), s.sem("filled")
        with nc.Block() as block:

            @block.sync
            def _(sp):
                sp.dma_start(g.x[:, 0:NP, :], x_prompt.rearrange("(t p) d -> p t d", p=P)).then_inc(x_loaded, 16)
                sp.dma_start(g.x[:, NP, :], x_sample).then_inc(x_loaded, 16)
                wait(sp, x_loaded, 32)

            @block.gpsimd
            def _(pool):
                pool.memset(g.one[:, :], 1.0).then_inc(filled, 1)
                pool.memset(g.ident[:, :], 0.0).then_inc(filled, 1)
                pool.memset(g.mask_kq[:, :, :], 0.0).then_inc(filled, 1)
                pool.memset(g.mask_qk[:, :], 0.0).then_inc(filled, 1)
                wait(pool, filled, 4)
                pool.affine_select(out=g.ident[:, :], in_=g.ident[:, :], compare_op=ALU.not_equal, fill=1.0,
                                   base=0, pattern=[[-1, P]], channel_multiplier=1).then_inc(made, 1)
                pool.affine_select(out=g.mask_kq[:, :, :], in_=g.mask_kq[:, :, :], compare_op=ALU.is_ge, fill=NEG,
                                   base=0, pattern=[[0, 2], [1, P]], channel_multiplier=-1).then_inc(made, 1)
                pool.affine_select(out=g.mask_qk[:, :], in_=g.mask_qk[:, :], compare_op=ALU.is_ge, fill=NEG,
                                   base=0, pattern=[[-1, P]], channel_multiplier=1).then_inc(made, 1)
                wait(pool, made, 3)


class Activations:
    SLOTS = 2
    HV = "p (h v) -> p h v"

    def __init__(self, nc, g, s, xth, xtl, kind, tok, psum, a=None, b=None, gain_row=None):
        self.g, self.xth, self.xtl, self.kind, self.a, self.b, self.gain_row = g, xth, xtl, kind, a, b, gain_row
        self.tok, self.psum = tok, psum
        self.gain_loaded, self.tile_made = s.sem("x_gain_loaded"), s.sem("tile_made")
        self.transposed, self.high_done, self.low_done = s.sem("transposed"), s.sem("high_done"), s.sem("low_done")
        self.square_done, self.mean_done, self.root_done, self.chain_sem = (s.sem(n) for n in ("x_square", "x_mean", "x_root", "x_chain"))
        if kind != "gated":
            self.gain = s.sb("x_gain", [P, D])
        if kind == "norm":
            self.ss, self.rms = s.sb("x_ss", [P, NT]), s.sb("x_rms", [P, NT])
        else:
            self.b_in = s.sb("b_in", [P, self.SLOTS, D])
            self.a_loaded = [s.sem(f"a_loaded{i}") for i in range(self.SLOTS)]
            self.b_loaded = [s.sem(f"b_loaded{i}") for i in range(self.SLOTS)]
            self.b_scaled = s.sem("b_scaled")
        if kind == "mlstm":
            self.junk, self.ss, self.rms = s.sb("junk", [P, D]), s.sb("x_ss", [P, A_H]), s.sb("x_rms", [P, A_H])

    def load_gain(self, sp):
        if self.kind != "gated":
            sp.dma_start(self.gain[:, :], self.gain_row.to_broadcast((P, D))).then_inc(self.gain_loaded, 16)

    def scale_gates(self, pool, t):
        if self.kind != "mlstm" or t >= NT:
            return
        k = t % self.SLOTS
        if t == 0:
            wait(pool, self.gain_loaded, 16)
        wait(pool, self.b_loaded[k], t // self.SLOTS * 16 + 16)
        pool.tensor_tensor(self.b_in[:, k, :], self.b_in[:, k, :], self.gain[:, :], ALU.mult).then_inc(self.b_scaled, 1)

    def load(self, act, t):
        if self.kind == "norm" or t >= NT:
            return
        k = t % self.SLOTS
        if t >= self.SLOTS:
            act.wait_ge(self.transposed, 2 * (t - self.SLOTS) + 2)
        act.dma_start(self.tok[:, k, :], self.a[t]).then_inc(self.a_loaded[k], 16)
        act.dma_start(self.b_in[:, k, :], self.b[t]).then_inc(self.b_loaded[k], 16)

    def root(self, act, t):
        if self.kind == "gated" or t >= NT:
            return
        k = t % self.SLOTS
        if self.kind == "norm":
            if t >= self.SLOTS:
                act.wait_ge(self.transposed, 2 * (t - self.SLOTS) + 2)
            act.activation(self.tok[:, k, :], self.g.x[:, t, :], ACT.Square, accum_out=self.ss[:, t:t + 1]).then_inc(self.square_done, 1)
            act.wait_ge(self.mean_done, t + 1)
            act.activation(self.rms[:, t:t + 1], self.ss[:, t:t + 1], ACT.Sqrt).then_inc(self.root_done, 1)
            return
        act.wait_ge(self.a_loaded[k], t // self.SLOTS * 16 + 16)
        if t:
            act.wait_ge(self.mean_done, t)
        act.activation(self.junk[:, :], self.tok[:, k, :], ACT.Square).then_inc(self.square_done, 1)
        act.wait_ge(self.mean_done, t + 1)
        act.activation(self.rms[:, :], self.ss[:, :], ACT.Sqrt).then_inc(self.root_done, 1)

    def high(self, act, t):
        if t >= NT:
            return
        for q in range(2):
            act.wait_ge(self.transposed, 2 * t + q + 1)
            act.activation(self.xth[:, 4 * q:4 * q + 4, t * P:(t + 1) * P],
                           self.psum[q][:, :].rearrange("p (c n) -> p c n", n=P), ACT.Copy).then_inc(self.high_done, 1)
        self.load(act, t + self.SLOTS)
        self.root(act, t + self.SLOTS)

    def make(self, dve, c, t):
        if t >= NT:
            return
        k = t % self.SLOTS
        tile = self.tok[:, k, :]
        if self.kind == "norm":
            dve.wait_ge(self.square_done, t + 1)
            dve.tensor_scalar(self.ss[:, t:t + 1], self.ss[:, t:t + 1], 1.0 / D, EPS, ALU.mult, ALU.add).then_inc(self.mean_done, 1)
            dve.wait_ge(self.root_done, t + 1)
            c.link(dve.reciprocal(self.rms[:, t:t + 1], self.rms[:, t:t + 1]))
            if t == 0:
                dve.wait_ge(self.gain_loaded, 16)
            dve.scalar_tensor_tensor(tile, self.g.x[:, t, :], self.rms[:, t:t + 1], self.gain[:, :],
                                     ALU.mult, ALU.mult).then_inc(self.tile_made, 1)
            return
        if self.kind == "gated":
            dve.wait_ge(self.a_loaded[k], t // self.SLOTS * 16 + 16)
            dve.wait_ge(self.b_loaded[k], t // self.SLOTS * 16 + 16)
            dve.tensor_tensor(tile, tile, self.b_in[:, k, :], ALU.mult).then_inc(self.tile_made, 1)
            return
        dve.wait_ge(self.square_done, t + 1)
        c.link(dve.tensor_reduce(self.ss[:, :], self.junk[:, :].rearrange(self.HV, v=A_V), axis=AX.X, op=ALU.add))
        dve.tensor_scalar(self.ss[:, :], self.ss[:, :], 1.0 / A_V, EPS, ALU.mult, ALU.add).then_inc(self.mean_done, 1)
        dve.wait_ge(self.root_done, t + 1)
        c.link(dve.reciprocal(self.rms[:, :], self.rms[:, :]))
        c.link(dve.tensor_tensor(tile.rearrange(self.HV, v=A_V), tile.rearrange(self.HV, v=A_V), spread(self.rms[:, :], A_V), ALU.mult))
        dve.wait_ge(self.b_scaled, t + 1)
        dve.tensor_tensor(tile, tile, self.b_in[:, k, :], ALU.mult).then_inc(self.tile_made, 1)

    def low(self, dve, c, t):
        if t >= NT:
            return
        for q in range(2):
            dve.wait_ge(self.high_done, 2 * t + q + 1)
            cs, ts = slice(4 * q, 4 * q + 4), slice(t * P, (t + 1) * P)
            dve.tensor_tensor(self.xtl[:, cs, ts], self.psum[q][:, :].rearrange("p (c n) -> p c n", n=P),
                              f32(self.xth[:, cs, ts]), ALU.subtract).then_inc(self.low_done, 1)
        self.make(dve, c, t + self.SLOTS)

    def start_act(self, act):
        for t in range(self.SLOTS):
            self.load(act, t)
        for t in range(self.SLOTS):
            self.root(act, t)

    def start_dve(self, dve, c):
        for t in range(self.SLOTS):
            self.make(dve, c, t)

    def transpose(self, pe, t):
        if t >= NT:
            return
        pe.wait_ge(self.tile_made, t + 1)
        for q in range(2):
            if t:
                pe.wait_ge(self.low_done, 2 * (t - 1) + q + 1)
            for n in range(4):
                ins = pe.transpose(self.psum[q][:, n * P:(n + 1) * P],
                                   self.tok[:, t % self.SLOTS, (4 * q + n) * P:(4 * q + n + 1) * P], self.g.ident[:, :])
            ins.then_inc(self.transposed, 1)


def linear(nc, g, xth, xtl, tag, w, segments, gates=None, **source):
    BANKS = 3
    wv = w.rearrange("(k p) n -> p k n", p=P)
    QUARTERS = 4
    HK = KC // QUARTERS
    nb = sum(n for _, n, _, _ in segments)
    with Scope(nc, tag) as s:
        raw = s.sb("raw", [P, 2, HK, CB])
        wh, wl = s.sb("wh", [P, 2, KC, CB], fp32r), s.sb("wl", [P, 2, KC, CB], fp32r)
        if segments[0][2] != "residual":
            stage = s.sb("stage", [P, BANKS, CB])
        normed = [m for _, _, m, _ in segments if isinstance(m, tuple)]
        loaded = [s.sem(f"w_loaded{i}") for i in range(2)]
        w_split, high_sem = s.sem("w_split"), s.sem("w_high")
        psum_ready, stage_ready = s.sem("psum_ready"), s.sem("stage_ready")
        psum_used = [s.sem(f"psum_used{i}") for i in range(len(segments))]
        stored = [s.sem(f"stored{i}") for i in range(BANKS)]
        psum = [s.ps(f"y{i}", [P, CB]) for i in range(BANKS)]
        if normed:
            gain_small, gain = s.sb("gain_small", [P, B_HD]), s.sb("gain", [P, B_HD])
            squares, ss, rms = s.sb("squares", [P, CB]), s.sb("ss", [P, A_H]), s.sb("rms", [P, A_H])
            gain_loaded, square_done, mean_done, root_done = s.sem("gain_loaded"), s.sem("square"), s.sem("mean"), s.sem("root")
        chain_sem = s.sem("chain")
        tok = s.brief("tok", [P, Activations.SLOTS, D]) if gates else s.sb("tok", [P, Activations.SLOTS, D])
        if gates:
            gh, gl = s.sb("gh", [P, KC, P], fp32r), s.sb("gl", [P, KC, P], fp32r)
        xt = Activations(nc, g, s, xth, xtl, tok=tok, psum=[s.ps(f"xt{i}", [P, CB]) for i in range(2)], **source)
        if gates:
            g_col, g_n, g_dst = gates
            g_raw = s.sb("g_raw", [P, KC, g_n])
            g_out = stage[0:g_n, :, :].rearrange("p a n -> p (a n)")
            g_loaded, g_split, g_ready, g_copied, g_stored = (s.sem(n) for n in ("g_loaded", "g_split", "g_ready", "g_copied", "g_stored"))
            g_psum = [s.ps(f"g{i}", [P, THIRD]) for i in range(3)]

        def each_segment(engine, body, chain=None, when=lambda m: True):
            b0 = 0
            for n, (col0, blocks, mode, target) in enumerate(segments):
                if when(mode):
                    start = chain.n if chain else 0
                    pairs = blocks // 2
                    run(engine, pairs, lambda i: body(n, i, b0), chain)
                b0 += blocks

        with nc.Block() as block:

            @block.sync
            def _(sp):
                if normed:
                    sp.dma_start(gain_small[:, :], normed[0][1].to_broadcast((P, B_HD))).then_inc(gain_loaded, 16)

                xt.load_gain(sp)

                def load(n, i, b0):
                    for par in range(2):
                        b = b0 + 2 * i + par
                        col = segments[n][0] + (2 * i + par) * CB
                        for h in range(QUARTERS):
                            if h >= 2 or not below(b, 1):
                                wait(sp, w_split, QUARTERS * b + h - 1)
                            sp.dma_start(raw[:, h % 2], wv[:, h * HK:(h + 1) * HK, bass.ds(col, CB)]).then_inc(loaded[h % 2], 16)

                each_segment(sp, load)
                if gates:
                    sp.dma_start(g_raw[:, :, :], wv[:, :, g_col:g_col + g_n]).then_inc(g_loaded, 16)
                    wait(sp, g_copied, 3)
                    sp.dma_start(g_dst, g_out[:, 0:T_ALL]).then_inc(g_stored, 16)
                    wait(sp, g_stored, 16)

            @block.gpsimd
            def _(pool):
                def split(n, i, b0):
                    for par in range(2):
                        b = b0 + 2 * i + par
                        for h in range(QUARTERS):
                            wait(pool, loaded[h % 2], (2 * b + h // 2) * 16 + 16)
                            if not below(b, 2):
                                wait(pool, psum_ready, (b - 1) * NT)
                            ks = slice(h * HK, (h + 1) * HK)
                            round_high(pool, g, wh[:, par, ks], raw[:, h % 2]).then_inc(high_sem, 1)
                            wait(pool, high_sem, QUARTERS * b + h + 1)
                            pool.tensor_tensor(wl[:, par, ks], raw[:, h % 2], f32(wh[:, par, ks]), ALU.subtract).then_inc(w_split, 1)
                            if below(b, 1):
                                xt.scale_gates(pool, h)
                        if below(b, 1):
                            for t in range(QUARTERS, NT):
                                xt.scale_gates(pool, t)

                each_segment(pool, split)
                if gates:
                    wait(pool, g_loaded, 16)
                    wait(pool, xt.transposed, 2 * NT)
                    pool.memset(f32(gh[:, :, :]), 0.0).then_inc(g_split, 1)
                    pool.memset(f32(gl[:, :, :]), 0.0).then_inc(g_split, 1)
                    wait(pool, g_split, 2)
                    pool.tensor_copy(gh[:, :, 0:g_n], g_raw[:, :, :]).then_inc(g_split, 1)
                    wait(pool, g_split, 3)
                    pool.tensor_tensor(gl[:, :, 0:g_n], g_raw[:, :, :], f32(gh[:, :, 0:g_n]), ALU.subtract).then_inc(g_split, 1)

            @block.tensor
            def _(pe):
                def products(n, i, b0):
                    for par in range(2):
                        b = b0 + 2 * i + par
                        for t in range(NT):
                            bank = t % BANKS
                            if below(b, 1):
                                if t == 0:
                                    xt.transpose(pe, 0)
                                    xt.transpose(pe, 1)
                                else:
                                    xt.transpose(pe, t + 1)
                                pe.wait_ge(xt.low_done, 2 * t + 2)
                            if t < BANKS and b0 == 0 and par == 0 and below(i, 1):
                                pass
                            elif t < BANKS and par == 0 and below(i, 1):
                                pe.wait_ge(psum_used[n - 1], NT * segments[n - 1][1] - BANKS + t + 1)
                            else:
                                pe.wait_ge(psum_used[n], (b - b0) * NT + t - BANKS + 1)
                            for k in range(KC):
                                if t == 0 and k % HK == 0:
                                    pe.wait_ge(w_split, QUARTERS * b + k // HK + 1)
                                xs = slice(t * P, (t + 1) * P)
                                pe.matmul(psum[bank][:, :], xth[:, k, xs], wh[:, par, k], start=(k == 0), stop=False)
                                pe.matmul(psum[bank][:, :], xth[:, k, xs], wl[:, par, k], start=False, stop=False)
                                ins = pe.matmul(psum[bank][:, :], xtl[:, k, xs], wh[:, par, k], start=False, stop=(k == KC - 1))
                            ins.then_inc(psum_ready, 1)

                each_segment(pe, products)
                if gates:
                    pe.wait_ge(g_split, 4)
                    for j in range(3):
                        xs = slice(j * THIRD, (j + 1) * THIRD)
                        for k in range(KC):
                            pe.matmul(g_psum[j][:, :], gh[:, k], xth[:, k, xs], start=(k == 0), stop=False)
                            pe.matmul(g_psum[j][:, :], gl[:, k], xth[:, k, xs], start=False, stop=False)
                            ins = pe.matmul(g_psum[j][:, :], gh[:, k], xtl[:, k, xs], start=False, stop=(k == KC - 1))
                        ins.then_inc(g_ready, 1)

            @block.scalar
            def _(act):
                xt.start_act(act)
                xt.high(act, 0)
                xt.high(act, 1)

                def evacuate(n, i, b0):
                    _, _, mode, target = segments[n]
                    for par in range(2):
                        bl = 2 * i + par
                        for t in range(NT):
                            bank = t % BANKS
                            u = (b0 + bl) * NT + t
                            act.wait_ge(psum_ready, u + 1)
                            if isinstance(mode, tuple):
                                if t or not below(bl, 1):
                                    act.wait_ge(mean_done, bl * NT + t)
                                act.activation(squares[:, :], psum[bank][:, :], ACT.Square).then_inc(square_done, 1)
                                act.wait_ge(mean_done, bl * NT + t + 1)
                                act.activation(rms[:, :], ss[:, :], ACT.Sqrt).then_inc(root_done, 1)
                                act.wait_ge(psum_used[n], bl * NT + t + 1)
                            else:
                                if not below(u, BANKS):
                                    act.wait_ge(stored[bank], store_count(b0 + bl, t))
                                act.activation(stage[:, bank, :], psum[bank][:, :],
                                               ACT.Sigmoid if mode == "sigmoid" else ACT.Copy).then_inc(psum_used[n], 1)
                                act.wait_ge(psum_used[n], bl * NT + t + 1)
                            act.dma_start(target(bl, t), stage[:, bank, :]).then_inc(stored[bank], 16)
                            if below(u, NT):
                                xt.high(act, t + 2)

                def store_count(b, t):
                    return (b * (NT // BANKS) + t // BANKS) * 16

                each_segment(act, evacuate, when=lambda m: m != "residual")
                if segments[0][2] == "residual":
                    for t in range(2, NT):
                        xt.high(act, t)
                else:
                    for k in range(BANKS):
                        act.wait_ge(stored[k], nb * (NT // BANKS) * 16)
                if gates:
                    for j in range(3):
                        act.wait_ge(g_ready, j + 1)
                        act.activation(g_out[:, j * THIRD:(j + 1) * THIRD], g_psum[j][0:g_n, :], ACT.Copy).then_inc(g_copied, 1)

            @block.vector
            def _(dve):
                c, xc = Chain(dve, chain_sem), Chain(dve, xt.chain_sem)
                xt.start_dve(dve, xc)
                xt.low(dve, xc, 0)
                xt.low(dve, xc, 1)
                if normed:
                    dve.wait_ge(gain_loaded, 16)
                    c.link(dve.tensor_scalar(gain[:, :], gain_small[:, :], normed[0][2], None, ALU.mult))

                def evacuate(n, i, b0):
                    col0, _, mode, _ = segments[n]
                    for par in range(2):
                        bl = 2 * i + par
                        for t in range(NT):
                            bank = t % BANKS
                            dve.wait_ge(psum_ready, (b0 + bl) * NT + t + 1)
                            if mode == "residual":
                                xs = g.x[:, t, bass.ds(bl * CB, CB)]
                                dve.tensor_tensor(xs, psum[bank][:, :], xs, ALU.add).then_inc(psum_used[n], 1)
                                if below(b0 + bl, 1):
                                    xt.low(dve, xc, t + 2)
                                continue
                            dve.wait_ge(square_done, bl * NT + t + 1)
                            c.link(dve.tensor_reduce(ss[:, :], squares[:, :].rearrange("p (h d) -> p h d", d=B_HD), axis=AX.X, op=ALU.add))
                            dve.tensor_scalar(ss[:, :], ss[:, :], 1.0 / B_HD, EPS, ALU.mult, ALU.add).then_inc(mean_done, 1)
                            dve.wait_ge(root_done, bl * NT + t + 1)
                            c.link(dve.reciprocal(rms[:, :], rms[:, :]))
                            if not (b0 == 0 and t < BANKS and below(bl, 1)):
                                dve.wait_ge(stored[bank], ((b0 + bl) * (NT // BANKS) + t // BANKS) * 16)
                            sv = stage[:, bank, :].rearrange("p (h d) -> p h d", d=B_HD)
                            c.link(dve.tensor_tensor(sv, psum[bank][:, :].rearrange("p (h d) -> p h d", d=B_HD), spread(rms[:, :], B_HD), ALU.mult))
                            dve.tensor_tensor(sv, sv, repeat(gain[:, :], A_H), ALU.mult).then_inc(psum_used[n], 1)
                            if below(b0 + bl, 1):
                                xt.low(dve, xc, t + 2)

                each_segment(dve, evacuate, c, when=lambda m: m == "residual" or isinstance(m, tuple))
                if segments[0][2] == "store":
                    for t in range(2, NT):
                        xt.low(dve, xc, t)


def ffn(nc, g, xth, xtl, tag, w_gu, w_down, gain_row):
    FW = FG * P
    guv = w_gu.rearrange("(k p) n -> p k n", p=P)
    dv = w_down.rearrange("(f p) n -> p f n", p=P)
    G = FFN_GROUPS
    with Scope(nc, tag) as s:
        raw_a, raw_b = s.sb("raw_a", [P, KC * FW]), s.sb("raw_b", [P, KC, FW])
        raw_gate = raw_a[:, :].rearrange("p (k n) -> p k n", k=KC)
        raw_down = raw_a[:, :].rearrange("p (f n) -> p f n", f=FG)
        gh, gl = s.sb("gate_h", [P, FG, KC, P], fp32r), s.sb("gate_l", [P, FG, KC, P], fp32r)
        uh, ul = s.sb("up_h", [P, FG, KC, P], fp32r), s.sb("up_l", [P, FG, KC, P], fp32r)
        dh, dl = s.sb("down_h", [P, FG, D], fp32r), s.sb("down_l", [P, FG, D], fp32r)
        hid = s.sb("hid", [P, T_ALL])
        tok = s.brief("tok", [P, Activations.SLOTS, D])
        hh, hl = s.sb("hid_h", [P, FG, T_ALL], fp32r), s.sb("hid_l", [P, FG, T_ALL], fp32r)
        names = ("gate_loaded", "up_loaded", "down_loaded", "gate_split", "up_split", "down_split", "split_high",
                 "gate_ready", "up_ready", "silu_done", "prod_done", "hid_high", "hid_low", "down_ready", "added")
        (gate_loaded, up_loaded, down_loaded, gate_split, up_split, down_split, split_high,
         gate_ready, up_ready, silu_done, prod_done, hid_high, hid_low, down_ready, added) = (s.sem(n) for n in names)
        gp = [s.ps(f"gate{j}", [P, THIRD]) for j in range(3)]
        up = [s.ps(f"up{j}", [P, THIRD]) for j in range(3)]
        yp = [s.ps(f"y{j}", [P, CB]) for j in range(2)]
        thirds = [slice(j * THIRD, (j + 1) * THIRD) for j in range(3)]
        NY = NT * (D // CB)
        xt = Activations(nc, g, s, xth, xtl, "norm", tok, yp, gain_row=gain_row)

        with nc.Block() as block:

            @block.sync
            def _(sp):
                xt.load_gain(sp)

                def load(n):
                    first = below(n, 1)
                    if not first:
                        wait(sp, down_split, n)
                    sp.dma_start(raw_gate, guv[:, :, bass.ds(n * FW, FW)]).then_inc(gate_loaded, 16)
                    if not first:
                        wait(sp, up_split, n * FG)
                    sp.dma_start(raw_b[:, :, :], guv[:, :, bass.ds(D_FF + n * FW, FW)]).then_inc(up_loaded, 16)
                    wait(sp, gate_split, n * FG + FG)
                    sp.dma_start(raw_down, dv[:, bass.ds(n * FG, FG), :]).then_inc(down_loaded, 16)

                run(sp, G, load)
                wait(sp, down_loaded, 16 * G)

            @block.gpsimd
            def _(pool):
                def split(n):
                    first = below(n, 1)
                    for f in range(FG):
                        fs = slice(f * P, (f + 1) * P)
                        for part, (raw, h, l, loaded, ready, done) in enumerate((
                                (raw_gate, gh, gl, gate_loaded, gate_ready, gate_split),
                                (raw_b, uh, ul, up_loaded, up_ready, up_split))):
                            wait(pool, loaded, n * 16 + 16)
                            if not first:
                                wait(pool, ready, ((n - 1) * FG + f) * 3 + 3)
                            round_high(pool, g, h[:, f], raw[:, :, fs]).then_inc(split_high, 1)
                            wait(pool, split_high, n * (2 * FG + 1) + 2 * f + part + 1)
                            pool.tensor_tensor(l[:, f], raw[:, :, fs], f32(h[:, f]), ALU.subtract).then_inc(done, 1)
                    wait(pool, down_loaded, n * 16 + 16)
                    if not first:
                        wait(pool, down_ready, n * NY)
                    round_high(pool, g, dh[:, :, :], raw_down).then_inc(split_high, 1)
                    wait(pool, split_high, n * (2 * FG + 1) + 2 * FG + 1)
                    pool.tensor_tensor(dl[:, :, :], raw_down, f32(dh[:, :, :]), ALU.subtract).then_inc(down_split, 1)

                run(pool, G, split)

            @block.tensor
            def _(pe):
                def hidden(n, f, banks, h, l, split, freed, ready):
                    pe.wait_ge(split, n * FG + f + 1)
                    making = h is gh and f == 0 and below(n, 1)
                    for j in range(3):
                        if making:
                            for t in ((0, 1, 2), (5,), (8,))[j]:
                                xt.transpose(pe, t)
                            pe.wait_ge(xt.low_done, 2 * (3 * j + 3))
                        if f or not below(n, 1):
                            pe.wait_ge(freed, (n * FG + f - 1) * 3 + j + 1)
                        for k in range(KC):
                            if making and k in (2, 5):
                                xt.transpose(pe, 3 * j + 3 + k // 3)
                            pe.matmul(banks[j][:, :], h[:, f, k], xth[:, k, thirds[j]], start=(k == 0), stop=False)
                            pe.matmul(banks[j][:, :], l[:, f, k], xth[:, k, thirds[j]], start=False, stop=False)
                            ins = pe.matmul(banks[j][:, :], h[:, f, k], xtl[:, k, thirds[j]], start=False, stop=(k == KC - 1))
                        ins.then_inc(ready, 1)

                def gate(n, f):
                    hidden(n, f, gp, gh, gl, gate_split, silu_done, gate_ready)

                def upward(n, f):
                    hidden(n, f, up, uh, ul, up_split, prod_done, up_ready)

                def down(n):
                    pe.wait_ge(down_split, n + 1)
                    pe.wait_ge(hid_low, (n + 1) * FG * 3)
                    for t in range(NT):
                        ts = slice(t * P, (t + 1) * P)
                        for c in range(2):
                            cs = slice(c * CB, (c + 1) * CB)
                            if t or not below(n, 1):
                                pe.wait_ge(added, n * NY + 2 * t + c - 1)
                            for f in range(FG):
                                pe.matmul(yp[c][:, :], hh[:, f, ts], dh[:, f, cs], start=(f == 0), stop=False)
                                pe.matmul(yp[c][:, :], hh[:, f, ts], dl[:, f, cs], start=False, stop=False)
                                ins = pe.matmul(yp[c][:, :], hl[:, f, ts], dh[:, f, cs], start=False, stop=(f == FG - 1))
                            ins.then_inc(down_ready, 1)

                def group(n):
                    upward(n, 0)
                    for f in range(1, FG):
                        gate(n, f)
                        upward(n, f)
                    gate(n + 1, 0)
                    down(n)

                gate(0, 0)
                pe.wait_ge(xt.low_done, 2 * NT)
                run(pe, G - 1, group)
                upward(G - 1, 0)
                for f in range(1, FG):
                    gate(G - 1, f)
                    upward(G - 1, f)
                down(G - 1)

            @block.scalar
            def _(act):
                def silu(n, f):
                    for j in range(3):
                        act.wait_ge(gate_ready, (n * FG + f) * 3 + j + 1)
                        if f or not below(n, 1):
                            act.wait_ge(hid_low, (n * FG + f - 1) * 3 + j + 1)
                        act.activation(hid[:, thirds[j]], gp[j][:, :], ACT.Silu).then_inc(silu_done, 1)

                def high(n, f):
                    for j in range(3):
                        act.wait_ge(prod_done, (n * FG + f) * 3 + j + 1)
                        if not below(n, 1):
                            act.wait_ge(down_ready, n * NY)
                        act.activation(hh[:, f, thirds[j]], hid[:, thirds[j]], ACT.Copy).then_inc(hid_high, 1)

                def group(n):
                    high(n, 0)
                    for f in range(1, FG):
                        silu(n, f)
                        high(n, f)
                    silu(n + 1, 0)

                xt.start_act(act)
                for t in range(NT):
                    xt.high(act, t)
                silu(0, 0)
                run(act, G - 1, group)
                high(G - 1, 0)
                for f in range(1, FG):
                    silu(G - 1, f)
                    high(G - 1, f)

            @block.vector
            def _(dve):
                xc = Chain(dve, xt.chain_sem)
                xt.start_dve(dve, xc)
                for t in range(NT):
                    xt.low(dve, xc, t)

                def group(n):
                    for f in range(FG):
                        for j in range(3):
                            dve.wait_ge(up_ready, (n * FG + f) * 3 + j + 1)
                            dve.wait_ge(silu_done, (n * FG + f) * 3 + j + 1)
                            dve.tensor_tensor(hid[:, thirds[j]], up[j][:, :], hid[:, thirds[j]], ALU.mult).then_inc(prod_done, 1)
                        for j in range(3):
                            dve.wait_ge(hid_high, (n * FG + f) * 3 + j + 1)
                            dve.tensor_tensor(hl[:, f, thirds[j]], hid[:, thirds[j]], f32(hh[:, f, thirds[j]]), ALU.subtract).then_inc(hid_low, 1)
                    for t in range(NT):
                        for c in range(2):
                            dve.wait_ge(down_ready, n * NY + 2 * t + c + 1)
                            xs = g.x[:, t, c * CB:(c + 1) * CB]
                            dve.tensor_tensor(xs, yp[c][:, :], xs, ALU.add).then_inc(added, 1)

                run(dve, G, group)


def log_sigmoid_act(act, u, w, ready_exp, exp_done, ready_ln, ln_done):
    act.wait_ge(*ready_exp)
    act.activation(u, u, ACT.Exp, scale=-1.0).then_inc(exp_done, 1)
    act.wait_ge(*ready_ln)
    act.activation(w[1], w[0], ACT.Ln).then_inc(ln_done, 1)


def log_sigmoid_dve(dve, c, z, u, w, lw, abs_done, exp_done, sum_done, ln_done):
    dve.scalar_tensor_tensor(u, z, -1.0, z, ALU.mult, ALU.max).then_inc(abs_done, 1)
    dve.wait_ge(exp_done, 1)
    dve.tensor_scalar(w, u, 1.0, None, ALU.add).then_inc(sum_done, 1)
    dve.wait_ge(sum_done, 1)
    c.link(dve.scalar_tensor_tensor(u, w, 1.0, u, ALU.subtract, ALU.subtract))
    dve.wait_ge(ln_done, 1)
    c.link(dve.reciprocal(w, w))
    c.link(dve.tensor_tensor(u, u, w, ALU.mult))
    c.link(dve.tensor_tensor(lw, lw, u, ALU.subtract))
    c.link(dve.scalar_tensor_tensor(z, z, 0.0, lw, ALU.min, ALU.subtract))


KIND_A, KIND_G, KIND_W, KIND_E = range(4)


def mlstm_gates(nc, g, gates_d, b_i, b_f, state_m, m_prompt, m_sample):
    NG = NP + DEC_BATCH
    with Scope(nc, "mgates") as s:
        li, lf, u, w, lw = (s.sb(n, [A_H, T_ALL]) for n in ("li", "lf", "u", "w", "lw"))
        b, m, reset = s.sb("b", [A_H, T_ALL]), s.sb("m", [A_H, T_ALL]), s.sb("reset", [A_H, T_ALL])
        gg, ws, en, A = s.sb("gg", [A_H, T_ALL]), s.sb("ws", [A_H, T_ALL]), s.sb("en", [A_H, T_ALL]), s.sb("A", [A_H, T_ALL])
        bi, bf, bi15, bf15 = (s.sb(n, [A_H, 1]) for n in ("bi", "bf", "bi15", "bf15"))
        m0, mprev, bend, gend = s.sb("m0", [A_H, DEC_BATCH]), s.sb("mprev", [A_H, NG]), s.sb("bend", [A_H, NG]), s.sb("gend", [A_H, NG])
        diag, gcs = s.sb("diag", [A_H, A_H, DEC_BATCH]), s.sb("gcs", [DEC_BATCH, A_H])
        loaded = s.sem("loaded")
        chain_sem, scaled, tanh_done, abs_done, exp_done, sum_done, ln_done = (s.sem(n) for n in (
            "chain", "scaled", "tanh", "abs", "exp", "sum", "ln"))
        arg_done, exps_done, A_done, filled, made, turned, out_sem, gend_done = (s.sem(n) for n in (
            "arg", "exps", "A", "filled", "made", "turned", "out", "gend"))
        copied = s.sem("copied")
        tp = s.ps("tok", [P, NT, 4, A_H])
        sp_ = s.ps("small", [P, CB])

        def groups(ap):
            return (ap[:, 0:SEQ].rearrange("h (c t) -> h c t", t=P),
                    ap[:, SEQ:T_ALL].rearrange("h (c t) -> h c t", t=DEC_SEQ))

        with nc.Block() as block:

            @block.sync
            def _(sp):
                sp.dma_start(li[:, :], gates_d[0:A_H, :]).then_inc(loaded, 16)
                sp.dma_start(lf[:, :], gates_d[A_H:2 * A_H, :]).then_inc(loaded, 16)
                sp.dma_start(bi[:, :], b_i.rearrange("o h -> h o")).then_inc(loaded, 16)
                sp.dma_start(bf[:, :], b_f.rearrange("o h -> h o")).then_inc(loaded, 16)
                sp.dma_start(m0[:, :], state_m.rearrange("s o h -> h (s o)"), allow_slow_non_contiguous=True).then_inc(loaded, 16)
                wait(sp, gend_done, 1)
                sp.dma_start(m_prompt.rearrange("a o h -> h (a o)"), m[:, SEQ - 1:SEQ]).then_inc(out_sem, 16)
                sp.dma_start(m_sample.rearrange("s o h -> h (s o)"), groups(m)[1][:, :, DEC_SEQ - 1], allow_slow_non_contiguous=True).then_inc(out_sem, 16)
                wait(sp, out_sem, 32)

            @block.gpsimd
            def _(pool):
                pool.memset(g.sel[:, :, :], 0.0).then_inc(filled, 1)
                pool.memset(g.pair_sel[:, :, :, :], 0.0).then_inc(filled, 1)
                pool.memset(g.own[:, :], 1.0).then_inc(filled, 1)
                pool.memset(g.ones8[:, :], 1.0).then_inc(filled, 1)
                pool.memset(reset[:, :], 1.0).then_inc(filled, 1)
                wait(pool, filled, 5)
                pool.affine_select(out=g.sel[:, :, :], in_=g.sel[:, :, :], compare_op=ALU.not_equal, fill=1.0,
                                   base=0, pattern=[[-1, A_H], [0, P]], channel_multiplier=1).then_inc(made, 1)
                pool.affine_select(out=g.pair_sel[:, :, :, :], in_=g.pair_sel[:, :, :, :], compare_op=ALU.not_equal, fill=1.0,
                                   base=0, pattern=[[-2, A_PAIRS], [-1, 2], [0, A_QK]], channel_multiplier=1).then_inc(made, 1)
                pool.affine_select(out=g.own[:, :], in_=g.own[:, :], compare_op=ALU.is_ge, fill=0.0,
                                   base=0, pattern=[[-DEC_SEQ, DEC_BATCH]], channel_multiplier=1).then_inc(made, 1)
                wait(pool, made, 3)
                pool.affine_select(out=g.own[:, :], in_=g.own[:, :], compare_op=ALU.is_ge, fill=0.0,
                                   base=DEC_SEQ - 1, pattern=[[DEC_SEQ, DEC_BATCH]], channel_multiplier=-1).then_inc(made, 1)
                mk = g.mask_dec[:, :, :].rearrange("p e (c t) -> p e c t", t=DEC_SEQ)
                pool.affine_select(out=mk, in_=g.mask_kq[:, :, :].rearrange("p e (c t) -> p e c t", t=DEC_SEQ), compare_op=ALU.is_ge, fill=NEG,
                                   base=0, pattern=[[0, 2], [-DEC_SEQ, DEC_BATCH], [0, DEC_SEQ]], channel_multiplier=1).then_inc(made, 1)
                for view in groups(reset):
                    pool.memset(view[:, :, 0:1], 0.0).then_inc(made, 1)
                wait(pool, made, 7)

            @block.scalar
            def _(act):
                act.wait_ge(scaled, 2)
                act.activation(li[:, :], li[:, :], ACT.Tanh, bias=bi15[:, :], scale=1.0 / CAP).then_inc(tanh_done, 1)
                act.activation(lf[:, :], lf[:, :], ACT.Tanh, bias=bf15[:, :], scale=1.0 / CAP).then_inc(tanh_done, 1)
                log_sigmoid_act(act, u[:, :], (w[:, :], lw[:, :]), (abs_done, 1), exp_done, (sum_done, 1), ln_done)
                act.wait_ge(arg_done, 3)
                act.activation(gg[:, :], gg[:, :], ACT.Exp).then_inc(exps_done, 1)
                act.activation(ws[:, :], ws[:, :], ACT.Exp).then_inc(exps_done, 1)
                act.activation(en[:, :], m[:, :], ACT.Exp, scale=-1.0).then_inc(exps_done, 1)

            @block.vector
            def _(dve):
                c = Chain(dve, chain_sem)
                dve.wait_ge(loaded, 80)
                dve.tensor_scalar(bi15[:, :], bi[:, :], 1.0 / CAP, None, ALU.mult).then_inc(scaled, 1)
                dve.tensor_scalar(bf15[:, :], bf[:, :], 1.0 / CAP, None, ALU.mult).then_inc(scaled, 1)
                dve.wait_ge(tanh_done, 2)
                c.link(dve.tensor_scalar(li[:, :], li[:, :], CAP, None, ALU.mult))
                c.link(dve.tensor_scalar(lf[:, :], lf[:, :], CAP, None, ALU.mult))
                log_sigmoid_dve(dve, c, lf[:, :], u[:, :], w[:, :], lw[:, :], abs_done, exp_done, sum_done, ln_done)
                dve.wait_ge(made, 7)
                c.link(dve.tensor_tensor_scan(b[:, :], reset[:, :], lf[:, :], 0.0, ALU.mult, ALU.add))
                c.link(dve.tensor_tensor_scan(m[:, 0:SEQ], lf[:, 0:SEQ], li[:, 0:SEQ], 0.0, ALU.add, ALU.max))
                for k in range(DEC_BATCH):
                    ks = slice(SEQ + k * DEC_SEQ, SEQ + (k + 1) * DEC_SEQ)
                    c.link(dve.tensor_tensor_scan(m[:, ks], lf[:, ks], li[:, ks], m0[:, k:k + 1], ALU.add, ALU.max))
                c.link(dve.memset(mprev[:, 0:1], 0.0))
                c.link(dve.tensor_copy(mprev[:, 1:NP], groups(m)[0][:, 0:NP - 1, P - 1]))
                c.link(dve.tensor_copy(mprev[:, NP:NG], m0[:, :]))
                c.link(dve.tensor_tensor(g.B[:, :], b[:, :], m[:, :], ALU.subtract))
                dve.tensor_tensor(A[:, :], li[:, :], b[:, :], ALU.subtract).then_inc(A_done, 1)
                dve.wait_ge(A_done, 1)
                for part, (lo, hi, n, last) in enumerate(((0, NP, P, P - 1), (NP, NG, DEC_SEQ, DEC_SEQ - 1))):
                    c.link(dve.tensor_copy(bend[:, lo:hi], groups(g.B)[part][:, :, last]))
                for part, (lo, hi, n, last) in enumerate(((0, NP, P, P - 1), (NP, NG, DEC_SEQ, DEC_SEQ - 1))):
                    c.link(dve.tensor_tensor(groups(gg)[part], groups(g.B)[part], spread(mprev[:, lo:hi], n), ALU.add))
                    dve.tensor_tensor(groups(ws)[part], groups(A)[part], spread(bend[:, lo:hi], n), ALU.add).then_inc(arg_done, 1)
                dve.wait_ge(arg_done, 2)
                dve.sem_inc(arg_done, 1)
                dve.wait_ge(exps_done, 3)
                c.link(dve.tensor_copy(gend[:, 0:NP], groups(gg)[0][:, :, P - 1]))
                c.link(dve.tensor_copy(gend[:, NP:NG], groups(gg)[1][:, :, DEC_SEQ - 1]))
                c.link(dve.tensor_tensor(diag[:, :, :], spread(g.ident[0:A_H, 0:A_H], DEC_BATCH), repeat(gend[:, NP:NG], A_H), ALU.mult))
                dve.sem_inc(gend_done, 1)
                dve.wait_ge(turned, 2)
                dve.tensor_copy(g.tok[:, :, :, :], tp[:, :, :, :]).then_inc(copied, 1)
                dve.tensor_copy(g.gc_pair[:, :, :], sp_[:, 0:A_PAIRS * NP].rearrange("p (j c) -> p j c", j=A_PAIRS)).then_inc(copied, 1)
                dve.tensor_copy(g.gc_dec[:, :, :], sp_[:, 64:128].rearrange("p (h c) -> p h c", h=A_H)).then_inc(copied, 1)
                dve.tensor_copy(g.gc_s[:, :], sp_[0:DEC_BATCH, 128:128 + A_H]).then_inc(copied, 1)

            @block.tensor
            def _(pe):
                pe.wait_ge(A_done, 1)
                pe.wait_ge(exps_done, 3)
                for t in range(NT):
                    for kind, row in ((KIND_A, A), (KIND_G, gg), (KIND_W, ws), (KIND_E, en)):
                        ins = pe.transpose(tp[:, t, kind, :], row[:, t * P:(t + 1) * P], g.ident[0:A_H, 0:A_H])
                ins.then_inc(turned, 1)
                pe.wait_ge(gend_done, 1)
                pe.wait_ge(made, 7)
                for j in range(A_PAIRS):
                    pe.matmul(sp_[:, j * NP:(j + 1) * NP], g.pair_sel[:, j].rearrange("k e d -> k (e d)"), gend[:, 0:NP], start=True, stop=True)
                pe.matmul(sp_[:, 64:128], g.ones8[:, :], diag[:, :, :].rearrange("k h c -> k (h c)"), start=True, stop=True)
                pe.transpose(sp_[0:DEC_BATCH, 128:128 + A_H], gend[:, NP:NG], g.ident[0:A_H, 0:A_H]).then_inc(turned, 1)


def mlstm(nc, g, qkvo, h_d, running, c_out, n_out, state_c=None, state_n=None):
    tag = "mrun" if running else "mprompt"
    N_C = 1 if running else NP
    V1 = A_V + 1
    NPAIR = DEC_BATCH // 2
    with Scope(nc, tag) as s:
        qk, v1 = s.sb("qk", [P, 2 * A_H * A_QK]), s.sb("v1", [P, A_H, V1])
        k8, wsv = s.sb("k8", [P, A_H * A_QK]), s.sb("wsv", [P, A_H, V1])
        qt, kt = s.sb("qt", [P, A_PAIRS, P]), s.sb("kt", [P, A_PAIRS, P])
        tokc, gcc = s.sb("tokc", [P, 4, A_H]), s.sb("gcc", [P, A_PAIRS])
        arg, st = s.sb("arg", [P, 2, 2, P]), s.sb("st", [P, 2, 2, P])
        ig, num = s.sb("ig", [P, 2, 2, V1]), s.sb("num", [P, A_H, V1])
        den, hout = s.sb("den", [P, A_H]), s.sb("hout", [P, A_H, A_V])
        names = ("qk_loaded", "v_loaded", "ones", "tok_done", "k8_done", "wsv_done", "turned", "t_copied", "bias_ready",
                 "arg_done", "exp_done", "score_ready", "st_done", "num_ready", "inter_ready", "ig_done", "num_done",
                 "state_ready", "state_done", "h_done", "stored", "chain")
        (qk_loaded, v_loaded, ones, tok_done, k8_done, wsv_done, turned, t_copied, bias_ready,
         arg_done, exp_done, score_ready, st_done, num_ready, inter_ready, ig_done, num_done,
         state_ready, state_done, h_done, stored, chain_sem) = (s.sem(n) for n in names)
        psc, pi = s.ps("scores", [P, 2, CB]), s.ps("inter", [P, 2, CB])
        pb, pn, pc, pt = s.ps("bias", [P, 2, P]), s.ps("num_p", [P, 2, V1]), s.ps("state", [P, CB]), s.ps("turn", [P, 4, P])
        final_t, final_c, final_s, final_n = (s.sem(n) for n in ("final_t", "final_c", "final_s", "final_n"))
        if running:
            cold, c0t = s.sb("cold", [P, A_H, DEC_BATCH, A_QK]), s.sb("c0t", [P, NPAIR, A_H, V1])
            nload, nold = s.sb("nload", [NPAIR * A_H, P]), s.sb("nold", [DEC_BATCH, A_H * A_QK])
            qm, km = s.sb("qm", [P, 2, DEC_BATCH, A_QK]), s.sb("km", [P, 2, DEC_BATCH, A_QK])
            qmt, wsk, ccur = s.sb("qmt", [P, 2, NPAIR, P]), s.sb("wsk", [P, A_H, A_QK]), s.sb("ccur", [P, 2, DEC_BATCH, A_QK])
            c_loaded, n_loaded, c0_turned, c0_copied, qm_done, qm_turned, qm_copied = (s.sem(n) for n in (
                "c_loaded", "n_loaded", "c0_turned", "c0_copied", "qm_done", "qm_turned", "qm_copied"))
            decayed, km_done, wsk_done, c_ready, c_done, n_ready, n_done = (s.sem(n) for n in (
                "decayed", "km_done", "wsk_done", "c_ready", "c_done", "n_ready", "n_done"))
            mask = g.mask_dec
        else:
            ct = s.sb("ct", [P, A_PAIRS, V1])
            cfin, nfin = s.sb("cfin", [P, A_PAIRS, P]), s.sb("nfin", [A_PAIRS, P])
            mask = g.mask_kq

        def tile(i):
            return NT - 1 if running else i

        with nc.Block() as block:

            @block.sync
            def _(sp):
                if running:
                    for j in range(NPAIR):
                        sp.dma_start(nload[j * A_H:(j + 1) * A_H, :].rearrange("h (s d) -> h s d", s=2),
                                     state_n[2 * j:2 * j + 2, 0].rearrange("s h d -> h s d")).then_inc(n_loaded, 16)
                    sp.dma_start(nold[:, :], state_n.rearrange("s o h d -> s (o h d)")).then_inc(n_loaded, 16)
                    for h in range(A_H):
                        sp.dma_start(cold[:, h], state_c[:, 0, h].rearrange("s v d -> v s d")).then_inc(c_loaded, 16)

                def load(i):
                    t = tile(i)
                    if not below(i, 1):
                        wait(sp, t_copied, 2 * i)
                        wait(sp, k8_done, i)
                    sp.dma_start(qk[:, :], qkvo[t, :, 0:A_V0]).then_inc(qk_loaded, 16)
                    if not below(i, 1):
                        wait(sp, wsv_done, i)
                        wait(sp, num_ready, i * A_PAIRS)
                    sp.dma_start(v1[:, :, 0:A_V], qkvo[t, :, A_V0:A_O0].rearrange("t (h v) -> t h v", v=A_V)).then_inc(v_loaded, 16)

                run(sp, N_C, load)
                if not running:
                    wait(sp, final_c, 5)
                    for j in range(A_PAIRS):
                        sp.dma_start(c_out[0, 0, 2 * j:2 * j + 2].rearrange("h v d -> v h d"),
                                     cfin[:, j, :].rearrange("v (h d) -> v h d", h=2)).then_inc(final_s, 16)
                    sp.dma_start(n_out.rearrange("a b (j h) d -> (a b j) (h d)", j=A_PAIRS), nfin[:, :]).then_inc(final_s, 16)
                    wait(sp, final_s, 16 * (A_PAIRS + 1))
                else:
                    for h in range(A_H):
                        wait(sp, c_done, h + 1)
                        sp.dma_start(c_out[:, 0, h].rearrange("s v d -> v s d"), cold[:, h]).then_inc(final_s, 16)
                    wait(sp, n_done, 1)
                    sp.dma_start(n_out.rearrange("s o h d -> s (o h d)"), nold[:, :]).then_inc(final_s, 16)
                    wait(sp, final_s, 16 * (A_H + 1))

            @block.gpsimd
            def _(pool):
                pool.memset(v1[:, :, A_V:V1], 1.0).then_inc(ones, 1)
                if not running:
                    pool.memset(ct[:, :, :], 0.0).then_inc(ones, 1)
                else:
                    pool.sem_inc(ones, 1)

                def weigh(i):
                    wait(pool, qk_loaded, i * 16 + 16)
                    if not below(i, 1):
                        wait(pool, state_ready, i * A_PAIRS)
                    wait(pool, v_loaded, i * 16 + 16)
                    wait(pool, tok_done, i + 1)
                    wait(pool, ones, 2)
                    pool.tensor_tensor(wsv[:, :, :], v1[:, :, :], spread(tokc[:, KIND_W, :], V1), ALU.mult).then_inc(wsv_done, 1)
                    pool.tensor_scalar(k8[:, :], qk[:, A_K0:A_V0], A_QK ** -0.5, None, ALU.mult).then_inc(k8_done, 1)

                run(pool, N_C, weigh)
                if running:
                    wait(pool, k8_done, 1)
                    k8v = k8[:, :].rearrange("p (h d) -> p h d", d=A_QK)
                    pool.tensor_tensor(wsk[:, :, :], k8v, spread(tokc[:, KIND_W, :], A_QK), ALU.mult).then_inc(wsk_done, 1)
                    for h in range(A_H):
                        if h >= 2:
                            wait(pool, c_ready, h - 1)
                        pool.tensor_tensor(km[:, h % 2], repeat(k8v[:, h, :], DEC_BATCH), spread(g.own[:, :], A_QK), ALU.mult).then_inc(km_done, 1)

            @block.tensor
            def _(pe):
                if running:
                    for h in range(A_H):
                        pe.wait_ge(c_loaded, 16 * A_H)
                        if h:
                            pe.wait_ge(c0_copied, h)
                        for j in range(NPAIR):
                            ins = pe.transpose(pt[:, j, :], cold[:, h, 2 * j:2 * j + 2, :].rearrange("v s d -> v (s d)"), g.ident[:, :])
                        ins.then_inc(c0_turned, 1)
                    pe.wait_ge(c0_copied, A_H)
                    pe.wait_ge(n_loaded, 16 * (NPAIR + 1))
                    pe.transpose(pt[:, 0, 0:NPAIR * A_H], nload[:, :], g.ident[0:NPAIR * A_H, 0:NPAIR * A_H]).then_inc(c0_turned, 1)
                    pe.wait_ge(c0_copied, A_H + 1)

                def head_pair(i, j):
                    return i * A_PAIRS + j

                def bias(i, j):
                    u = head_pair(i, j)
                    if not below(u, 1):
                        pe.wait_ge(arg_done, u)
                    cols = bass.ds(tile(i) * P, P)
                    pe.matmul(pb[:, :, :], g.ident[:, :], mask[:, :, :], start=True, stop=False)
                    for e in range(2):
                        ins = pe.matmul(pb[:, e, :], g.sel[:, 2 * j + e, :], g.B[:, cols], start=False, stop=(e == 1))
                    ins.then_inc(bias_ready, 1)

                def scores(i, j):
                    u = head_pair(i, j)
                    if not below(u, 1):
                        pe.wait_ge(st_done, u)
                    for e in range(2):
                        es = slice(e * A_QK, (e + 1) * A_QK)
                        ins = pe.matmul(psc[:, e, 0:P], kt[es, j, :], qt[es, j, :], start=True, stop=True)
                    ins.then_inc(score_ready, 1)

                def chunk(i):
                    pe.wait_ge(qk_loaded, i * 16 + 16)
                    for part in range(2):
                        if part or not below(i, 1):
                            pe.wait_ge(t_copied, 2 * i + part)
                        for n in range(A_PAIRS):
                            ins = pe.transpose(pt[:, n, :], qk[:, (part * A_PAIRS + n) * P:(part * A_PAIRS + n + 1) * P], g.ident[:, :])
                        ins.then_inc(turned, 1)
                    pe.wait_ge(t_copied, 2 * i + 2)
                    bias(i, 0)
                    scores(i, 0)
                    for j in range(A_PAIRS):
                        u = head_pair(i, j)
                        slot = j % 2
                        if j + 1 < A_PAIRS:
                            bias(i, j + 1)
                            scores(i, j + 1)
                        pe.wait_ge(st_done, u + 1)
                        pe.wait_ge(v_loaded, i * 16 + 16)
                        pe.wait_ge(ones, 2)
                        if not below(u, 1):
                            pe.wait_ge(num_done, u)
                        for e in range(2):
                            ins = pe.matmul(pn[:, e, :], st[:, slot, e, :], v1[:, 2 * j + e, :], start=True, stop=True)
                        ins.then_inc(num_ready, 1)
                        if not below(u, 1):
                            pe.wait_ge(ig_done, 2 * u)
                        if running:
                            for e in range(2):
                                h = 2 * j + e
                                pe.wait_ge(qm_done, h + 1)
                                if h >= 1:
                                    pe.wait_ge(qm_copied, h)
                                for n in range(NPAIR):
                                    ins = pe.transpose(pt[:, n, :], qm[:, e, 2 * n:2 * n + 2, :].rearrange("t s d -> t (s d)"), g.ident[:, :])
                                ins.then_inc(qm_turned, 1)
                                pe.wait_ge(qm_copied, h + 1)
                                for n in range(NPAIR):
                                    ins = pe.matmul(pi[:, e, 0:V1], qmt[:, e, n, :], c0t[:, n, h, :], start=(n == 0), stop=(n == NPAIR - 1))
                            ins.then_inc(inter_ready, 1)
                        else:
                            if not below(i, 1):
                                pe.wait_ge(state_done, u - A_PAIRS + 1)
                            for e in range(2):
                                es = slice(e * A_QK, (e + 1) * A_QK)
                                ins = pe.matmul(pi[:, e, 0:V1], qt[es, j, :], ct[es, j, :], start=True, stop=True)
                            ins.then_inc(inter_ready, 1)
                            pe.wait_ge(k8_done, i + 1)
                            pe.wait_ge(wsv_done, i + 1)
                            if not below(u, 1):
                                pe.wait_ge(state_done, u)
                            for e in range(2):
                                h = 2 * j + e
                                ins = pe.matmul(pc[e * A_QK:(e + 1) * A_QK, 0:V1], k8[:, h * A_QK:(h + 1) * A_QK], wsv[:, h, :], start=True, stop=True)
                            ins.then_inc(state_ready, 1)

                run(pe, N_C, chunk)
                if not running:
                    pe.wait_ge(state_done, N_C * A_PAIRS)
                    for j in range(A_PAIRS):
                        ins = pe.transpose(pt[:, j, :], ct[:, j, 0:A_V], g.ident[:, :])
                    ins.then_inc(final_t, 1)
                    pe.wait_ge(final_c, 4)
                    pe.transpose(pt[0:A_PAIRS, 0, :], ct[:, :, A_V:V1].rearrange("p j o -> p (j o)"), g.ident[:, :]).then_inc(final_t, 1)
                else:
                    pe.wait_ge(wsk_done, 1)
                    pe.matmul(pc[0:DEC_BATCH, :], g.own[:, :], wsk[:, :, :].rearrange("p h d -> p (h d)"), start=True, stop=True).then_inc(n_ready, 1)
                    for h in range(A_H):
                        bank = pt[:, :, :].rearrange("p a b -> p (a b)") if h % 2 == 0 else pc[:, :]
                        if h == 1:
                            pe.wait_ge(n_done, 1)
                        if h >= 2:
                            pe.wait_ge(c_done, h - 1)
                        pe.wait_ge(km_done, h + 1)
                        pe.wait_ge(wsv_done, 1)
                        pe.matmul(bank, wsv[:, h, 0:A_V], km[:, h % 2].rearrange("p s d -> p (s d)"), start=True, stop=True).then_inc(c_ready, 1)

            @block.scalar
            def _(act):
                if running:
                    for h in range(A_H):
                        act.wait_ge(c0_turned, h + 1)
                        act.activation(c0t[:, :, h, 0:A_V], pt[:, :, :], ACT.Copy).then_inc(c0_copied, 1)
                    act.wait_ge(c0_turned, A_H + 1)
                    act.activation(c0t[:, :, :, A_V:V1].rearrange("p n h o -> p (n h o)"), pt[:, 0, 0:NPAIR * A_H], ACT.Copy).then_inc(c0_copied, 1)

                def exponent(i, j):
                    u = i * A_PAIRS + j
                    act.wait_ge(arg_done, u + 1)
                    act.activation(arg[:, j % 2], arg[:, j % 2], ACT.Exp).then_inc(exp_done, 1)

                def chunk(i):
                    for part, (dst, scale) in enumerate(((qt, 1.0), (kt, A_QK ** -0.5))):
                        act.wait_ge(turned, 2 * i + part + 1)
                        act.activation(dst[:, :, :], pt[:, :, :], ACT.Copy, scale=scale).then_inc(t_copied, 1)
                    exponent(i, 0)
                    for j in range(A_PAIRS):
                        u = i * A_PAIRS + j
                        if j + 1 < A_PAIRS:
                            exponent(i, j + 1)
                        if running:
                            for e in range(2):
                                act.wait_ge(qm_turned, 2 * j + e + 1)
                                act.activation(qmt[:, e], pt[:, :, :], ACT.Copy).then_inc(qm_copied, 1)
                        act.wait_ge(inter_ready, u + 1)
                        act.wait_ge(tok_done, i + 1)
                        if not below(u, 2):
                            act.wait_ge(num_done, u - 1)
                        for e in range(2):
                            act.activation(ig[:, j % 2, e, :], pi[:, e, 0:V1], ACT.Copy,
                                           scale=tokc[:, KIND_G, 2 * j + e:2 * j + e + 1]).then_inc(ig_done, 1)
                    act.wait_ge(h_done, i + 1)
                    act.dma_start(h_d[tile(i)], hout[:, :, :].rearrange("t h v -> t (h v)")).then_inc(stored, 16)

                run(act, N_C, chunk)
                act.wait_ge(stored, 16 * N_C)
                if not running:
                    for n in range(1):
                        act.wait_ge(final_t, 1)
                        for j in range(A_PAIRS):
                            act.activation(cfin[:, j, :], pt[:, j, :], ACT.Copy).then_inc(final_c, 1)
                        act.wait_ge(final_t, 2)
                        act.activation(nfin[:, :], pt[0:A_PAIRS, 0, :], ACT.Copy).then_inc(final_c, 1)

            @block.vector
            def _(dve):
                c = Chain(dve, chain_sem)
                if running:
                    for h in range(2):
                        dve.wait_ge(qk_loaded, 16)
                        dve.tensor_tensor(qm[:, h % 2], repeat(qk[:, h * A_QK:(h + 1) * A_QK], DEC_BATCH), spread(g.own[:, :], A_QK), ALU.mult).then_inc(qm_done, 1)

                def argument(i, j):
                    u = i * A_PAIRS + j
                    dve.wait_ge(bias_ready, u + 1)
                    dve.tensor_tensor(arg[:, j % 2], pb[:, :, :], spread(tokc[:, KIND_A, 2 * j:2 * j + 2], P), ALU.add).then_inc(arg_done, 1)

                def chunk(i):
                    dve.tensor_copy(tokc[:, :, :], g.tok[:, tile(i)]).then_inc(tok_done, 1)
                    if not running:
                        c.link(dve.tensor_copy(gcc[:, :], g.gc_pair[:, :, i]))
                    dve.wait_ge(tok_done, i + 1)
                    argument(i, 0)
                    for j in range(A_PAIRS):
                        u = i * A_PAIRS + j
                        if j + 1 < A_PAIRS:
                            argument(i, j + 1)
                        dve.wait_ge(exp_done, u + 1)
                        dve.wait_ge(score_ready, u + 1)
                        dve.tensor_tensor(st[:, j % 2], psc[:, :, 0:P], arg[:, j % 2], ALU.mult).then_inc(st_done, 1)
                        if running and j + 1 < A_PAIRS:
                            for e in range(2):
                                h = 2 * j + 2 + e
                                dve.wait_ge(qm_turned, h - 1)
                                dve.tensor_tensor(qm[:, e], repeat(qk[:, h * A_QK:(h + 1) * A_QK], DEC_BATCH), spread(g.own[:, :], A_QK), ALU.mult).then_inc(qm_done, 1)
                        dve.wait_ge(num_ready, u + 1)
                        dve.wait_ge(ig_done, 2 * u + 2)
                        dve.tensor_tensor(num[:, 2 * j:2 * j + 2, :], pn[:, :, :], ig[:, j % 2], ALU.add).then_inc(num_done, 1)
                        if not running:
                            dve.wait_ge(state_ready, u + 1)
                            dve.wait_ge(ones, 2)
                            dve.scalar_tensor_tensor(ct[:, j, :], ct[:, j, :], gcc[:, j:j + 1], pc[:, 0:V1], ALU.mult, ALU.add).then_inc(state_done, 1)
                    dve.wait_ge(num_done, i * A_PAIRS + A_PAIRS)
                    c.link(dve.scalar_tensor_tensor(den[:, :], num[:, :, A_V], -1.0, num[:, :, A_V], ALU.mult, ALU.max))
                    c.link(dve.tensor_tensor(den[:, :], den[:, :], tokc[:, KIND_E, :], ALU.max))
                    c.link(dve.reciprocal(den[:, :], den[:, :]))
                    if not below(i, 1):
                        dve.wait_ge(stored, 16 * i)
                    dve.tensor_tensor(hout[:, :, :], num[:, :, 0:A_V], spread(den[:, :], A_V), ALU.mult).then_inc(h_done, 1)

                run(dve, N_C, chunk, c)
                if running:
                    dve.wait_ge(n_loaded, 16 * (NPAIR + 1))
                    nv = nold[:, :].rearrange("s (h d) -> s h d", h=A_H)
                    c.link(dve.tensor_tensor(nv, nv, spread(g.gc_s[:, :], A_QK), ALU.mult))
                    dve.wait_ge(n_ready, 1)
                    dve.tensor_tensor(nold[:, :], pc[0:DEC_BATCH, :], nold[:, :], ALU.add).then_inc(n_done, 1)
                    dve.wait_ge(c0_turned, A_H + 1)
                    for h in range(A_H):
                        bank = pt[:, :, :].rearrange("p a b -> p (a b)") if h % 2 == 0 else pc[:, :]
                        c.link(dve.tensor_tensor(cold[:, h], cold[:, h], spread(g.gc_dec[:, h, :], A_QK), ALU.mult))
                        dve.wait_ge(c_ready, h + 1)
                        cv = cold[:, h].rearrange("v s d -> v (s d)")
                        dve.tensor_tensor(cv, bank, cv, ALU.add).then_inc(c_done, 1)


def fox_gates(nc, g, gates_d, b_f, cache_logf, logf_prompt, logf_sample, ncp_d, ncd_d):
    with Scope(nc, "fgates") as s:
        lf, u, w, lw, ones = (s.sb(n, [B_H, T_ALL]) for n in ("lf", "u", "w", "lw", "ones"))
        bias, cached = s.sb("bias", [B_H, 1]), s.sb("cached", [P, DEC_BATCH, PAST_T, B_H])
        lall, ncd, ncp = s.sb("lall", [B_H, DEC_BATCH, DK]), s.sb("ncd", [B_H, DEC_BATCH, DK]), s.sb("ncp", [B_H, SEQ])
        out, wide = s.sb("out", [P, NT, B_H]), s.sb("wide", [P, DEC_BATCH, DEC_SEQ])
        loaded, filled, made, own_made, abs_done, exp_done, sum_done, ln_done, lf_done, out_turned, out_copied, turned, copied, cum_done, stored, chain_sem, wide_made = (
            s.sem(n) for n in ("loaded", "filled", "made", "own_made", "abs", "exp", "sum", "ln", "lf_done", "out_turned", "out_copied",
                               "turned", "copied", "cum_done", "stored", "chain", "wide"))
        banks = [s.ps(f"turn{i}", [P, CB]) for i in range(2)]
        outp = s.ps("outp", [P, NT, B_H])
        with nc.Block() as block:

            @block.sync
            def _(sp):
                sp.dma_start(lf[:, :], gates_d).then_inc(loaded, 16)
                sp.dma_start(bias[:, :], b_f.rearrange("(h o) -> h o", o=1)).then_inc(loaded, 16)
                for k in range(DEC_BATCH):
                    sp.dma_start(cached[:, k], cache_logf[k].rearrange("(t p) h -> p t h", p=P)).then_inc(loaded, 16)
                sp.wait_ge(out_copied, 1)
                sp.dma_start(logf_prompt[0].rearrange("(t p) h -> p t h", p=P), out[:, 0:NP, :]).then_inc(stored, 16)
                sp.dma_start(logf_sample.rearrange("s t h -> (s t) h"), out[:, NP, :]).then_inc(stored, 16)
                sp.wait_ge(cum_done, 1)
                sp.dma_start(ncp_d, ncp[:, :]).then_inc(stored, 16)
                for k in range(DEC_BATCH):
                    sp.wait_ge(cum_done, 2 + k)
                    sp.dma_start(ncd_d[k], ncd[:, k:k + 1, :].to_broadcast((B_H, DEC_SEQ, DK))).then_inc(stored, 16)
                sp.wait_ge(stored, 16 * (3 + DEC_BATCH))

            @block.gpsimd
            def _(pool):
                pool.memset(ones[:, :], 1.0).then_inc(filled, 1)
                pool.memset(g.own[:, :], 1.0).then_inc(filled, 1)
                pool.memset(wide[:, :, :], 0.0).then_inc(filled, 1)
                pool.wait_ge(filled, 3)
                pool.affine_select(out=g.own[:, :], in_=g.own[:, :], compare_op=ALU.is_ge, fill=0.0,
                                   base=0, pattern=[[-DEC_SEQ, DEC_BATCH]], channel_multiplier=1).then_inc(own_made, 1)
                pool.wait_ge(own_made, 1)
                pool.affine_select(out=g.own[:, :], in_=g.own[:, :], compare_op=ALU.is_ge, fill=0.0,
                                   base=DEC_SEQ - 1, pattern=[[DEC_SEQ, DEC_BATCH]], channel_multiplier=-1).then_inc(own_made, 1)
                pool.affine_select(out=wide[:, :, :], in_=wide[:, :, :], compare_op=ALU.is_ge, fill=NEG,
                                   base=0, pattern=[[-DEC_SEQ, DEC_BATCH], [-1, DEC_SEQ]], channel_multiplier=1).then_inc(made, 1)

            @block.scalar
            def _(act):
                log_sigmoid_act(act, u[:, :], (w[:, :], lw[:, :]), (abs_done, 1), exp_done, (sum_done, 1), ln_done)
                for k in range(DEC_BATCH):
                    act.wait_ge(turned, k + 1)
                    act.activation(lall[:, k, 0:PAST], banks[k % 2][0:B_H, :], ACT.Copy).then_inc(copied, 1)

            @block.vector
            def _(dve):
                c = Chain(dve, chain_sem)
                dve.wait_ge(loaded, 16 * (2 + DEC_BATCH))
                c.link(dve.tensor_scalar(lf[:, :], lf[:, :], bias[:, :], None, ALU.add))
                log_sigmoid_dve(dve, c, lf[:, :], u[:, :], w[:, :], lw[:, :], abs_done, exp_done, sum_done, ln_done)
                dve.sem_inc(lf_done, 1)
                dve.wait_ge(filled, 3)
                dve.tensor_tensor_scan(ncp[:, :], ones[:, 0:SEQ], lf[:, 0:SEQ], 0.0, ALU.mult, ALU.subtract).then_inc(cum_done, 1)
                c.link(dve.tensor_copy(lall[:, :, PAST:DK], lf[:, SEQ:T_ALL].rearrange("h (s t) -> h s t", t=DEC_SEQ)))
                for k in range(DEC_BATCH):
                    dve.wait_ge(copied, k + 1)
                    dve.tensor_tensor_scan(ncd[:, k, :], ones[:, 0:DK], lall[:, k, :], 0.0, ALU.mult, ALU.subtract).then_inc(cum_done, 1)
                dve.wait_ge(out_turned, 1)
                dve.tensor_copy(out[:, :, :], outp[:, :, :]).then_inc(out_copied, 1)
                dve.wait_ge(own_made, 2)
                dve.wait_ge(made, 1)
                c.link(dve.tensor_reduce(g.parity[:, :], g.own[:, :].rearrange("p (c e) -> p e c", e=2), axis=AX.X, op=ALU.add))
                c.link(dve.tensor_tensor(wide[:, :, :], wide[:, :, :], spread(g.own[:, :], DEC_SEQ), ALU.mult))
                c.link(dve.tensor_reduce(g.mask_new[:, :], wide[:, :, :].rearrange("p c k -> p k c"), axis=AX.X, op=ALU.add))

            @block.tensor
            def _(pe):
                pe.wait_ge(loaded, 16 * (2 + DEC_BATCH))
                for k in range(DEC_BATCH):
                    if k >= 2:
                        pe.wait_ge(copied, k - 1)
                    for t in range(PAST_T):
                        ins = pe.transpose(banks[k % 2][0:B_H, t * P:(t + 1) * P], cached[:, k, t, :], g.ident[:, :])
                    ins.then_inc(turned, 1)
                pe.wait_ge(lf_done, 1)
                for t in range(NT):
                    ins = pe.transpose(outp[:, t, :], lf[:, t * P:(t + 1) * P], g.ident[0:B_H, 0:B_H])
                ins.then_inc(out_turned, 1)


def fox_prompt(nc, g, q_d, k_prompt, v_prompt, ncp_d, o_d):
    UNITS = 2 * NP
    CPP = P
    SLOTS = 2
    AHEAD, PROBS = 2, 4
    kv = k_prompt.rearrange("(t p) d -> p t d", p=P)
    vv = v_prompt.rearrange("(t p) d -> p t d", p=P)
    qv = q_d[0:NP].rearrange("t p d -> p t d")
    ov = o_d[0:NP].rearrange("t p d -> p t d")

    IN = [(part, e, h) for part in range(2) for e in range(2) for h in range(NP // 4)]
    FIRST_IN = 4

    def layout(with_incoming):
        at, freed_at, incoming, groups = 0, [0, 0], {}, {}
        for u in range(UNITS):
            if with_incoming and FIRST_IN <= u < FIRST_IN + len(IN):
                at, freed_at[0] = at + 1, freed_at[0] + 1
                incoming[u] = (IN[u - FIRST_IN], at, freed_at[0])
            groups[u] = []
            for a in range(0, u // 2 + 1, 4):
                bank = (u + a // 4) % 2
                at, freed_at[bank] = at + 1, freed_at[bank] + 1
                groups[u].append((bank, range(a, min(a + 4, u // 2 + 1)), at, freed_at[bank]))
        return groups, incoming, at, freed_at

    every, incoming, PER_PAIR, FREED = layout(True)
    final = layout(False)[0]
    last_in, last_in_freed = incoming[FIRST_IN + len(IN) - 1][1:]

    def groups(j, u):
        return (final if not exists(j + 1) else every)[u]

    def exists(j):
        return not isinstance(j, int) or 0 <= j < B_PAIRS

    def turned_count(j, n):
        return len(IN) + j * PER_PAIR + n

    def freed_count(j, bank, n):
        return (len(IN) if bank == 0 else 0) + j * FREED[bank] + n

    with Scope(nc, "fprompt") as s:
        kq = s.sb("kq", [P, 2, NP, CPP])
        twice = s.sb("twice", [P, 2, NP * 2, 2, B_HD])
        v, ncum = s.sb("v", [P, SLOTS, NP, CPP]), s.sb("ncum", [P, SLOTS, 2, SEQ])
        kk, kl = s.sb("kk", [P, SLOTS, 2, SEQ], fp32r), s.sb("kl", [P, SLOTS, 2, SEQ], fp32r)
        qq = s.sb("qq", [P, SLOTS, 2, SEQ], fp32r)
        ident_r, mask_r = s.sb("ident_r", [P, P], fp32r), s.sb("mask_r", [P, P], fp32r)
        prob, pt = s.sb("prob", [P, PROBS, SEQ]), s.sb("pt", [P, 2, NP, P])
        mx, rs, rinv = s.sb("mx", [P, PROBS]), s.sb("rs", [P, PROBS]), s.sb("rinv", [P, 2])
        o = s.sb("o", [P, SLOTS, NP, CPP])
        (k_loaded, q_loaded, turned, in_high, scores_ready, shifted, max_done, exp_done, pv_ready, o_done, chain_sem, made) = (
            s.sem(n) for n in ("k_loaded", "q_loaded", "turned", "in_high", "scores_ready", "shifted", "max_done",
                               "exp_done", "pv_ready", "o_done", "chain", "made"))
        doubled = s.sem("doubled")
        freed = [s.sem("freed_by_dve"), s.sem("freed_by_act")]
        nc_loaded, v_loaded, stored = ([s.sem(f"{n}{i}") for i in range(SLOTS)] for n in ("nc_loaded", "v_loaded", "stored"))
        settled = s.sem("settled")
        ps = [s.ps(f"scores{e}", [P, SEQ]) for e in range(2)]
        tb = [s.ps(f"turn{i}", [P, 4, P]) for i in range(2)]
        po = [s.ps(f"o_psum{e}", [P, B_HD]) for e in range(2)]

        def pairs(engine, body, chain=None):
            run(engine, B_PAIRS // SLOTS, lambda i: [body(SLOTS * i + slot, slot) for slot in range(SLOTS)], chain, peel_last=True)

        def ahead(j, slot, u):
            return (j, slot, u + AHEAD) if u + AHEAD < UNITS else (j + 1, 1 - slot, u + AHEAD - UNITS)

        def before(j, slot, u):
            return (j, slot, u - 1) if u else (j - 1, 1 - slot, UNITS - 1)

        def copy_probs(engine, copy, bank, j, u):
            for b, tiles, n, _ in groups(j, u):
                if b != bank:
                    continue
                engine.wait_ge(turned, turned_count(j, n))
                if u >= 2 or not below(j, 1):
                    engine.wait_ge(pv_ready, j * UNITS + u - 1)
                copy(pt[:, u % 2, tiles[0]:tiles[-1] + 1, :], tb[bank][:, 0:len(tiles), :]).then_inc(freed[bank], 1)

        with nc.Block() as block:

            @block.sync
            def _(sp):
                def load_kq(j):
                    cols = bass.ds(j * CPP, CPP)
                    sp.dma_start(kq[:, 0], kv[:, :, cols]).then_inc(k_loaded, 16)
                    sp.dma_start(kq[:, 1], qv[:, :, cols]).then_inc(q_loaded, 16)

                def load(j, slot):
                    cols = bass.ds(j * CPP, CPP)
                    if not below(j, SLOTS):
                        wait(sp, shifted, (j - 1) * UNITS)
                    for e in range(2):
                        sp.dma_start(ncum[:, slot, e, :], ncp_d[bass.ds(2 * j + e, 1), :].to_broadcast((P, SEQ))).then_inc(nc_loaded[slot], 16)
                    if not below(j, SLOTS):
                        wait(sp, pv_ready, (j - 1) * UNITS)
                    sp.dma_start(v[:, slot], vv[:, :, cols]).then_inc(v_loaded[slot], 16)
                    if exists(j + 1):
                        wait(sp, doubled, 4 * j + 4)
                        load_kq(j + 1)

                load_kq(0)
                pairs(sp, load)
                for slot in range(SLOTS):
                    sp.wait_ge(v_loaded[slot], 16 * (B_PAIRS // SLOTS))

            @block.gpsimd
            def _(pool):
                def double(j):
                    if not below(j, 1):
                        wait(pool, turned, len(IN) if below(j, 2) else turned_count(j - 2, last_in))
                    for part in range(2):
                        wait(pool, (k_loaded, q_loaded)[part], j * 16 + 16)
                        src = kq[:, part].rearrange("p t (e d) -> p (t e) d", d=B_HD)
                        for r in range(2):
                            pool.tensor_tensor(twice[:, part, :, r, :], src, g.one[:, :].rearrange("p (a b) -> p a b", a=1).to_broadcast(src.shape),
                                               ALU.mult).then_inc(doubled, 1)

                def store(j, slot):
                    if exists(j + 1):
                        double(j + 1)
                    wait(pool, o_done, j * UNITS + UNITS)
                    pool.dma_start(ov[:, :, bass.ds(j * CPP, CPP)], o[:, slot]).then_inc(stored[slot], 16)

                double(0)
                pairs(pool, store)
                for slot in range(SLOTS):
                    pool.wait_ge(stored[slot], 16 * (B_PAIRS // SLOTS))

            @block.tensor
            def _(pe):
                def turn_in(j, slot, item, bank_count):
                    part, e, h = item
                    pe.wait_ge(doubled, 4 * j + 2 * part + 2)
                    if bank_count is not None:
                        pe.wait_ge(freed[0], bank_count)
                    for m in range(4):
                        both = twice[:, part, 2 * (4 * h + m) + e].rearrange("p r d -> p (r d)")
                        ins = pe.transpose(tb[0][:, m, :], both, g.ident[:, :])
                    ins.then_inc(turned, 1)

                def scores(j, slot, u):
                    i, e = u // 2, u % 2
                    if u >= 2 or not below(j, 1):
                        pe.wait_ge(shifted, j * UNITS + u - 1)
                    if u == 0:
                        pe.wait_ge(freed[0], len(IN) if below(j, 1) else freed_count(j - 1, 0, last_in_freed))
                    qs, width = slice(i * P, (i + 1) * P), (i + 1) * P
                    for a in range(0, width, CB):
                        b = min(a + CB, width)
                        pe.matmul(ps[e][:, a:b], qq[:, slot, e, qs], kk[:, slot, e, a:b], start=True, stop=False)
                        pe.matmul(ps[e][:, a:b], qq[0:B_HD, slot, e, qs], kl[0:B_HD, slot, e, a:b], start=False, stop=(b < width))
                    pe.matmul(ps[e][:, width - P:width], ident_r[:, :], mask_r[:, :], start=False, stop=True).then_inc(scores_ready, 1)

                def turn(j, u):
                    pe.wait_ge(exp_done, j * UNITS + u + 1)
                    for bank, tiles, n, freed_n in groups(j, u):
                        if freed_n > 1 or bank == 0 or not below(j, 1):
                            pe.wait_ge(freed[bank], freed_count(j, bank, freed_n - 1))
                        for m, t in enumerate(tiles):
                            ins = pe.transpose(tb[bank][:, m, :], prob[:, u % PROBS, t * P:(t + 1) * P], g.ident[:, :])
                        ins.then_inc(turned, 1)

                def weigh(j, slot, u):
                    i, e = u // 2, u % 2
                    for bank, tiles, n, freed_n in groups(j, u):
                        pe.wait_ge(freed[bank], freed_count(j, bank, freed_n))
                    if u >= 2 or not below(j, 1):
                        pe.wait_ge(o_done, j * UNITS + u - 1)
                    if u == 0:
                        pe.wait_ge(v_loaded[slot], (j - slot) * 8 + 16)
                    for t in range(i + 1):
                        ins = pe.matmul(po[e][:, :], pt[:, u % 2, t, :], v[:, slot, t, e * B_HD:(e + 1) * B_HD], start=(t == 0), stop=(t == i))
                    ins.then_inc(pv_ready, 1)

                def pair(j, slot):
                    for u in range(UNITS):
                        if u in incoming and exists(j + 1):
                            item, n, freed_n = incoming[u]
                            turn_in(j + 1, 1 - slot, item, freed_count(j, 0, freed_n - 1))
                        nj, nslot, nu = ahead(j, slot, u)
                        if exists(nj):
                            scores(nj, nslot, nu)
                        turn(j, u)
                        bj, bslot, bu = before(j, slot, u)
                        if exists(bj):
                            weigh(bj, bslot, bu)

                pe.wait_ge(made, 2)
                for n, item in enumerate(IN):
                    turn_in(0, 0, item, n if n else None)
                for u in range(AHEAD):
                    scores(0, 0, u)
                pairs(pe, pair)
                weigh(B_PAIRS - 1, SLOTS - 1, UNITS - 1)

            @block.vector
            def _(dve):
                c = Chain(dve, chain_sem)

                def low_in(j, slot, item, n):
                    part, e, h = item
                    cols = slice(h * CB, (h + 1) * CB)
                    dve.wait_ge(in_high, n)
                    rows, high, low = ((slice(0, B_HD), kk, kl), (slice(B_HD, P), qq, qq))[part]
                    dve.tensor_tensor(low[rows, slot, e, cols], tb[0][rows, :, :].rearrange("p t n -> p (t n)"),
                                      f32(high[rows, slot, e, cols]), ALU.subtract).then_inc(freed[0], 1)

                def shift(j, slot, u):
                    e, width, k = u % 2, (u // 2 + 1) * P, u % PROBS
                    dve.wait_ge(scores_ready, j * UNITS + u + 1)
                    if u == 0:
                        dve.wait_ge(nc_loaded[slot], (j - slot) * 16 + 32)
                    if u >= PROBS or not below(j, 1):
                        fu, fj = (u - PROBS, j) if u >= PROBS else (u - PROBS + UNITS, j - 1)
                        dve.wait_ge(turned, turned_count(fj, groups(fj, fu)[-1][2]))
                    settle(dve, settled)
                    dve.tensor_tensor_reduce(out=prob[:, k, 0:width], in0=ps[e][:, 0:width], in1=ncum[:, slot, e, 0:width], scale=1.0, scalar=-3e38,
                                             op0=ALU.add, op1=ALU.max, accum_out=mx[:, k:k + 1]).then_inc(shifted, 1)
                    dve.wait_ge(shifted, j * UNITS + u + 1)
                    dve.tensor_scalar(mx[:, k:k + 1], mx[:, k:k + 1], -1.0, None, ALU.mult).then_inc(max_done, 1)

                def scale_out(j, slot, u):
                    i, e, k = u // 2, u % 2, u % PROBS
                    c.link(dve.reciprocal(rinv[:, e:e + 1], rs[:, k:k + 1]))
                    dve.wait_ge(pv_ready, j * UNITS + u + 1)
                    if u == 0 and not below(j, SLOTS):
                        dve.wait_ge(stored[slot], (j - slot) * 8)
                    dve.tensor_scalar(o[:, slot, i, e * B_HD:(e + 1) * B_HD], po[e][:, :], rinv[:, e:e + 1], None, ALU.mult).then_inc(o_done, 1)

                def pair(j, slot):
                    for u in range(UNITS):
                        if u in incoming and exists(j + 1):
                            low_in(j + 1, 1 - slot, incoming[u][0], (j + 1) * len(IN) + u - FIRST_IN + 1)
                        nj, nslot, nu = ahead(j, slot, u)
                        if exists(nj):
                            shift(nj, nslot, nu)
                        copy_probs(dve, dve.tensor_copy, 0, j, u)
                        bj, bslot, bu = before(j, slot, u)
                        if exists(bj):
                            scale_out(bj, bslot, bu)
                        else:
                            c.link(dve.tensor_copy(rinv[:, :], g.ident[:, 0:2]))

                dve.tensor_copy(ident_r[:, :], g.ident[:, :]).then_inc(made, 1)
                dve.tensor_copy(mask_r[:, :], g.mask_qk[:, :]).then_inc(made, 1)
                for n, item in enumerate(IN):
                    low_in(0, 0, item, n + 1)
                for u in range(AHEAD):
                    shift(0, 0, u)
                pairs(dve, pair, c)
                scale_out(B_PAIRS - 1, SLOTS - 1, UNITS - 1)

            @block.scalar
            def _(act):
                def high_in(j, slot, item, count):
                    part, e, h = item
                    act.wait_ge(turned, count)
                    act.activation((kk, qq)[part][:, slot, e, h * CB:(h + 1) * CB], tb[0][:, :, :].rearrange("p t n -> p (t n)"),
                                   ACT.Copy).then_inc(in_high, 1)

                def exponential(j, u):
                    k, width = u % PROBS, (u // 2 + 1) * P
                    act.wait_ge(max_done, j * UNITS + u + 1)
                    if u >= PROBS or not below(j, 1):
                        act.wait_ge(o_done, j * UNITS + u - PROBS + 1)
                    act.activation(prob[:, k, 0:width], prob[:, k, 0:width], ACT.Exp, bias=mx[:, k:k + 1],
                                   accum_out=rs[:, k:k + 1]).then_inc(exp_done, 1)

                def copy(out, in_):
                    return act.activation(out, in_, ACT.Copy)

                def pair(j, slot):
                    for u in range(UNITS):
                        if u in incoming and exists(j + 1):
                            item, n, _ = incoming[u]
                            high_in(j + 1, 1 - slot, item, turned_count(j, n))
                        copy_probs(act, copy, 1, j, u)
                        nj, _, nu = ahead(j, slot, u)
                        if exists(nj):
                            exponential(nj, nu)

                for n, item in enumerate(IN):
                    high_in(0, 0, item, n + 1)
                for u in range(AHEAD):
                    exponential(0, u)
                pairs(act, pair)


def fox_running(nc, g, q_d, cache_k, cache_v, k_sample, v_sample, ncd_d, half_d, o_d):
    HALVES = 2
    JH = B_PAIRS // HALVES
    NS = DEC_SEQ
    SLOTS = 2
    kc = cache_k.rearrange("s (t p) h d -> s p t (h d)", p=P)
    vc = cache_v.rearrange("s (t p) h d -> s p t (h d)", p=P)
    kn_d, vn_d = k_sample.rearrange("s t h d -> s t (h d)"), v_sample.rearrange("s t h d -> s t (h d)")
    qn_d = q_d[NT - 1].rearrange("(s t) d -> s t d", t=NS)
    with Scope(nc, "frun") as s:
        k, small = s.sb("k", [P, PAST_T, D]), s.sb("small", [NS, 2, D])
        v, vn, ncum = s.sb("v", [P, SLOTS, PAST_T, D]), s.sb("vn", [NS, SLOTS, D]), s.sb("ncum", [P, SLOTS, HALVES, DK])
        kt, ktn, qb = s.sb("kt", [P, B_PAIRS, PAST]), s.sb("ktn", [P, B_PAIRS, NS]), s.sb("qb", [P, B_PAIRS, 2 * NS])
        prob, pt, ptn = s.sb("prob", [P, HALVES, DK]), s.sb("pt", [P, HALVES, PAST_T, P]), s.sb("ptn", [NS, HALVES, P])
        mx, rs, rinv, sel = s.sb("mx", [P, 2]), s.sb("rs", [P, 2]), s.sb("rinv", [P, 2]), s.sb("sel", [P, 2, 2])
        o = s.sb("o", [P, HALVES, B_HD])
        names = ("k_loaded", "kn_loaded", "qn_loaded", "turned", "copied", "small_turned", "kn_copied", "qn_copied", "filled", "scores_ready",
                 "shifted", "max_done", "exp_done", "p_turned", "p_copied", "pv_ready", "o_done", "chain", "moved")
        (k_loaded, kn_loaded, qn_loaded, turned, copied, small_turned, kn_copied, qn_copied, filled, scores_ready,
         shifted, max_done, exp_done, p_turned, p_copied, pv_ready, o_done, chain_sem, moved) = (s.sem(n) for n in names)
        v_loaded, vn_loaded, nc_loaded = ([s.sem(f"{n}{i}") for i in range(SLOTS)] for n in ("v_loaded", "vn_loaded", "nc_loaded"))
        stored = [s.sem(f"stored{i}") for i in range(HALVES)]
        settled, pe_settled = s.sem("settled"), s.sem("pe_settled")
        ps = s.ps("scores", [P, 2 * CB])
        tb = [s.ps(f"turn{i}", [P, 4, P]) for i in range(2)]
        tp = [s.ps(f"pturn{i}", [P, 4, P]) for i in range(2)]
        small_p, po = s.ps("small_p", [P, CB]), s.ps("o_psum", [P, P])

        with nc.Block() as block:

            @block.sync
            def _(sp):
                def load(i2):
                    for slot in range(SLOTS):
                        i = SLOTS * i2 + slot
                        if not below(i, 1):
                            wait(sp, turned, i * B_PAIRS)
                        sp.dma_start(k[:, :, :], kc[i]).then_inc(k_loaded, 16)
                        if not below(i, 1):
                            wait(sp, small_turned, 2 * i)
                        sp.dma_start(small[:, 0], kn_d[i]).then_inc(kn_loaded, 16)
                        sp.dma_start(small[:, 1], qn_d[i]).then_inc(qn_loaded, 16)
                        if not below(i, SLOTS):
                            wait(sp, pv_ready, (i - 1) * HALVES)
                        sp.dma_start(v[:, slot], vc[i]).then_inc(v_loaded[slot], 16)
                        sp.dma_start(vn[:, slot], vn_d[i]).then_inc(vn_loaded[slot], 16)
                        for e in range(HALVES):
                            sp.dma_start(ncum[:, slot, e, :], ncd_d[i, 8 * e:8 * e + 8].rearrange("h q k -> (h q) k")).then_inc(nc_loaded[slot], 16)

                run(sp, DEC_BATCH // SLOTS, load)
                for e in range(HALVES):
                    sp.wait_ge(stored[e], 16 * DEC_BATCH)
                for i in range(DEC_BATCH):
                    sp.dma_start(o_d[NT - 1, i * NS:(i + 1) * NS, :].rearrange("q (h d) -> h q d", d=B_HD),
                                 half_d[i].rearrange("e (h q) d -> (e h) q d", q=NS)).then_inc(moved, 16)
                sp.wait_ge(moved, 16 * DEC_BATCH)

            @block.gpsimd
            def _(pool):
                pool.memset(qb[:, :, :], 0.0).then_inc(filled, 1)

                def store(i):
                    for e in range(HALVES):
                        wait(pool, o_done, i * HALVES + e + 1)
                        pool.dma_start(half_d[i, e], o[:, e, :]).then_inc(stored[e], 16)

                run(pool, DEC_BATCH, store)

            @block.tensor
            def _(pe):
                def stream(i, slot):
                    first = below(i, 1)
                    pe.wait_ge(k_loaded, i * 16 + 16)
                    for j in range(B_PAIRS):
                        if j >= 2 or not first:
                            pe.wait_ge(copied, i * B_PAIRS + j - 1)
                        for t in range(PAST_T):
                            ins = pe.transpose(tb[j % 2][:, t, :], k[:, t, j * P:(j + 1) * P], g.ident[:, :])
                        ins.then_inc(turned, 1)
                    for part, (loaded, used) in enumerate(((kn_loaded, qn_copied), (qn_loaded, kn_copied))):
                        pe.wait_ge(loaded, i * 16 + 16)
                        if part or not first:
                            pe.wait_ge(used, i + part)
                        settle(pe, pe_settled)
                        for j in range(B_PAIRS):
                            ins = pe.transpose(small_p[:, j * NS:(j + 1) * NS], small[:, part, j * P:(j + 1) * P], g.ident[0:NS, 0:NS])
                        ins.then_inc(small_turned, 1)
                    pe.wait_ge(copied, i * B_PAIRS + B_PAIRS)
                    pe.wait_ge(kn_copied, i + 1)
                    pe.wait_ge(qn_copied, i + 1)

                    def scores(e):
                        u = i * HALVES + e
                        if not below(u, 1):
                            pe.wait_ge(shifted, u)
                        for n in range(JH):
                            pe.matmul(ps[32 * n:32 * n + 32, 0:PAST], qb[:, JH * e + n, :], kt[:, JH * e + n, :], start=True, stop=True)
                        for n in range(JH):
                            rows = slice(32 * n, 32 * n + 32)
                            pe.matmul(ps[rows, CB:CB + NS], qb[:, JH * e + n, :], ktn[:, JH * e + n, :], start=True, stop=False)
                            ins = pe.matmul(ps[rows, CB:CB + NS], g.ident[:, rows], g.mask_new[:, :], start=False, stop=True)
                        ins.then_inc(scores_ready, 1)

                    def turn_and_weigh(e):
                        u = i * HALVES + e
                        pe.wait_ge(exp_done, u + 1)
                        if not below(u, 1):
                            pe.wait_ge(p_copied, 2 * u)
                        for t in range(PAST_T):
                            ins = pe.transpose(tp[0][:, t, :], prob[:, e, t * P:(t + 1) * P], g.ident[:, :])
                        ins.then_inc(p_turned, 1)
                        pe.transpose(tp[1][0:NS, 0, :], prob[:, e, PAST:DK], g.ident[:, :]).then_inc(p_turned, 1)
                        pe.wait_ge(p_copied, 2 * u + 2)
                        if not below(u, 1):
                            pe.wait_ge(o_done, u)
                        if e == 0:
                            pe.wait_ge(v_loaded[slot], (i - slot) * 8 + 16)
                            pe.wait_ge(vn_loaded[slot], (i - slot) * 8 + 16)
                        for n in range(JH):
                            rows, cols = slice(32 * n, 32 * n + 32), slice((JH * e + n) * P, (JH * e + n + 1) * P)
                            for t in range(PAST_T):
                                pe.matmul(po[rows, :], pt[:, e, t, rows], v[:, slot, t, cols], start=(t == 0), stop=False)
                            ins = pe.matmul(po[rows, :], ptn[:, e, rows], vn[:, slot, cols], start=False, stop=True)
                        ins.then_inc(pv_ready, 1)

                    scores(0)
                    scores(1)
                    turn_and_weigh(0)
                    turn_and_weigh(1)

                run(pe, DEC_BATCH // SLOTS, lambda i2: [stream(SLOTS * i2 + slot, slot) for slot in range(SLOTS)])

            @block.scalar
            def _(act):
                def stream(i, slot):
                    for j in range(B_PAIRS):
                        act.wait_ge(turned, i * B_PAIRS + j + 1)
                        if j == 0 and not below(i, 1):
                            act.wait_ge(scores_ready, i * HALVES)
                        act.activation(kt[:, j, :], tb[j % 2][:, :, :].rearrange("p t n -> p (t n)"), ACT.Copy).then_inc(copied, 1)
                    act.wait_ge(small_turned, 2 * i + 1)
                    act.activation(ktn[:, :, :], small_p[:, 0:B_PAIRS * NS].rearrange("p (j n) -> p j n", n=NS), ACT.Copy).then_inc(kn_copied, 1)
                    for e in range(HALVES):
                        u = i * HALVES + e
                        act.wait_ge(max_done, u + 1)
                        if not below(u, HALVES):
                            act.wait_ge(o_done, u - 1)
                        act.activation(prob[:, e, :], prob[:, e, :], ACT.Exp, bias=mx[:, e:e + 1], accum_out=rs[:, e:e + 1]).then_inc(exp_done, 1)

                run(act, DEC_BATCH // SLOTS, lambda i2: [stream(SLOTS * i2 + slot, slot) for slot in range(SLOTS)])

            @block.vector
            def _(dve):
                c = Chain(dve, chain_sem)

                def stream(i, slot):
                    dve.wait_ge(small_turned, 2 * i + 2)
                    dve.wait_ge(filled, 1)
                    for half in range(2):
                        rows = slice(half * B_HD, (half + 1) * B_HD)
                        ins = dve.tensor_copy(qb[rows, :, half * NS:(half + 1) * NS], small_p[rows, 0:B_PAIRS * NS].rearrange("p (j n) -> p j n", n=NS))
                        if half == 0:
                            c.link(ins)
                    ins.then_inc(qn_copied, 1)
                    for e in range(HALVES):
                        u = i * HALVES + e
                        dve.wait_ge(scores_ready, u + 1)
                        dve.wait_ge(nc_loaded[slot], (i - slot) * 16 + 32)
                        if not below(u, HALVES):
                            dve.wait_ge(p_turned, 2 * u - 2)
                        settle(dve, settled)
                        dve.tensor_tensor_reduce(out=prob[:, e, :], in0=ps[:, 0:DK], in1=ncum[:, slot, e, :], scale=1.0, scalar=-3e38,
                                                 op0=ALU.add, op1=ALU.max, accum_out=mx[:, e:e + 1]).then_inc(shifted, 1)
                        dve.wait_ge(shifted, u + 1)
                        dve.tensor_scalar(mx[:, e:e + 1], mx[:, e:e + 1], -1.0, None, ALU.mult).then_inc(max_done, 1)
                    for e in range(HALVES):
                        u = i * HALVES + e
                        dve.wait_ge(p_turned, 2 * u + 1)
                        dve.tensor_copy(pt[:, e], tp[0][:, :, :]).then_inc(p_copied, 1)
                        dve.wait_ge(p_turned, 2 * u + 2)
                        dve.tensor_copy(ptn[:, e], tp[1][0:NS, 0, :]).then_inc(p_copied, 1)
                        c.link(dve.reciprocal(rinv[:, e:e + 1], rs[:, e:e + 1]))
                        c.link(dve.tensor_scalar(sel[:, e, :], g.parity[:, :], rinv[:, e:e + 1], None, ALU.mult))
                        dve.wait_ge(pv_ready, u + 1)
                        if not below(i, 1):
                            dve.wait_ge(stored[e], i * 16)
                        c.link(dve.tensor_scalar(o[:, e, :], po[:, 0:B_HD], sel[:, e, 0:1], None, ALU.mult))
                        dve.scalar_tensor_tensor(o[:, e, :], po[:, B_HD:P], sel[:, e, 1:2], o[:, e, :], ALU.mult, ALU.add).then_inc(o_done, 1)

                run(dve, DEC_BATCH // SLOTS, lambda i2: [stream(SLOTS * i2 + slot, slot) for slot in range(SLOTS)], c)


def store_x(nc, g, y_prompt, y_sample):
    with Scope(nc, "out") as s:
        stored = s.sem("stored")
        with nc.Block() as block:

            @block.sync
            def _(sp):
                sp.dma_start(y_prompt.rearrange("(t p) d -> p t d", p=P), g.x[:, 0:NP, :]).then_inc(stored, 16)
                sp.dma_start(y_sample, g.x[:, NP, :]).then_inc(stored, 16)
                sp.wait_ge(stored, 32)


def build(nc, A, O):
    (y_prompt, y_sample, k_prompt, v_prompt, logf_prompt, c_prompt, n_prompt, m_prompt,
     k_sample, v_sample, logf_sample, c_sample, n_sample, m_sample) = O

    def scratch(name, shape):
        return nc.dram_tensor(name, shape, fp32, kind="Internal").ap()

    qkvo = scratch("qkvo", (NT, P, A_O0 + A_H * A_V))
    gates_d = scratch("mlstm_gates_rows", (2 * A_H, T_ALL))
    h_d = scratch("mlstm_h", (NT, P, D))
    fgates_d = scratch("fox_gates_rows", (B_H, T_ALL))
    q_d, sg_d, o_d = scratch("fox_q", (NT, P, D)), scratch("fox_out_gate", (NT, P, D)), scratch("fox_o", (NT, P, D))
    ncp_d = scratch("neg_cum_prompt", (B_H, SEQ))
    ncd_d = scratch("neg_cum_running", (DEC_BATCH, B_H, DEC_SEQ, DK))
    half_d = scratch("fox_o_running", (DEC_BATCH, 2, P, B_HD))

    class Globals:
        pass

    g = Globals()
    with Scope(nc, "g") as top:
        g.x = top.sb("x", [P, NT, D])
        g.ident = top.sb("ident", [P, P])
        g.one = top.sb("one", [P, 1])
        g.mask_kq, g.mask_qk = top.sb("mask_kq", [P, 2, P]), top.sb("mask_qk", [P, P])
        setup(nc, g, A["x_prompt"][0], A["x_sample"].rearrange("s t d -> (s t) d"))
        with Scope(nc, "A1") as s:
            xth, xtl = s.sb("xth", [P, KC, T_ALL], fp32r), s.sb("xtl", [P, KC, T_ALL], fp32r)
            linear(nc, g, xth, xtl, "w_in", A["w_in_a"][0],
                   [(0, 4, "store", lambda b, t: qkvo[t, :, bass.ds(b * CB, CB)]),
                    (A_O0, 2, "sigmoid", lambda b, t: qkvo[t, :, bass.ds(A_O0 + b * CB, CB)])],
                   gates=(A_O0 + A_H * A_V, 2 * A_H, gates_d), kind="norm", gain_row=A["g_mix"][0:1, :])
        with Scope(nc, "A2") as s:
            g.sel, g.pair_sel = s.sb("sel", [A_H, A_H, P]), s.sb("pair_sel", [A_H, A_PAIRS, 2, A_QK])
            g.own, g.ones8 = s.sb("own", [P, DEC_BATCH]), s.sb("ones8", [A_H, P])
            g.mask_dec = s.sb("mask_dec", [P, 2, P])
            g.B, g.tok = s.sb("B", [A_H, T_ALL]), s.sb("tok", [P, NT, 4, A_H])
            g.gc_pair, g.gc_dec, g.gc_s = s.sb("gc_pair", [P, A_PAIRS, NP]), s.sb("gc_dec", [P, A_H, DEC_BATCH]), s.sb("gc_s", [DEC_BATCH, A_H])
            mlstm_gates(nc, g, gates_d, A["b_i_a"], A["b_f_a"], A["state_m"], m_prompt, m_sample)
            mlstm(nc, g, qkvo, h_d, False, c_prompt, n_prompt)
            mlstm(nc, g, qkvo, h_d, True, c_sample, n_sample, A["state_c"], A["state_n"])
        with Scope(nc, "A3") as s:
            xth, xtl = s.sb("xth", [P, KC, T_ALL], fp32r), s.sb("xtl", [P, KC, T_ALL], fp32r)
            linear(nc, g, xth, xtl, "w_out", A["w_out_a"][0], [(0, 2, "residual", None)],
                   kind="mlstm", a=h_d, b=qkvo[:, :, A_O0:A_O0 + D], gain_row=A["g_head_a"])
            ffn(nc, g, xth, xtl, "ffn0", A["w_gu"][0], A["w_down"][0], A["g_ffn"][0:1, :])

            def rows(prompt, sample):
                pv, sv = prompt.rearrange("o (t p) h d -> (o t) p (h d)", p=P), sample.rearrange("s t h d -> (s t) (h d)")
                return lambda b, t: (pv[t] if t < NP else sv)[:, bass.ds(b * CB, CB)]

            linear(nc, g, xth, xtl, "w_kvf", A["w_kvf"],
                   [(0, 2, ("norm", A["g_k"].rearrange("(o d) -> o d", o=1), 1.0), rows(k_prompt, k_sample)),
                    (D, 2, "store", rows(v_prompt, v_sample))], gates=(2 * D, B_H, fgates_d),
                   kind="norm", gain_row=A["g_kv"].rearrange("(o d) -> o d", o=1))
            linear(nc, g, xth, xtl, "w_qg", A["w_qg_b"][0],
                   [(0, 2, ("norm", A["g_q_b"], B_HD ** -0.5), lambda b, t: q_d[t, :, bass.ds(b * CB, CB)]),
                    (D, 2, "sigmoid", lambda b, t: sg_d[t, :, bass.ds(b * CB, CB)])],
                   kind="norm", gain_row=A["g_mix"][1:2, :])
        with Scope(nc, "B1") as s:
            g.own, g.parity, g.mask_new = s.sb("own", [P, DEC_BATCH]), s.sb("parity", [P, 2]), s.sb("mask_new", [P, DEC_SEQ])
            fox_gates(nc, g, fgates_d, A["b_f_b"], A["cache_logf"], logf_prompt, logf_sample, ncp_d, ncd_d)
            fox_prompt(nc, g, q_d, k_prompt.rearrange("o t h d -> (o t) (h d)"), v_prompt.rearrange("o t h d -> (o t) (h d)"), ncp_d, o_d)
            fox_running(nc, g, q_d, A["cache_k"], A["cache_v"], k_sample, v_sample, ncd_d, half_d, o_d)
        with Scope(nc, "B2") as s:
            xth, xtl = s.sb("xth", [P, KC, T_ALL], fp32r), s.sb("xtl", [P, KC, T_ALL], fp32r)
            linear(nc, g, xth, xtl, "w_o", A["w_o_b"][0], [(0, 2, "residual", None)], kind="gated", a=o_d, b=sg_d)
            ffn(nc, g, xth, xtl, "ffn1", A["w_gu"][1], A["w_down"][1], A["g_ffn"][1:2, :])
        store_x(nc, g, y_prompt[0], y_sample.rearrange("s t d -> (s t) d"))


_INS = ['x_prompt', 'x_sample', 'cache_k', 'cache_v', 'cache_logf', 'state_c', 'state_n', 'state_m', 'g_mix', 'g_ffn',
        'w_in_a', 'b_i_a', 'b_f_a', 'g_head_a', 'w_out_a', 'g_kv', 'w_kvf', 'b_f_b', 'g_k', 'w_qg_b', 'g_q_b', 'w_o_b',
        'w_gu', 'w_down']
_OUTS = [(1, SEQ, D), (DEC_BATCH, DEC_SEQ, D), (1, SEQ, B_H, B_HD), (1, SEQ, B_H, B_HD), (1, SEQ, B_H),
         (1, 1, A_H, A_V, A_QK), (1, 1, A_H, A_QK), (1, 1, A_H),
         (DEC_BATCH, DEC_SEQ, B_H, B_HD), (DEC_BATCH, DEC_SEQ, B_H, B_HD), (DEC_BATCH, DEC_SEQ, B_H),
         (DEC_BATCH, 1, A_H, A_V, A_QK), (DEC_BATCH, 1, A_H, A_QK), (DEC_BATCH, 1, A_H)]


def kernel(**inputs):
    import numpy as _np
    import concourse.bacc as _bacc
    from concourse import mybir as _mybir
    from concourse.bass_utils import run_bass_kernel_spmd as _run

    nc = _bacc.Bacc("TRN2", target_bir_lowering=False, num_devices=1)
    arrays, args = {}, {}
    for name in _INS:
        a = _np.ascontiguousarray(inputs[name])
        arrays[f"in_{name}_dram"] = a
        args[name] = nc.dram_tensor(f"in_{name}_dram", a.shape, _mybir.dt.from_np(a.dtype), kind="ExternalInput").ap()
    outs = [nc.dram_tensor(f"out_{i}_dram", shape, _mybir.dt.float32, kind="ExternalOutput").ap() for i, shape in enumerate(_OUTS)]
    build(nc, args, outs)
    r = _run(nc, [arrays], core_ids=[0])
    return tuple(r.results[0][f"out_{i}_dram"] for i in range(len(_OUTS)))
```

```python
import concourse.bass as bass
from concourse import mybir
from contextlib import ExitStack, contextmanager

fp32 = mybir.dt.float32
fp32r = mybir.dt.float32r
ACT = mybir.ActivationFunctionType
ALU = mybir.AluOpType
AX = mybir.AxisListType

P = 128
D = 1024
SEQ = 1024
DEC_BATCH, DEC_SEQ, PAST = 8, 16, 512
T_ALL = SEQ + DEC_BATCH * DEC_SEQ
NT = T_ALL // P
NP = SEQ // P
KC = D // P
CB = 512
THIRD = T_ALL // 3
A_H, A_QK, A_V = 8, 64, 128
A_PAIRS = A_H // 2
B_H, B_HD = 16, 64
B_PAIRS = B_H // 2
D_FF = 2816
FG = 2
FFN_GROUPS = D_FF // (FG * P)
EPS = 1e-6
CAP = 15.0
NEG = -1e30
X_AHEAD = 3
A_Q0, A_K0, A_V0, A_O0 = 0, 512, 1024, 2048
PAST_T = PAST // P
DK = PAST + DEC_SEQ


def below(i, n):
    return isinstance(i, int) and i < n


def wait(engine, sem, count):
    if not isinstance(count, int):
        engine.wait_ge(sem, 1)
    engine.wait_ge(sem, count)


def settle(engine, sem):
    engine.sem_inc(sem, 1)


def round_high(pool, g, out, in_):
    ones = g.one[:, :].rearrange("p (a b) -> p a b", a=1).to_broadcast((P, *in_.shape[1:]))
    return pool.tensor_tensor(out, in_, ones, ALU.mult)


class Chain:

    def __init__(self, engine, sem):
        self.engine, self.sem, self.n, self.base = engine, sem, 0, 0

    def link(self, ins):
        self.n += 1
        ins.then_inc(self.sem, 1)
        self.engine.wait_ge(self.sem, self.base + self.n)


    def mark(self, ins):
        self.n += 1
        ins.then_inc(self.sem, 1)

    def join(self):
        self.engine.wait_ge(self.sem, self.base + self.n)


def run(engine, count, body, chain=None, peel_last=False, per=None):
    start = chain.n if chain else 0
    end = count - 1 if peel_last else count
    body(0)
    first = chain.n if chain else 0
    per = per or first - start
    if end > 1:
        with engine.Fori(1, end) as i:
            if chain:
                chain.base, chain.n = i * per + (first - per), 0
            body(i)
            if chain:
                assert chain.n == per
        if chain:
            chain.base, chain.n = 0, first + (end - 1) * per
    if peel_last:
        body(count - 1)


class Scope:

    def __init__(self, nc, tag):
        self.nc, self.tag, self.ctx, self.sems = nc, tag, ExitStack(), []

    def __enter__(self):
        return self

    def __exit__(self, *a):
        if a[0] is not None:
            return
        if self.sems:
            self.nc.clear_and_free_semaphores(self.sems)
            self.nc.all_engine_barrier()
        self.ctx.close()

    def sb(self, name, shape, dt=fp32):
        return self.ctx.enter_context(self.nc.sbuf_tensor(f"{self.tag}_{name}", shape, dt))

    def brief(self, name, shape):
        with self.nc.sbuf_tensor(f"{self.tag}_{name}", shape, fp32) as tile:
            return tile

    def ps(self, name, shape):
        cols = 1
        for n in shape[1:]:
            cols *= n
        banks = -(-cols // CB)
        whole = self.ctx.enter_context(self.nc.psum_tensor(f"{self.tag}_{name}", [P, banks * CB], fp32))
        letters = "abc"[:len(shape) - 1]
        sizes = {k: n for k, n in zip(letters, shape[1:])}
        return whole[:, 0:cols].rearrange(f"p ({' '.join(letters)}) -> p {' '.join(letters)}", **sizes)

    def sem(self, name):
        self.sems.append(self.nc.alloc_semaphore(f"{self.tag}_{name}"))
        return self.sems[-1]


def spread(ap, n):
    return ap.rearrange("p (h o) -> p h o", o=1).to_broadcast((ap.shape[0], ap.shape[1], n))


def repeat(ap, n):
    return ap.rearrange("p (o d) -> p o d", o=1).to_broadcast((ap.shape[0], n, ap.shape[1]))


def f32(ap):
    return ap.bitcast(fp32)


def setup(nc, g):
    with Scope(nc, "setup") as s:
        made, filled = s.sem("made"), s.sem("filled")
        with nc.Block() as block:

            @block.sync
            def _(sp):
                for t in range(X_AHEAD):
                    sp.dma_start(g.x[:, t, :], g.x_tile(t)).then_inc(g.x_loaded[t], 16)

            @block.gpsimd
            def _(pool):
                pool.memset(g.one[:, :], 1.0).then_inc(filled, 1)
                pool.memset(g.ident[:, :], 0.0).then_inc(filled, 1)
                pool.memset(g.mask_kq[:, :, :], 0.0).then_inc(filled, 1)
                pool.memset(g.mask_qk[:, :], 0.0).then_inc(filled, 1)
                wait(pool, filled, 4)
                pool.affine_select(out=g.ident[:, :], in_=g.ident[:, :], compare_op=ALU.not_equal, fill=1.0,
                                   base=0, pattern=[[-1, P]], channel_multiplier=1).then_inc(made, 1)
                pool.affine_select(out=g.mask_kq[:, :, :], in_=g.mask_kq[:, :, :], compare_op=ALU.is_ge, fill=NEG,
                                   base=0, pattern=[[0, 2], [1, P]], channel_multiplier=-1).then_inc(made, 1)
                pool.affine_select(out=g.mask_qk[:, :], in_=g.mask_qk[:, :], compare_op=ALU.is_ge, fill=NEG,
                                   base=0, pattern=[[-1, P]], channel_multiplier=1).then_inc(made, 1)
                wait(pool, made, 3)


class Activations:
    SLOTS = 2
    HV = "p (h v) -> p h v"

    def __init__(self, nc, g, s, xth, xtl, kind, tok, psum, a=None, b=None, gain_row=None, x_arrives=False):
        self.x_arrives = x_arrives
        self.g, self.xth, self.xtl, self.kind, self.a, self.b, self.gain_row = g, xth, xtl, kind, a, b, gain_row
        self.tok, self.psum = tok, psum
        self.gain_loaded, self.tile_made = s.sem("x_gain_loaded"), s.sem("tile_made")
        self.transposed, self.high_done, self.low_done = s.sem("transposed"), s.sem("high_done"), s.sem("low_done")
        self.square_done, self.mean_done, self.root_done, self.chain_sem = (s.sem(n) for n in ("x_square", "x_mean", "x_root", "x_chain"))
        if kind != "gated":
            self.gain = s.sb("x_gain", [P, D])
        if kind == "norm":
            self.ss, self.rms = s.sb("x_ss", [P, NT]), s.sb("x_rms", [P, NT])
        else:
            self.b_in = s.sb("b_in", [P, self.SLOTS, D])
            self.a_loaded = [s.sem(f"a_loaded{i}") for i in range(self.SLOTS)]
            self.b_loaded = [s.sem(f"b_loaded{i}") for i in range(self.SLOTS)]
            self.b_scaled = s.sem("b_scaled")
        if kind == "mlstm":
            self.junk, self.ss, self.rms = s.sb("junk", [P, D]), s.sb("x_ss", [P, A_H]), s.sb("x_rms", [P, A_H])

    def load_gain(self, sp):
        if self.kind != "gated":
            sp.dma_start(self.gain[:, :], self.gain_row.to_broadcast((P, D))).then_inc(self.gain_loaded, 16)

    def scale_gates(self, pool, t):
        if self.kind != "mlstm" or t >= NT:
            return
        k = t % self.SLOTS
        if t < self.SLOTS:
            return
        if t == self.SLOTS:
            wait(pool, self.gain_loaded, 16)
        wait(pool, self.b_loaded[k], t // self.SLOTS * 16 + 16)
        pool.tensor_tensor(self.b_in[:, k, :], self.b_in[:, k, :], self.gain[:, :], ALU.mult).then_inc(self.b_scaled, 1)

    def load(self, act, t):
        if self.kind == "norm" or t >= NT:
            return
        k = t % self.SLOTS
        if t >= self.SLOTS:
            act.wait_ge(self.transposed, 2 * (t - self.SLOTS) + 2)
        act.dma_start(self.tok[:, k, :], self.a[t]).then_inc(self.a_loaded[k], 16)
        act.dma_start(self.b_in[:, k, :], self.b[t]).then_inc(self.b_loaded[k], 16)

    def root(self, act, t):
        if self.kind == "gated" or t >= NT:
            return
        k = t % self.SLOTS
        if self.kind == "norm":
            if self.x_arrives:
                if t + X_AHEAD < NT:
                    act.dma_start(self.g.x[:, t + X_AHEAD, :], self.g.x_tile(t + X_AHEAD)).then_inc(self.g.x_loaded[t + X_AHEAD], 16)
                act.wait_ge(self.g.x_loaded[t], 16)
            if t >= self.SLOTS:
                act.wait_ge(self.transposed, 2 * (t - self.SLOTS) + 2)
            act.activation(self.tok[:, k, :], self.g.x[:, t, :], ACT.Square, accum_out=self.ss[:, t:t + 1]).then_inc(self.square_done, 1)
            act.wait_ge(self.mean_done, t + 1)
            act.activation(self.rms[:, t:t + 1], self.ss[:, t:t + 1], ACT.Sqrt).then_inc(self.root_done, 1)
            return
        act.wait_ge(self.a_loaded[k], t // self.SLOTS * 16 + 16)
        if t:
            act.wait_ge(self.mean_done, t)
        act.activation(self.junk[:, :], self.tok[:, k, :], ACT.Square).then_inc(self.square_done, 1)
        act.wait_ge(self.mean_done, t + 1)
        act.activation(self.rms[:, :], self.ss[:, :], ACT.Sqrt).then_inc(self.root_done, 1)

    def high(self, act, t):
        if t >= NT:
            return
        for q in range(2):
            act.wait_ge(self.transposed, 2 * t + q + 1)
            act.activation(self.xth[:, 4 * q:4 * q + 4, t * P:(t + 1) * P],
                           self.psum[q][:, :].rearrange("p (c n) -> p c n", n=P), ACT.Copy).then_inc(self.high_done, 1)
        self.load(act, t + self.SLOTS)
        self.root(act, t + self.SLOTS)

    def make(self, dve, c, t):
        if t >= NT:
            return
        k = t % self.SLOTS
        tile = self.tok[:, k, :]
        if self.kind == "norm":
            dve.wait_ge(self.square_done, t + 1)
            dve.tensor_scalar(self.ss[:, t:t + 1], self.ss[:, t:t + 1], 1.0 / D, EPS, ALU.mult, ALU.add).then_inc(self.mean_done, 1)
            dve.wait_ge(self.root_done, t + 1)
            c.link(dve.reciprocal(self.rms[:, t:t + 1], self.rms[:, t:t + 1]))
            if t == 0:
                dve.wait_ge(self.gain_loaded, 16)
            dve.scalar_tensor_tensor(tile, self.g.x[:, t, :], self.rms[:, t:t + 1], self.gain[:, :],
                                     ALU.mult, ALU.mult).then_inc(self.tile_made, 1)
            return
        if self.kind == "gated":
            dve.wait_ge(self.a_loaded[k], t // self.SLOTS * 16 + 16)
            dve.wait_ge(self.b_loaded[k], t // self.SLOTS * 16 + 16)
            dve.tensor_tensor(tile, tile, self.b_in[:, k, :], ALU.mult).then_inc(self.tile_made, 1)
            return
        if t < self.SLOTS:
            dve.wait_ge(self.gain_loaded, 16)
            dve.wait_ge(self.b_loaded[k], 16)
            c.link(dve.tensor_tensor(self.b_in[:, k, :], self.b_in[:, k, :], self.gain[:, :], ALU.mult))
        dve.wait_ge(self.square_done, t + 1)
        c.link(dve.tensor_reduce(self.ss[:, :], self.junk[:, :].rearrange(self.HV, v=A_V), axis=AX.X, op=ALU.add))
        dve.tensor_scalar(self.ss[:, :], self.ss[:, :], 1.0 / A_V, EPS, ALU.mult, ALU.add).then_inc(self.mean_done, 1)
        dve.wait_ge(self.root_done, t + 1)
        c.link(dve.reciprocal(self.rms[:, :], self.rms[:, :]))
        c.link(dve.tensor_tensor(tile.rearrange(self.HV, v=A_V), tile.rearrange(self.HV, v=A_V), spread(self.rms[:, :], A_V), ALU.mult))
        if t >= self.SLOTS:
            dve.wait_ge(self.b_scaled, t - self.SLOTS + 1)
        dve.tensor_tensor(tile, tile, self.b_in[:, k, :], ALU.mult).then_inc(self.tile_made, 1)

    def low(self, dve, c, t):
        if t >= NT:
            return
        for q in range(2):
            dve.wait_ge(self.high_done, 2 * t + q + 1)
            cs, ts = slice(4 * q, 4 * q + 4), slice(t * P, (t + 1) * P)
            dve.tensor_tensor(self.xtl[:, cs, ts], self.psum[q][:, :].rearrange("p (c n) -> p c n", n=P),
                              f32(self.xth[:, cs, ts]), ALU.subtract).then_inc(self.low_done, 1)
        self.make(dve, c, t + self.SLOTS)

    def start_act(self, act):
        for t in range(self.SLOTS):
            self.load(act, t)
        for t in range(self.SLOTS):
            self.root(act, t)

    def start_dve(self, dve, c):
        for t in range(self.SLOTS):
            self.make(dve, c, t)

    def transpose(self, pe, t):
        if t >= NT:
            return
        pe.wait_ge(self.tile_made, t + 1)
        for q in range(2):
            if t:
                pe.wait_ge(self.low_done, 2 * (t - 1) + q + 1)
            for n in range(4):
                ins = pe.transpose(self.psum[q][:, n * P:(n + 1) * P],
                                   self.tok[:, t % self.SLOTS, (4 * q + n) * P:(4 * q + n + 1) * P], self.g.ident[:, :])
            ins.then_inc(self.transposed, 1)


def linear(nc, g, xth, xtl, tag, w, segments, gates=None, **source):
    BANKS = 3
    wv = w.rearrange("(k p) n -> p k n", p=P)
    QUARTERS = 4
    HK = KC // QUARTERS
    nb = sum(n for _, n, _, _ in segments)
    with Scope(nc, tag) as s:
        raw = s.sb("raw", [P, 2, HK, CB])
        wh, wl = s.sb("wh", [P, 2, KC, CB], fp32r), s.sb("wl", [P, 2, KC, CB], fp32r)
        if segments[0][2] != "residual":
            stage = s.sb("stage", [P, BANKS, CB])
        normed = [m for _, _, m, _ in segments if isinstance(m, tuple)]
        loaded = [s.sem(f"w_loaded{i}") for i in range(2)]
        w_split, high_sem = s.sem("w_split"), s.sem("w_high")
        psum_ready, stage_ready = s.sem("psum_ready"), s.sem("stage_ready")
        psum_used = [s.sem(f"psum_used{i}") for i in range(len(segments))]
        stored = [s.sem(f"stored{i}") for i in range(BANKS)]
        psum = [s.ps(f"y{i}", [P, CB]) for i in range(BANKS)]
        if normed:
            gain_small, gain = s.sb("gain_small", [P, B_HD]), s.sb("gain", [P, B_HD])
            squares, ss, rms = s.sb("squares", [P, CB]), s.sb("ss", [P, A_H]), s.sb("rms", [P, A_H])
            gain_loaded, square_done, mean_done, root_done = s.sem("gain_loaded"), s.sem("square"), s.sem("mean"), s.sem("root")
        chain_sem = s.sem("chain")
        tok = s.brief("tok", [P, Activations.SLOTS, D]) if gates else s.sb("tok", [P, Activations.SLOTS, D])
        if gates:
            gh, gl = s.sb("gh", [P, KC, P], fp32r), s.sb("gl", [P, KC, P], fp32r)
        xt = Activations(nc, g, s, xth, xtl, tok=tok, psum=[s.ps(f"xt{i}", [P, CB]) for i in range(2)], **source)
        if gates:
            g_col, g_n, g_dst = gates
            g_raw = s.sb("g_raw", [P, KC, g_n])
            g_out = stage[0:g_n, :, :].rearrange("p a n -> p (a n)")
            g_loaded, g_split, g_ready, g_copied, g_stored = (s.sem(n) for n in ("g_loaded", "g_split", "g_ready", "g_copied", "g_stored"))
            g_psum = [s.ps(f"g{i}", [P, THIRD]) for i in range(3)]

        def each_segment(engine, body, chain=None, when=lambda m: True):
            b0 = 0
            for n, (col0, blocks, mode, target) in enumerate(segments):
                if when(mode):
                    start = chain.n if chain else 0
                    pairs = blocks // 2
                    run(engine, pairs, lambda i: body(n, i, b0), chain)
                b0 += blocks

        with nc.Block() as block:

            @block.sync
            def _(sp):
                if normed:
                    sp.dma_start(gain_small[:, :], normed[0][1].to_broadcast((P, B_HD))).then_inc(gain_loaded, 16)

                xt.load_gain(sp)

                def load(n, i, b0):
                    for par in range(2):
                        b = b0 + 2 * i + par
                        col = segments[n][0] + (2 * i + par) * CB
                        for h in range(QUARTERS):
                            if h >= 2 or not below(b, 1):
                                wait(sp, w_split, QUARTERS * b + h - 1)
                            sp.dma_start(raw[:, h % 2], wv[:, h * HK:(h + 1) * HK, bass.ds(col, CB)]).then_inc(loaded[h % 2], 16)

                each_segment(sp, load)
                if gates:
                    sp.dma_start(g_raw[:, :, :], wv[:, :, g_col:g_col + g_n]).then_inc(g_loaded, 16)
                    wait(sp, g_copied, 3)
                    sp.dma_start(g_dst, g_out[:, 0:T_ALL]).then_inc(g_stored, 16)
                    wait(sp, g_stored, 16)

            @block.gpsimd
            def _(pool):
                def split(n, i, b0):
                    for par in range(2):
                        b = b0 + 2 * i + par
                        for h in range(QUARTERS):
                            wait(pool, loaded[h % 2], (2 * b + h // 2) * 16 + 16)
                            if not below(b, 2):
                                wait(pool, psum_ready, (b - 1) * NT)
                            ks = slice(h * HK, (h + 1) * HK)
                            round_high(pool, g, wh[:, par, ks], raw[:, h % 2]).then_inc(high_sem, 1)
                            wait(pool, high_sem, QUARTERS * b + h + 1)
                            pool.tensor_tensor(wl[:, par, ks], raw[:, h % 2], f32(wh[:, par, ks]), ALU.subtract).then_inc(w_split, 1)
                            if below(b, 1):
                                xt.scale_gates(pool, h)
                        if below(b, 1):
                            for t in range(QUARTERS, NT):
                                xt.scale_gates(pool, t)

                each_segment(pool, split)
                if gates:
                    wait(pool, g_loaded, 16)
                    wait(pool, xt.transposed, 2 * NT)
                    pool.memset(f32(gh[:, :, :]), 0.0).then_inc(g_split, 1)
                    pool.memset(f32(gl[:, :, :]), 0.0).then_inc(g_split, 1)
                    wait(pool, g_split, 2)
                    pool.tensor_copy(gh[:, :, 0:g_n], g_raw[:, :, :]).then_inc(g_split, 1)
                    wait(pool, g_split, 3)
                    pool.tensor_tensor(gl[:, :, 0:g_n], g_raw[:, :, :], f32(gh[:, :, 0:g_n]), ALU.subtract).then_inc(g_split, 1)

            @block.tensor
            def _(pe):
                def products(n, i, b0):
                    for par in range(2):
                        b = b0 + 2 * i + par
                        for t in range(NT):
                            bank = t % BANKS
                            if below(b, 1):
                                if t == 0:
                                    xt.transpose(pe, 0)
                                    xt.transpose(pe, 1)
                                else:
                                    xt.transpose(pe, t + 1)
                                pe.wait_ge(xt.low_done, 2 * t + 2)
                            if t < BANKS and b0 == 0 and par == 0 and below(i, 1):
                                pass
                            elif t < BANKS and par == 0 and below(i, 1):
                                pe.wait_ge(psum_used[n - 1], NT * segments[n - 1][1] - BANKS + t + 1)
                            else:
                                pe.wait_ge(psum_used[n], (b - b0) * NT + t - BANKS + 1)
                            for k in range(KC):
                                if t == 0 and k % HK == 0:
                                    pe.wait_ge(w_split, QUARTERS * b + k // HK + 1)
                                xs = slice(t * P, (t + 1) * P)
                                pe.matmul(psum[bank][:, :], xth[:, k, xs], wh[:, par, k], start=(k == 0), stop=False)
                                pe.matmul(psum[bank][:, :], xth[:, k, xs], wl[:, par, k], start=False, stop=False)
                                ins = pe.matmul(psum[bank][:, :], xtl[:, k, xs], wh[:, par, k], start=False, stop=(k == KC - 1))
                            ins.then_inc(psum_ready, 1)

                each_segment(pe, products)
                if gates:
                    pe.wait_ge(g_split, 4)
                    for j in range(3):
                        xs = slice(j * THIRD, (j + 1) * THIRD)
                        for k in range(KC):
                            pe.matmul(g_psum[j][:, :], gh[:, k], xth[:, k, xs], start=(k == 0), stop=False)
                            pe.matmul(g_psum[j][:, :], gl[:, k], xth[:, k, xs], start=False, stop=False)
                            ins = pe.matmul(g_psum[j][:, :], gh[:, k], xtl[:, k, xs], start=False, stop=(k == KC - 1))
                        ins.then_inc(g_ready, 1)

            @block.scalar
            def _(act):
                xt.start_act(act)
                xt.high(act, 0)
                xt.high(act, 1)

                def evacuate(n, i, b0):
                    _, _, mode, target = segments[n]
                    for par in range(2):
                        bl = 2 * i + par
                        for t in range(NT):
                            bank = t % BANKS
                            u = (b0 + bl) * NT + t
                            act.wait_ge(psum_ready, u + 1)
                            if isinstance(mode, tuple):
                                if t or not below(bl, 1):
                                    act.wait_ge(mean_done, bl * NT + t)
                                act.activation(squares[:, :], psum[bank][:, :], ACT.Square).then_inc(square_done, 1)
                                act.wait_ge(mean_done, bl * NT + t + 1)
                                act.activation(rms[:, :], ss[:, :], ACT.Sqrt).then_inc(root_done, 1)
                                act.wait_ge(psum_used[n], bl * NT + t + 1)
                            else:
                                if not below(u, BANKS):
                                    act.wait_ge(stored[bank], store_count(b0 + bl, t))
                                act.activation(stage[:, bank, :], psum[bank][:, :],
                                               ACT.Sigmoid if mode == "sigmoid" else ACT.Copy).then_inc(psum_used[n], 1)
                                act.wait_ge(psum_used[n], bl * NT + t + 1)
                            act.dma_start(target(bl, t), stage[:, bank, :]).then_inc(stored[bank], 16)
                            if below(u, NT):
                                xt.high(act, t + 2)

                def store_count(b, t):
                    return (b * (NT // BANKS) + t // BANKS) * 16

                each_segment(act, evacuate, when=lambda m: m != "residual")
                if segments[0][2] == "residual":
                    for t in range(2, NT):
                        xt.high(act, t)
                else:
                    for k in range(BANKS):
                        act.wait_ge(stored[k], nb * (NT // BANKS) * 16)
                if gates:
                    for j in range(3):
                        act.wait_ge(g_ready, j + 1)
                        act.activation(g_out[:, j * THIRD:(j + 1) * THIRD], g_psum[j][0:g_n, :], ACT.Copy).then_inc(g_copied, 1)

            @block.vector
            def _(dve):
                c, xc = Chain(dve, chain_sem), Chain(dve, xt.chain_sem)
                xt.start_dve(dve, xc)
                xt.low(dve, xc, 0)
                xt.low(dve, xc, 1)
                if normed:
                    dve.wait_ge(gain_loaded, 16)
                    c.link(dve.tensor_scalar(gain[:, :], gain_small[:, :], normed[0][2], None, ALU.mult))

                def evacuate(n, i, b0):
                    col0, _, mode, _ = segments[n]
                    for par in range(2):
                        bl = 2 * i + par
                        for t in range(NT):
                            bank = t % BANKS
                            dve.wait_ge(psum_ready, (b0 + bl) * NT + t + 1)
                            if mode == "residual":
                                xs = g.x[:, t, bass.ds(bl * CB, CB)]
                                dve.tensor_tensor(xs, psum[bank][:, :], xs, ALU.add).then_inc(psum_used[n], 1)
                                if below(b0 + bl, 1):
                                    xt.low(dve, xc, t + 2)
                                continue
                            dve.wait_ge(square_done, bl * NT + t + 1)
                            c.link(dve.tensor_reduce(ss[:, :], squares[:, :].rearrange("p (h d) -> p h d", d=B_HD), axis=AX.X, op=ALU.add))
                            dve.tensor_scalar(ss[:, :], ss[:, :], 1.0 / B_HD, EPS, ALU.mult, ALU.add).then_inc(mean_done, 1)
                            dve.wait_ge(root_done, bl * NT + t + 1)
                            c.link(dve.reciprocal(rms[:, :], rms[:, :]))
                            if not (b0 == 0 and t < BANKS and below(bl, 1)):
                                dve.wait_ge(stored[bank], ((b0 + bl) * (NT // BANKS) + t // BANKS) * 16)
                            sv = stage[:, bank, :].rearrange("p (h d) -> p h d", d=B_HD)
                            c.link(dve.tensor_tensor(sv, psum[bank][:, :].rearrange("p (h d) -> p h d", d=B_HD), spread(rms[:, :], B_HD), ALU.mult))
                            dve.tensor_tensor(sv, sv, repeat(gain[:, :], A_H), ALU.mult).then_inc(psum_used[n], 1)
                            if below(b0 + bl, 1):
                                xt.low(dve, xc, t + 2)

                each_segment(dve, evacuate, c, when=lambda m: m == "residual" or isinstance(m, tuple))
                if segments[0][2] == "store":
                    for t in range(2, NT):
                        xt.low(dve, xc, t)


def ffn(nc, g, xth, xtl, tag, w_gu, w_down, gain_row, out=None):
    FW = FG * P
    guv = w_gu.rearrange("(k p) n -> p k n", p=P)
    dv = w_down.rearrange("(f p) n -> p f n", p=P)
    G = FFN_GROUPS
    with Scope(nc, tag) as s:
        raw_a, raw_b = s.sb("raw_a", [P, KC * FW]), s.sb("raw_b", [P, KC, FW])
        raw_gate = raw_a[:, :].rearrange("p (k n) -> p k n", k=KC)
        raw_down = raw_a[:, :].rearrange("p (f n) -> p f n", f=FG)
        gh, gl = s.sb("gate_h", [P, FG, KC, P], fp32r), s.sb("gate_l", [P, FG, KC, P], fp32r)
        uh, ul = s.sb("up_h", [P, FG, KC, P], fp32r), s.sb("up_l", [P, FG, KC, P], fp32r)
        dh, dl = s.sb("down_h", [P, FG, D], fp32r), s.sb("down_l", [P, FG, D], fp32r)
        hid = s.sb("hid", [P, T_ALL])
        tok = s.brief("tok", [P, Activations.SLOTS, D])
        hh, hl = s.sb("hid_h", [P, FG, T_ALL], fp32r), s.sb("hid_l", [P, FG, T_ALL], fp32r)
        names = ("gate_loaded", "up_loaded", "down_loaded", "gate_split", "up_split", "down_split", "split_high",
                 "gate_ready", "up_ready", "silu_done", "prod_done", "hid_high", "hid_low", "down_ready", "added")
        (gate_loaded, up_loaded, down_loaded, gate_split, up_split, down_split, split_high,
         gate_ready, up_ready, silu_done, prod_done, hid_high, hid_low, down_ready, added) = (s.sem(n) for n in names)
        stored, first_loaded = s.sem("stored"), s.sem("first_loaded")
        gp = [s.ps(f"gate{j}", [P, THIRD]) for j in range(3)]
        up = [s.ps(f"up{j}", [P, THIRD]) for j in range(3)]
        yp = [s.ps(f"y{j}", [P, CB]) for j in range(2)]
        thirds = [slice(j * THIRD, (j + 1) * THIRD) for j in range(3)]
        NY = NT * (D // CB)
        xt = Activations(nc, g, s, xth, xtl, "norm", tok, yp, gain_row=gain_row)

        with nc.Block() as block:

            @block.sync
            def _(sp):
                def load(n):
                    first = below(n, 1)
                    if not first:
                        wait(sp, down_split, n)
                    if first:
                        sp.dma_start(raw_gate[:, :, 0:P], guv[:, :, 0:P]).then_inc(first_loaded, 16)
                        xt.load_gain(sp)
                        sp.dma_start(raw_gate[:, :, P:FW], guv[:, :, P:FW]).then_inc(gate_loaded, 16)
                    else:
                        sp.dma_start(raw_gate, guv[:, :, bass.ds(n * FW, FW)]).then_inc(gate_loaded, 16)
                    if not first:
                        wait(sp, up_split, n * FG)
                    sp.dma_start(raw_b[:, :, :], guv[:, :, bass.ds(D_FF + n * FW, FW)]).then_inc(up_loaded, 16)
                    wait(sp, gate_split, n * FG + FG)
                    sp.dma_start(raw_down, dv[:, bass.ds(n * FG, FG), :]).then_inc(down_loaded, 16)

                run(sp, G, load)
                wait(sp, down_loaded, 16 * G)
                if out:
                    for t in range(NT):
                        wait(sp, added, (G - 1) * NY + 2 * t + 2)
                        sp.dma_start(out(t), g.x[:, t, :]).then_inc(stored, 16)
                    wait(sp, stored, 16 * NT)

            @block.gpsimd
            def _(pool):
                def split(n):
                    first = below(n, 1)
                    for f in range(FG):
                        fs = slice(f * P, (f + 1) * P)
                        for part, (raw, h, l, loaded, ready, done) in enumerate((
                                (raw_gate, gh, gl, gate_loaded, gate_ready, gate_split),
                                (raw_b, uh, ul, up_loaded, up_ready, up_split))):
                            if first and part == 0 and f == 0:
                                wait(pool, first_loaded, 16)
                            else:
                                wait(pool, loaded, n * 16 + 16)
                            if not first:
                                wait(pool, ready, ((n - 1) * FG + f) * 3 + 3)
                            round_high(pool, g, h[:, f], raw[:, :, fs]).then_inc(split_high, 1)
                            wait(pool, split_high, n * (2 * FG + 1) + 2 * f + part + 1)
                            pool.tensor_tensor(l[:, f], raw[:, :, fs], f32(h[:, f]), ALU.subtract).then_inc(done, 1)
                    wait(pool, down_loaded, n * 16 + 16)
                    if not first:
                        wait(pool, down_ready, n * NY)
                    round_high(pool, g, dh[:, :, :], raw_down).then_inc(split_high, 1)
                    wait(pool, split_high, n * (2 * FG + 1) + 2 * FG + 1)
                    pool.tensor_tensor(dl[:, :, :], raw_down, f32(dh[:, :, :]), ALU.subtract).then_inc(down_split, 1)

                run(pool, G, split)

            @block.tensor
            def _(pe):
                def hidden(n, f, banks, h, l, split, freed, ready):
                    pe.wait_ge(split, n * FG + f + 1)
                    making = h is gh and f == 0 and below(n, 1)
                    for j in range(3):
                        if making:
                            for t in ((0, 1, 2), (5,), (8,))[j]:
                                xt.transpose(pe, t)
                            pe.wait_ge(xt.low_done, 2 * (3 * j + 3))
                        if f or not below(n, 1):
                            pe.wait_ge(freed, (n * FG + f - 1) * 3 + j + 1)
                        for k in range(KC):
                            if making and k in (2, 5):
                                xt.transpose(pe, 3 * j + 3 + k // 3)
                            pe.matmul(banks[j][:, :], h[:, f, k], xth[:, k, thirds[j]], start=(k == 0), stop=False)
                            pe.matmul(banks[j][:, :], l[:, f, k], xth[:, k, thirds[j]], start=False, stop=False)
                            ins = pe.matmul(banks[j][:, :], h[:, f, k], xtl[:, k, thirds[j]], start=False, stop=(k == KC - 1))
                        ins.then_inc(ready, 1)

                def gate(n, f):
                    hidden(n, f, gp, gh, gl, gate_split, silu_done, gate_ready)

                def upward(n, f):
                    hidden(n, f, up, uh, ul, up_split, prod_done, up_ready)

                def down(n):
                    pe.wait_ge(down_split, n + 1)
                    pe.wait_ge(hid_low, (n + 1) * FG * 3)
                    for t in range(NT):
                        ts = slice(t * P, (t + 1) * P)
                        for c in range(2):
                            cs = slice(c * CB, (c + 1) * CB)
                            if t or not below(n, 1):
                                pe.wait_ge(added, n * NY + 2 * t + c - 1)
                            for f in range(FG):
                                pe.matmul(yp[c][:, :], hh[:, f, ts], dh[:, f, cs], start=(f == 0), stop=False)
                                pe.matmul(yp[c][:, :], hh[:, f, ts], dl[:, f, cs], start=False, stop=False)
                                ins = pe.matmul(yp[c][:, :], hl[:, f, ts], dh[:, f, cs], start=False, stop=(f == FG - 1))
                            ins.then_inc(down_ready, 1)

                def group(n):
                    upward(n, 0)
                    for f in range(1, FG):
                        gate(n, f)
                        upward(n, f)
                    gate(n + 1, 0)
                    down(n)

                gate(0, 0)
                pe.wait_ge(xt.low_done, 2 * NT)
                run(pe, G - 1, group)
                upward(G - 1, 0)
                for f in range(1, FG):
                    gate(G - 1, f)
                    upward(G - 1, f)
                down(G - 1)

            @block.scalar
            def _(act):
                def silu(n, f):
                    for j in range(3):
                        act.wait_ge(gate_ready, (n * FG + f) * 3 + j + 1)
                        if f or not below(n, 1):
                            act.wait_ge(hid_low, (n * FG + f - 1) * 3 + j + 1)
                        act.activation(hid[:, thirds[j]], gp[j][:, :], ACT.Silu).then_inc(silu_done, 1)

                def high(n, f):
                    for j in range(3):
                        act.wait_ge(prod_done, (n * FG + f) * 3 + j + 1)
                        if not below(n, 1):
                            act.wait_ge(down_ready, n * NY)
                        act.activation(hh[:, f, thirds[j]], hid[:, thirds[j]], ACT.Copy).then_inc(hid_high, 1)

                def group(n):
                    high(n, 0)
                    for f in range(1, FG):
                        silu(n, f)
                        high(n, f)
                    silu(n + 1, 0)

                xt.start_act(act)
                for t in range(NT):
                    xt.high(act, t)
                silu(0, 0)
                run(act, G - 1, group)
                high(G - 1, 0)
                for f in range(1, FG):
                    silu(G - 1, f)
                    high(G - 1, f)

            @block.vector
            def _(dve):
                xc = Chain(dve, xt.chain_sem)
                xt.start_dve(dve, xc)
                for t in range(NT):
                    xt.low(dve, xc, t)

                def group(n):
                    for f in range(FG):
                        for j in range(3):
                            dve.wait_ge(up_ready, (n * FG + f) * 3 + j + 1)
                            dve.wait_ge(silu_done, (n * FG + f) * 3 + j + 1)
                            dve.tensor_tensor(hid[:, thirds[j]], up[j][:, :], hid[:, thirds[j]], ALU.mult).then_inc(prod_done, 1)
                        for j in range(3):
                            dve.wait_ge(hid_high, (n * FG + f) * 3 + j + 1)
                            dve.tensor_tensor(hl[:, f, thirds[j]], hid[:, thirds[j]], f32(hh[:, f, thirds[j]]), ALU.subtract).then_inc(hid_low, 1)
                    for t in range(NT):
                        for c in range(2):
                            dve.wait_ge(down_ready, n * NY + 2 * t + c + 1)
                            xs = g.x[:, t, c * CB:(c + 1) * CB]
                            dve.tensor_tensor(xs, yp[c][:, :], xs, ALU.add).then_inc(added, 1)

                run(dve, G, group)


def log_sigmoid_act(act, u, w, ready_exp, exp_done, ready_ln, ln_done):
    act.wait_ge(*ready_exp)
    act.activation(u, u, ACT.Exp, scale=-1.0).then_inc(exp_done, 1)
    act.wait_ge(*ready_ln)
    act.activation(w[1], w[0], ACT.Ln).then_inc(ln_done, 1)


def log_sigmoid_dve(dve, c, z, u, w, lw, abs_done, exp_done, sum_done, ln_done):
    dve.scalar_tensor_tensor(u, z, -1.0, z, ALU.mult, ALU.max).then_inc(abs_done, 1)
    dve.wait_ge(exp_done, 1)
    dve.tensor_scalar(w, u, 1.0, None, ALU.add).then_inc(sum_done, 1)
    dve.wait_ge(sum_done, 1)
    c.link(dve.scalar_tensor_tensor(u, w, 1.0, u, ALU.subtract, ALU.subtract))
    dve.wait_ge(ln_done, 1)
    c.link(dve.reciprocal(w, w))
    c.link(dve.tensor_tensor(u, u, w, ALU.mult))
    c.link(dve.tensor_tensor(lw, lw, u, ALU.subtract))
    c.link(dve.scalar_tensor_tensor(z, z, 0.0, lw, ALU.min, ALU.subtract))


KIND_A, KIND_G, KIND_W, KIND_E = range(4)


def mlstm_gates(nc, g, gates_d, b_i, b_f, state_m, m_prompt, m_sample):
    NG = NP + DEC_BATCH
    with Scope(nc, "mgates") as s:
        li, lf, u, w, lw = (s.sb(n, [A_H, T_ALL]) for n in ("li", "lf", "u", "w", "lw"))
        b, m, reset = s.sb("b", [A_H, T_ALL]), s.sb("m", [A_H, T_ALL]), s.sb("reset", [A_H, T_ALL])
        gg, ws, en, A = s.sb("gg", [A_H, T_ALL]), s.sb("ws", [A_H, T_ALL]), s.sb("en", [A_H, T_ALL]), s.sb("A", [A_H, T_ALL])
        bi, bf, bi15, bf15 = (s.sb(n, [A_H, 1]) for n in ("bi", "bf", "bi15", "bf15"))
        m0, mprev, bend, gend = s.sb("m0", [A_H, DEC_BATCH]), s.sb("mprev", [A_H, NG]), s.sb("bend", [A_H, NG]), s.sb("gend", [A_H, NG])
        diag, gcs = s.sb("diag", [A_H, A_H, DEC_BATCH]), s.sb("gcs", [DEC_BATCH, A_H])
        loaded = s.sem("loaded")
        chain_sem, scaled, tanh_done, abs_done, exp_done, sum_done, ln_done = (s.sem(n) for n in (
            "chain", "scaled", "tanh", "abs", "exp", "sum", "ln"))
        arg_done, exps_done, A_done, filled, made, turned, out_sem, gend_done = (s.sem(n) for n in (
            "arg", "exps", "A", "filled", "made", "turned", "out", "gend"))
        copied = s.sem("copied")
        tp = s.ps("tok", [P, NT, 4, A_H])
        sp_ = s.ps("small", [P, CB])

        def groups(ap):
            return (ap[:, 0:SEQ].rearrange("h (c t) -> h c t", t=P),
                    ap[:, SEQ:T_ALL].rearrange("h (c t) -> h c t", t=DEC_SEQ))

        with nc.Block() as block:

            @block.sync
            def _(sp):
                sp.dma_start(li[:, :], gates_d[0:A_H, :]).then_inc(loaded, 16)
                sp.dma_start(lf[:, :], gates_d[A_H:2 * A_H, :]).then_inc(loaded, 16)
                sp.dma_start(bi[:, :], b_i.rearrange("o h -> h o")).then_inc(loaded, 16)
                sp.dma_start(bf[:, :], b_f.rearrange("o h -> h o")).then_inc(loaded, 16)
                sp.dma_start(m0[:, :], state_m.rearrange("s o h -> h (s o)"), allow_slow_non_contiguous=True).then_inc(loaded, 16)
                wait(sp, gend_done, 1)
                sp.dma_start(m_prompt.rearrange("a o h -> h (a o)"), m[:, SEQ - 1:SEQ]).then_inc(out_sem, 16)
                sp.dma_start(m_sample.rearrange("s o h -> h (s o)"), groups(m)[1][:, :, DEC_SEQ - 1], allow_slow_non_contiguous=True).then_inc(out_sem, 16)
                wait(sp, out_sem, 32)

            @block.gpsimd
            def _(pool):
                pool.memset(g.sel[:, :, :], 0.0).then_inc(filled, 1)
                pool.memset(g.pair_sel[:, :, :, :], 0.0).then_inc(filled, 1)
                pool.memset(g.own[:, :], 1.0).then_inc(filled, 1)
                pool.memset(g.ones8[:, :], 1.0).then_inc(filled, 1)
                pool.memset(reset[:, :], 1.0).then_inc(filled, 1)
                wait(pool, filled, 5)
                pool.affine_select(out=g.sel[:, :, :], in_=g.sel[:, :, :], compare_op=ALU.not_equal, fill=1.0,
                                   base=0, pattern=[[-1, A_H], [0, P]], channel_multiplier=1).then_inc(made, 1)
                pool.affine_select(out=g.pair_sel[:, :, :, :], in_=g.pair_sel[:, :, :, :], compare_op=ALU.not_equal, fill=1.0,
                                   base=0, pattern=[[-2, A_PAIRS], [-1, 2], [0, A_QK]], channel_multiplier=1).then_inc(made, 1)
                pool.affine_select(out=g.own[:, :], in_=g.own[:, :], compare_op=ALU.is_ge, fill=0.0,
                                   base=0, pattern=[[-DEC_SEQ, DEC_BATCH]], channel_multiplier=1).then_inc(made, 1)
                wait(pool, made, 3)
                pool.affine_select(out=g.own[:, :], in_=g.own[:, :], compare_op=ALU.is_ge, fill=0.0,
                                   base=DEC_SEQ - 1, pattern=[[DEC_SEQ, DEC_BATCH]], channel_multiplier=-1).then_inc(made, 1)
                mk = g.mask_dec[:, :, :].rearrange("p e (c t) -> p e c t", t=DEC_SEQ)
                pool.affine_select(out=mk, in_=g.mask_kq[:, :, :].rearrange("p e (c t) -> p e c t", t=DEC_SEQ), compare_op=ALU.is_ge, fill=NEG,
                                   base=0, pattern=[[0, 2], [-DEC_SEQ, DEC_BATCH], [0, DEC_SEQ]], channel_multiplier=1).then_inc(made, 1)
                for view in groups(reset):
                    pool.memset(view[:, :, 0:1], 0.0).then_inc(made, 1)
                wait(pool, made, 7)

            @block.scalar
            def _(act):
                act.wait_ge(scaled, 2)
                act.activation(li[:, :], li[:, :], ACT.Tanh, bias=bi15[:, :], scale=1.0 / CAP).then_inc(tanh_done, 1)
                act.activation(lf[:, :], lf[:, :], ACT.Tanh, bias=bf15[:, :], scale=1.0 / CAP).then_inc(tanh_done, 1)
                log_sigmoid_act(act, u[:, :], (w[:, :], lw[:, :]), (abs_done, 1), exp_done, (sum_done, 1), ln_done)
                act.wait_ge(arg_done, 3)
                act.activation(gg[:, :], gg[:, :], ACT.Exp).then_inc(exps_done, 1)
                act.activation(ws[:, :], ws[:, :], ACT.Exp).then_inc(exps_done, 1)
                act.activation(en[:, :], m[:, :], ACT.Exp, scale=-1.0).then_inc(exps_done, 1)

            @block.vector
            def _(dve):
                c = Chain(dve, chain_sem)
                dve.wait_ge(loaded, 80)
                dve.tensor_scalar(bi15[:, :], bi[:, :], 1.0 / CAP, None, ALU.mult).then_inc(scaled, 1)
                dve.tensor_scalar(bf15[:, :], bf[:, :], 1.0 / CAP, None, ALU.mult).then_inc(scaled, 1)
                dve.wait_ge(tanh_done, 2)
                c.link(dve.tensor_scalar(li[:, :], li[:, :], CAP, None, ALU.mult))
                c.link(dve.tensor_scalar(lf[:, :], lf[:, :], CAP, None, ALU.mult))
                log_sigmoid_dve(dve, c, lf[:, :], u[:, :], w[:, :], lw[:, :], abs_done, exp_done, sum_done, ln_done)
                dve.wait_ge(made, 7)
                c.link(dve.tensor_tensor_scan(b[:, :], reset[:, :], lf[:, :], 0.0, ALU.mult, ALU.add))
                c.link(dve.tensor_tensor_scan(m[:, 0:SEQ], lf[:, 0:SEQ], li[:, 0:SEQ], 0.0, ALU.add, ALU.max))
                for k in range(DEC_BATCH):
                    ks = slice(SEQ + k * DEC_SEQ, SEQ + (k + 1) * DEC_SEQ)
                    c.link(dve.tensor_tensor_scan(m[:, ks], lf[:, ks], li[:, ks], m0[:, k:k + 1], ALU.add, ALU.max))
                c.link(dve.memset(mprev[:, 0:1], 0.0))
                c.link(dve.tensor_copy(mprev[:, 1:NP], groups(m)[0][:, 0:NP - 1, P - 1]))
                c.link(dve.tensor_copy(mprev[:, NP:NG], m0[:, :]))
                c.link(dve.tensor_tensor(g.B[:, :], b[:, :], m[:, :], ALU.subtract))
                dve.tensor_tensor(A[:, :], li[:, :], b[:, :], ALU.subtract).then_inc(A_done, 1)
                dve.wait_ge(A_done, 1)
                for part, (lo, hi, n, last) in enumerate(((0, NP, P, P - 1), (NP, NG, DEC_SEQ, DEC_SEQ - 1))):
                    c.link(dve.tensor_copy(bend[:, lo:hi], groups(g.B)[part][:, :, last]))
                for part, (lo, hi, n, last) in enumerate(((0, NP, P, P - 1), (NP, NG, DEC_SEQ, DEC_SEQ - 1))):
                    c.link(dve.tensor_tensor(groups(gg)[part], groups(g.B)[part], spread(mprev[:, lo:hi], n), ALU.add))
                    dve.tensor_tensor(groups(ws)[part], groups(A)[part], spread(bend[:, lo:hi], n), ALU.add).then_inc(arg_done, 1)
                dve.wait_ge(arg_done, 2)
                dve.sem_inc(arg_done, 1)
                dve.wait_ge(exps_done, 3)
                c.link(dve.tensor_copy(gend[:, 0:NP], groups(gg)[0][:, :, P - 1]))
                c.link(dve.tensor_copy(gend[:, NP:NG], groups(gg)[1][:, :, DEC_SEQ - 1]))
                c.link(dve.tensor_tensor(diag[:, :, :], spread(g.ident[0:A_H, 0:A_H], DEC_BATCH), repeat(gend[:, NP:NG], A_H), ALU.mult))
                dve.sem_inc(gend_done, 1)
                dve.wait_ge(turned, 2)
                dve.tensor_copy(g.tok[:, :, :, :], tp[:, :, :, :]).then_inc(copied, 1)
                dve.tensor_copy(g.gc_pair[:, :, :], sp_[:, 0:A_PAIRS * NP].rearrange("p (j c) -> p j c", j=A_PAIRS)).then_inc(copied, 1)
                dve.tensor_copy(g.gc_dec[:, :, :], sp_[:, 64:128].rearrange("p (h c) -> p h c", h=A_H)).then_inc(copied, 1)
                dve.tensor_copy(g.gc_s[:, :], sp_[0:DEC_BATCH, 128:128 + A_H]).then_inc(copied, 1)

            @block.tensor
            def _(pe):
                pe.wait_ge(A_done, 1)
                pe.wait_ge(exps_done, 3)
                for t in range(NT):
                    for kind, row in ((KIND_A, A), (KIND_G, gg), (KIND_W, ws), (KIND_E, en)):
                        ins = pe.transpose(tp[:, t, kind, :], row[:, t * P:(t + 1) * P], g.ident[0:A_H, 0:A_H])
                ins.then_inc(turned, 1)
                pe.wait_ge(gend_done, 1)
                pe.wait_ge(made, 7)
                for j in range(A_PAIRS):
                    pe.matmul(sp_[:, j * NP:(j + 1) * NP], g.pair_sel[:, j].rearrange("k e d -> k (e d)"), gend[:, 0:NP], start=True, stop=True)
                pe.matmul(sp_[:, 64:128], g.ones8[:, :], diag[:, :, :].rearrange("k h c -> k (h c)"), start=True, stop=True)
                pe.transpose(sp_[0:DEC_BATCH, 128:128 + A_H], gend[:, NP:NG], g.ident[0:A_H, 0:A_H]).then_inc(turned, 1)


def mlstm(nc, g, qkvo, h_d, running, c_out, n_out, state_c=None, state_n=None):
    tag = "mrun" if running else "mprompt"
    N_C = 1 if running else NP
    V1 = A_V + 1
    NPAIR = DEC_BATCH // 2
    with Scope(nc, tag) as s:
        SLOTS = 1 if running else 2
        qk, v1 = s.sb("qk", [P, SLOTS, 2 * A_H * A_QK]), s.sb("v1", [P, SLOTS, A_H, V1])
        qg, k8, wsv = s.sb("qg", [P, SLOTS, A_H * A_QK]), s.sb("k8", [P, SLOTS, A_H * A_QK]), s.sb("wsv", [P, SLOTS, A_H, V1])
        qt, kt, qgt = (s.sb(n, [P, SLOTS, A_PAIRS, P]) for n in ("qt", "kt", "qgt"))
        tokc, gcc = s.sb("tokc", [P, SLOTS, 4, A_H]), s.sb("gcc", [P, SLOTS, A_PAIRS])
        arg, st = s.sb("arg", [P, A_PAIRS, 2, P]), s.sb("st", [P, 2, 2, P])
        num = s.sb("num", [P, SLOTS, A_H, V1])
        den, hout = s.sb("den", [P, A_H]), s.sb("hout", [P, A_H, A_V])
        mask_r = s.sb("mask_r", [P, 2, P], fp32r)
        names = ("ones", "tok_done", "qg_done", "k8_done", "wsv_done", "turned", "t_copied", "bias_ready",
                 "arg_done", "exp_done", "score_ready", "st_done", "num_ready", "num_done",
                 "state_ready", "state_done", "h_done", "stored", "chain", "rounded")
        (ones, tok_done, qg_done, k8_done, wsv_done, turned, t_copied, bias_ready,
         arg_done, exp_done, score_ready, st_done, num_ready, num_done,
         state_ready, state_done, h_done, stored, chain_sem, rounded) = (s.sem(n) for n in names)
        qk_loaded, v_loaded = ([s.sem(f"{n}{i}") for i in range(SLOTS)] for n in ("qk_loaded", "v_loaded"))
        psc, pn = s.ps("scores", [P, 2, CB]), s.ps("num_p", [P, 2, CB])
        pb = [s.ps(f"bias{i}", [P, 2, P]) for i in range(2)]
        pc, pt = s.ps("state", [P, CB]), s.ps("turn", [P, 4, P])
        final_t, final_c, final_s = (s.sem(n) for n in ("final_t", "final_c", "final_s"))
        LINKS = 4
        PARTS = 2 if running else 3
        if running:
            cold, nload, nold, c0t = g.cold, g.nload, g.nold, s.sb("c0t", [P, NPAIR, A_H, V1])
            c_loaded, n_loaded = g.c_loaded, g.n_loaded
            qm, km = s.sb("qm", [P, 2, DEC_BATCH, A_QK]), s.sb("km", [P, 2, DEC_BATCH, A_QK])
            qmt, wsk, ccur = s.sb("qmt", [P, 2, NPAIR, P]), s.sb("wsk", [P, A_H, A_QK]), s.sb("ccur", [P, 2, DEC_BATCH, A_QK])
            c0_turned, c0_copied, qm_done, qm_turned, qm_copied = (s.sem(n) for n in (
                "c0_turned", "c0_copied", "qm_done", "qm_turned", "qm_copied"))
            decayed, km_done, wsk_done, c_ready, c_done, n_ready, n_done = (s.sem(n) for n in (
                "decayed", "km_done", "wsk_done", "c_ready", "c_done", "n_ready", "n_done"))
            mask = g.mask_dec
        else:
            ct = s.sb("ct", [P, A_PAIRS, V1])
            cfin, nfin = s.sb("cfin", [P, A_PAIRS, P]), s.sb("nfin", [A_PAIRS, P])
            mask = g.mask_kq

        def tile(i):
            return NT - 1 if running else i

        def chunks(engine, body, chain=None):
            if running:
                body(0, 0)
            else:
                run(engine, N_C // SLOTS, lambda i: [body(SLOTS * i + slot, slot) for slot in range(SLOTS)],
                    chain, peel_last=True, per=SLOTS * LINKS)

        def exists(i):
            return not isinstance(i, int) or 0 <= i < N_C

        def ahead(i, slot, j, n):
            return (i, slot, j + n) if j + n < A_PAIRS else (i + 1, 1 - slot, j + n - A_PAIRS)

        def loads(i, slot):
            return (i - slot) * 8 + 16 if SLOTS == 2 else 16

        with nc.Block() as block:

            @block.sync
            def _(sp):
                def load(i, slot):
                    t = tile(i)
                    if not below(i, SLOTS):
                        wait(sp, k8_done, i - SLOTS + 1)
                    sp.dma_start(qk[:, slot], qkvo[t, :, 0:A_V0]).then_inc(qk_loaded[slot], 16)
                    if not below(i, SLOTS):
                        wait(sp, num_ready, (i - SLOTS + 1) * A_PAIRS)
                    sp.dma_start(v1[:, slot, :, 0:A_V], qkvo[t, :, A_V0:A_O0].rearrange("t (h v) -> t h v", v=A_V)).then_inc(v_loaded[slot], 16)

                chunks(sp, load)
                if not running:
                    wait(sp, final_c, 5)
                    for j in range(A_PAIRS):
                        sp.dma_start(c_out[0, 0, 2 * j:2 * j + 2].rearrange("h v d -> v h d"),
                                     cfin[:, j, :].rearrange("v (h d) -> v h d", h=2)).then_inc(final_s, 16)
                    sp.dma_start(n_out.rearrange("a b (j h) d -> (a b j) (h d)", j=A_PAIRS), nfin[:, :]).then_inc(final_s, 16)
                    wait(sp, final_s, 16 * (A_PAIRS + 1))
                else:
                    for h in range(A_H):
                        wait(sp, c_done, h + 1)
                        sp.dma_start(c_out[:, 0, h].rearrange("s v d -> v s d"), cold[:, h]).then_inc(final_s, 16)
                    wait(sp, n_done, 1)
                    sp.dma_start(n_out.rearrange("s o h d -> s (o h d)"), nold[:, :]).then_inc(final_s, 16)
                    wait(sp, final_s, 16 * (A_H + 1))

            @block.gpsimd
            def _(pool):
                pool.memset(v1[:, :, :, A_V:V1], 1.0).then_inc(ones, 1)
                if not running:
                    pool.memset(ct[:, :, :], 0.0).then_inc(ones, 1)
                else:
                    pool.sem_inc(ones, 1)

                def weigh(i, slot):
                    wait(pool, qk_loaded[slot], loads(i, slot))
                    wait(pool, tok_done, i + 1)
                    if not below(i, SLOTS):
                        wait(pool, turned, PARTS * (i - SLOTS) + PARTS)
                        wait(pool, state_ready, (i - SLOTS + 1) * A_PAIRS)
                    pool.tensor_tensor(qg[:, slot, :].rearrange("p (h d) -> p h d", d=A_QK), qk[:, slot, 0:A_K0].rearrange("p (h d) -> p h d", d=A_QK),
                                       spread(tokc[:, slot, KIND_G, :], A_QK), ALU.mult).then_inc(qg_done, 1)
                    wait(pool, v_loaded[slot], loads(i, slot))
                    wait(pool, turned, PARTS * i + 2)
                    wait(pool, ones, 2)
                    pool.tensor_tensor(wsv[:, slot], v1[:, slot], spread(tokc[:, slot, KIND_W, :], V1), ALU.mult).then_inc(wsv_done, 1)
                    pool.tensor_scalar(k8[:, slot], qk[:, slot, A_K0:A_V0], A_QK ** -0.5, None, ALU.mult).then_inc(k8_done, 1)

                chunks(pool, weigh)
                if running:
                    wait(pool, k8_done, 1)
                    k8v = k8[:, 0, :].rearrange("p (h d) -> p h d", d=A_QK)
                    pool.tensor_tensor(wsk[:, :, :], k8v, spread(tokc[:, 0, KIND_W, :], A_QK), ALU.mult).then_inc(wsk_done, 1)
                    for h in range(A_H):
                        if h >= 2:
                            wait(pool, c_ready, h - 1)
                        pool.tensor_tensor(km[:, h % 2], repeat(k8v[:, h, :], DEC_BATCH), spread(g.own[:, :], A_QK), ALU.mult).then_inc(km_done, 1)

            @block.tensor
            def _(pe):
                if running:
                    for h in range(A_H):
                        pe.wait_ge(c_loaded, 16 * A_H)
                        if h:
                            pe.wait_ge(c0_copied, h)
                        for j in range(NPAIR):
                            ins = pe.transpose(pt[:, j, :], cold[:, h, 2 * j:2 * j + 2, :].rearrange("v s d -> v (s d)"), g.ident[:, :])
                        ins.then_inc(c0_turned, 1)
                    pe.wait_ge(c0_copied, A_H)
                    pe.wait_ge(n_loaded, 16 * (NPAIR + 1))
                    pe.transpose(pt[:, 0, 0:NPAIR * A_H], nload[:, :], g.ident[0:NPAIR * A_H, 0:NPAIR * A_H]).then_inc(c0_turned, 1)
                    pe.wait_ge(c0_copied, A_H + 1)

                def unit(i, j):
                    return i * A_PAIRS + j

                def turn(i, slot, part):
                    if part < 2:
                        pe.wait_ge(qk_loaded[slot], loads(i, slot))
                    else:
                        pe.wait_ge(qg_done, i + 1)
                    if part or not below(i, 1):
                        pe.wait_ge(t_copied, PARTS * i + part)
                    for n in range(A_PAIRS):
                        src = qk[:, slot, (part * A_PAIRS + n) * P:(part * A_PAIRS + n + 1) * P] if part < 2 else qg[:, slot, n * P:(n + 1) * P]
                        ins = pe.transpose(pt[:, n, :], src, g.ident[:, :])
                    ins.then_inc(turned, 1)

                def bias(i, slot, j):
                    u = unit(i, j)
                    if j >= 2 or not below(i, 1):
                        pe.wait_ge(arg_done, u - 1)
                    cols = bass.ds(tile(i) * P, P)
                    bank = pb[j % 2]
                    pe.matmul(bank[:, :, :], g.ident_r[:, :], mask_r[:, :, :], start=True, stop=False)
                    for e in range(2):
                        pe.matmul(bank[:, e, :], g.sel_r[:, 2 * j + e, :], g.Bh[:, cols], start=False, stop=False)
                        ins = pe.matmul(bank[:, e, :], g.sel_r[:, 2 * j + e, :], g.Bl[:, cols], start=False, stop=(e == 1))
                    ins.then_inc(bias_ready, 1)

                def scores(i, slot, j):
                    u = unit(i, j)
                    if j == 0:
                        pe.wait_ge(t_copied, PARTS * i + 2)
                    if j or not below(i, 1):
                        pe.wait_ge(st_done, u)
                    for e in range(2):
                        es = slice(e * A_QK, (e + 1) * A_QK)
                        ins = pe.matmul(psc[:, e, 0:P], kt[es, slot, j, :], qt[es, slot, j, :], start=True, stop=True)
                    ins.then_inc(score_ready, 1)

                def numerator(i, slot, j):
                    u = unit(i, j)
                    pe.wait_ge(st_done, u + 1)
                    pe.wait_ge(v_loaded[slot], loads(i, slot))
                    pe.wait_ge(ones, 2)
                    if j or not below(i, 1):
                        pe.wait_ge(num_done, u)
                    if running:
                        for e in range(2):
                            h = 2 * j + e
                            pe.wait_ge(qm_done, h + 1)
                            if h >= 1:
                                pe.wait_ge(qm_copied, h)
                            for n in range(NPAIR):
                                ins = pe.transpose(pt[:, n, :], qm[:, e, 2 * n:2 * n + 2, :].rearrange("t s d -> t (s d)"), g.ident[:, :])
                            ins.then_inc(qm_turned, 1)
                            pe.matmul(pn[:, e, 0:V1], st[:, j % 2, e, :], v1[:, slot, h, :], start=True, stop=False)
                            pe.wait_ge(qm_copied, h + 1)
                            for n in range(NPAIR):
                                ins = pe.matmul(pn[:, e, 0:V1], qmt[:, e, n, :], c0t[:, n, h, :], start=False, stop=(n == NPAIR - 1))
                        ins.then_inc(num_ready, 1)
                        return
                    for e in range(2):
                        pe.matmul(pn[:, e, 0:V1], st[:, j % 2, e, :], v1[:, slot, 2 * j + e, :], start=True, stop=False)
                    if not below(i, 1):
                        pe.wait_ge(state_done, u - A_PAIRS + 1)
                    if j == 0:
                        pe.wait_ge(t_copied, PARTS * i + PARTS)
                    for e in range(2):
                        es = slice(e * A_QK, (e + 1) * A_QK)
                        ins = pe.matmul(pn[:, e, 0:V1], qgt[es, slot, j, :], ct[es, j, :], start=False, stop=True)
                    ins.then_inc(num_ready, 1)
                    pe.wait_ge(k8_done, i + 1)
                    pe.wait_ge(wsv_done, i + 1)
                    if j or not below(i, 1):
                        pe.wait_ge(state_done, u)
                    for e in range(2):
                        h = 2 * j + e
                        ins = pe.matmul(pc[e * A_QK:(e + 1) * A_QK, 0:V1], k8[:, slot, h * A_QK:(h + 1) * A_QK], wsv[:, slot, h, :], start=True, stop=True)
                    ins.then_inc(state_ready, 1)

                def chunk(i, slot):
                    for j in range(A_PAIRS):
                        if j and exists(i + 1):
                            turn(i + 1, 1 - slot, j - 1)
                        ni, nslot, nj = ahead(i, slot, j, 2)
                        if exists(ni):
                            bias(ni, nslot, nj)
                        ni, nslot, nj = ahead(i, slot, j, 1)
                        if exists(ni):
                            scores(ni, nslot, nj)
                        numerator(i, slot, j)

                pe.wait_ge(rounded, 1 if running else 5)
                for part in range(PARTS):
                    turn(0, 0, part)
                bias(0, 0, 0)
                bias(0, 0, 1)
                scores(0, 0, 0)
                if running:
                    pe.wait_ge(t_copied, PARTS)
                chunks(pe, chunk)
                if not running:
                    pe.wait_ge(state_done, N_C * A_PAIRS)
                    for j in range(A_PAIRS):
                        ins = pe.transpose(pt[:, j, :], ct[:, j, 0:A_V], g.ident[:, :])
                    ins.then_inc(final_t, 1)
                    pe.wait_ge(final_c, 4)
                    pe.transpose(pt[0:A_PAIRS, 0, :], ct[:, :, A_V:V1].rearrange("p j o -> p (j o)"), g.ident[:, :]).then_inc(final_t, 1)
                else:
                    pe.wait_ge(wsk_done, 1)
                    pe.matmul(pc[0:DEC_BATCH, :], g.own[:, :], wsk[:, :, :].rearrange("p h d -> p (h d)"), start=True, stop=True).then_inc(n_ready, 1)
                    for h in range(A_H):
                        bank = pt[:, :, :].rearrange("p a b -> p (a b)") if h % 2 == 0 else pc[:, :]
                        if h == 1:
                            pe.wait_ge(n_done, 1)
                        if h >= 2:
                            pe.wait_ge(c_done, h - 1)
                        pe.wait_ge(km_done, h + 1)
                        pe.wait_ge(wsv_done, 1)
                        pe.matmul(bank, wsv[:, 0, h, 0:A_V], km[:, h % 2].rearrange("p s d -> p (s d)"), start=True, stop=True).then_inc(c_ready, 1)

            @block.scalar
            def _(act):
                if running:
                    for h in range(A_H):
                        act.wait_ge(c0_turned, h + 1)
                        act.activation(c0t[:, :, h, 0:A_V], pt[:, :, :], ACT.Copy).then_inc(c0_copied, 1)
                    act.wait_ge(c0_turned, A_H + 1)
                    act.activation(c0t[:, :, :, A_V:V1].rearrange("p n h o -> p (n h o)"), pt[:, 0, 0:NPAIR * A_H], ACT.Copy).then_inc(c0_copied, 1)

                def exponent(i, j):
                    act.wait_ge(arg_done, i * A_PAIRS + j + 1)
                    act.activation(arg[:, j], arg[:, j], ACT.Exp).then_inc(exp_done, 1)

                def copy_turned(i, slot, part):
                    dst, scale = ((qt, 1.0), (kt, A_QK ** -0.5), (qgt, 1.0))[part]
                    act.wait_ge(turned, PARTS * i + part + 1)
                    act.activation(dst[:, slot], pt[:, :, :], ACT.Copy, scale=scale).then_inc(t_copied, 1)

                def load_running_states():
                    for j in range(NPAIR):
                        act.dma_start(g.nload[j * A_H:(j + 1) * A_H, :].rearrange("h (s d) -> h s d", s=2),
                                      state_n[2 * j:2 * j + 2, 0].rearrange("s h d -> h s d")).then_inc(g.n_loaded, 16)
                    act.dma_start(g.nold[:, :], state_n.rearrange("s o h d -> s (o h d)")).then_inc(g.n_loaded, 16)
                    for h in range(A_H):
                        act.dma_start(g.cold[:, h], state_c[:, 0, h].rearrange("s v d -> v s d")).then_inc(g.c_loaded, 16)

                def store(i):
                    act.wait_ge(h_done, i + 1)
                    act.dma_start(h_d[tile(i)], hout[:, :, :].rearrange("t h v -> t (h v)")).then_inc(stored, 16)

                def chunk(i, slot):
                    for j in range(A_PAIRS):
                        u = i * A_PAIRS + j
                        if j and exists(i + 1):
                            copy_turned(i + 1, 1 - slot, j - 1)
                        ni, _, nj = ahead(i, slot, j, 2)
                        if exists(ni):
                            exponent(ni, nj)
                        if running:
                            for e in range(2):
                                act.wait_ge(qm_turned, 2 * j + e + 1)
                                act.activation(qmt[:, e], pt[:, :, :], ACT.Copy).then_inc(qm_copied, 1)
                        act.wait_ge(num_ready, u + 1)
                        if j == 0 and not below(i, SLOTS):
                            act.wait_ge(h_done, i - SLOTS + 1)
                        act.activation(num[:, slot, 2 * j:2 * j + 2, :], pn[:, :, 0:V1], ACT.Copy).then_inc(num_done, 1)
                        if j == A_PAIRS - 1 and exists(i - 1):
                            store(i - 1)
                        if j == A_PAIRS - 1 and not running and below(i, 1):
                            load_running_states()

                for part in range(PARTS):
                    copy_turned(0, 0, part)
                exponent(0, 0)
                exponent(0, 1)
                chunks(act, chunk)
                store(N_C - 1)
                act.wait_ge(stored, 16 * N_C)
                if not running:
                    act.wait_ge(final_t, 1)
                    for j in range(A_PAIRS):
                        act.activation(cfin[:, j, :], pt[:, j, :], ACT.Copy).then_inc(final_c, 1)
                    act.wait_ge(final_t, 2)
                    act.activation(nfin[:, :], pt[0:A_PAIRS, 0, :], ACT.Copy).then_inc(final_c, 1)

            @block.vector
            def _(dve):
                c = Chain(dve, chain_sem)
                dve.tensor_copy(mask_r[:, :, :], mask[:, :, :]).then_inc(rounded, 1)
                if not running:
                    dve.tensor_copy(g.ident_r[:, :], g.ident[:, :]).then_inc(rounded, 1)
                    dve.tensor_copy(g.sel_r[:, :, :], g.sel[:, :, :]).then_inc(rounded, 1)
                    dve.tensor_copy(g.Bh[:, :], g.B[:, :]).then_inc(rounded, 1)
                    dve.wait_ge(rounded, 4)
                    dve.tensor_tensor(g.Bl[:, :], g.B[:, :], f32(g.Bh[:, :]), ALU.subtract).then_inc(rounded, 1)

                def token_factors(i, slot):
                    if not below(i, SLOTS):
                        dve.wait_ge(wsv_done, i - SLOTS + 1)
                    if not running:
                        c.link(dve.tensor_copy(gcc[:, slot], g.gc_pair[:, :, i]))
                    dve.tensor_copy(tokc[:, slot], g.tok[:, tile(i)]).then_inc(tok_done, 1)
                    dve.wait_ge(tok_done, i + 1)

                def masked_q(h):
                    dve.tensor_tensor(qm[:, h % 2], repeat(qg[:, 0, h * A_QK:(h + 1) * A_QK], DEC_BATCH), spread(g.own[:, :], A_QK), ALU.mult).then_inc(qm_done, 1)

                def argument(i, slot, j):
                    dve.wait_ge(bias_ready, i * A_PAIRS + j + 1)
                    dve.tensor_tensor(arg[:, j], pb[j % 2][:, :, :], spread(tokc[:, slot, KIND_A, 2 * j:2 * j + 2], P), ALU.add).then_inc(arg_done, 1)

                def weighted_scores(i, slot, j):
                    u = i * A_PAIRS + j
                    dve.wait_ge(exp_done, u + 1)
                    dve.wait_ge(score_ready, u + 1)
                    if j >= 2 or not below(i, 1):
                        dve.wait_ge(num_ready, u - 1)
                    dve.tensor_tensor(st[:, j % 2], psc[:, :, 0:P], arg[:, j], ALU.mult).then_inc(st_done, 1)

                def finish(i, slot):
                    dve.wait_ge(num_done, i * A_PAIRS + A_PAIRS)
                    c.link(dve.scalar_tensor_tensor(den[:, :], num[:, slot, :, A_V], -1.0, num[:, slot, :, A_V], ALU.mult, ALU.max))
                    c.link(dve.tensor_tensor(den[:, :], den[:, :], tokc[:, slot, KIND_E, :], ALU.max))
                    c.link(dve.reciprocal(den[:, :], den[:, :]))
                    if not below(i, 1):
                        dve.wait_ge(stored, 16 * i)
                    dve.tensor_tensor(hout[:, :, :], num[:, slot, :, 0:A_V], spread(den[:, :], A_V), ALU.mult).then_inc(h_done, 1)

                def chunk(i, slot):
                    for j in range(A_PAIRS):
                        u = i * A_PAIRS + j
                        if j == 1:
                            if exists(i - 1):
                                finish(i - 1, 1 - slot)
                            if exists(i + 1):
                                token_factors(i + 1, 1 - slot)
                        ni, nslot, nj = ahead(i, slot, j, 2)
                        if exists(ni):
                            argument(ni, nslot, nj)
                        ni, nslot, nj = ahead(i, slot, j, 1)
                        if exists(ni):
                            weighted_scores(ni, nslot, nj)
                        if running and j + 1 < A_PAIRS:
                            for e in range(2):
                                h = 2 * j + 2 + e
                                dve.wait_ge(qm_turned, h - 1)
                                masked_q(h)
                        if not running:
                            dve.wait_ge(state_ready, u + 1)
                            dve.wait_ge(ones, 2)
                            dve.scalar_tensor_tensor(ct[:, j, :], ct[:, j, :], gcc[:, slot, j:j + 1], pc[:, 0:V1], ALU.mult, ALU.add).then_inc(state_done, 1)

                token_factors(0, 0)
                if running:
                    dve.wait_ge(qg_done, 1)
                    masked_q(0)
                    masked_q(1)
                argument(0, 0, 0)
                argument(0, 0, 1)
                weighted_scores(0, 0, 0)
                if running:
                    chunk(0, 0)
                else:
                    chunks(dve, chunk, c)
                finish(N_C - 1, (N_C - 1) % SLOTS)
                if running:
                    dve.wait_ge(n_loaded, 16 * (NPAIR + 1))
                    nv = nold[:, :].rearrange("s (h d) -> s h d", h=A_H)
                    c.link(dve.tensor_tensor(nv, nv, spread(g.gc_s[:, :], A_QK), ALU.mult))
                    dve.wait_ge(n_ready, 1)
                    dve.tensor_tensor(nold[:, :], pc[0:DEC_BATCH, :], nold[:, :], ALU.add).then_inc(n_done, 1)
                    dve.wait_ge(c0_turned, A_H + 1)
                    for h in range(A_H):
                        bank = pt[:, :, :].rearrange("p a b -> p (a b)") if h % 2 == 0 else pc[:, :]
                        c.link(dve.tensor_tensor(cold[:, h], cold[:, h], spread(g.gc_dec[:, h, :], A_QK), ALU.mult))
                        dve.wait_ge(c_ready, h + 1)
                        cv = cold[:, h].rearrange("v s d -> v (s d)")
                        dve.tensor_tensor(cv, bank, cv, ALU.add).then_inc(c_done, 1)


def fox_gates(nc, g, gates_d, b_f, cache_logf, logf_prompt, logf_sample, ncp_d, ncd_d):
    with Scope(nc, "fgates") as s:
        lf, u, w, lw, ones = (s.sb(n, [B_H, T_ALL]) for n in ("lf", "u", "w", "lw", "ones"))
        bias, cached = s.sb("bias", [B_H, 1]), s.sb("cached", [P, DEC_BATCH, PAST_T, B_H])
        lall, ncd, ncp = s.sb("lall", [B_H, DEC_BATCH, DK]), g.ncd, s.sb("ncp", [B_H, SEQ])
        out, wide = g.logf_out, s.sb("wide", [P, DEC_BATCH, DEC_SEQ])
        loaded, filled, made, own_made, abs_done, exp_done, sum_done, ln_done, lf_done, out_turned, out_copied, turned, copied, cum_done, stored, chain_sem, wide_made = (
            s.sem(n) for n in ("loaded", "filled", "made", "own_made", "abs", "exp", "sum", "ln", "lf_done", "out_turned", "out_copied",
                               "turned", "copied", "cum_done", "stored", "chain", "wide"))
        banks = [s.ps(f"turn{i}", [P, CB]) for i in range(2)]
        outp = s.ps("outp", [P, NT, B_H])
        with nc.Block() as block:

            @block.sync
            def _(sp):
                sp.dma_start(lf[:, :], gates_d).then_inc(loaded, 16)
                sp.dma_start(bias[:, :], b_f.rearrange("(h o) -> h o", o=1)).then_inc(loaded, 16)
                for k in range(DEC_BATCH):
                    sp.dma_start(cached[:, k], cache_logf[k].rearrange("(t p) h -> p t h", p=P)).then_inc(loaded, 16)
                sp.wait_ge(cum_done, 1)
                sp.dma_start(ncp_d, ncp[:, :]).then_inc(stored, 16)
                sp.wait_ge(out_copied, 1)
                sp.dma_start(logf_prompt[0].rearrange("(t p) h -> p t h", p=P), out[:, 0:NP, :]).then_inc(g.late_stored, 16)
                sp.dma_start(logf_sample.rearrange("s t h -> (s t) h"), out[:, NP, :]).then_inc(g.late_stored, 16)
                for k in range(DEC_BATCH):
                    sp.wait_ge(cum_done, 2 + k)
                    sp.dma_start(ncd_d[k], ncd[:, k:k + 1, :].to_broadcast((B_H, DEC_SEQ, DK))).then_inc(g.late_stored, 16)
                sp.wait_ge(stored, 16)

            @block.gpsimd
            def _(pool):
                pool.memset(ones[:, :], 1.0).then_inc(filled, 1)
                pool.memset(g.own[:, :], 1.0).then_inc(filled, 1)
                pool.memset(wide[:, :, :], 0.0).then_inc(filled, 1)
                pool.wait_ge(filled, 3)
                pool.affine_select(out=g.own[:, :], in_=g.own[:, :], compare_op=ALU.is_ge, fill=0.0,
                                   base=0, pattern=[[-DEC_SEQ, DEC_BATCH]], channel_multiplier=1).then_inc(own_made, 1)
                pool.wait_ge(own_made, 1)
                pool.affine_select(out=g.own[:, :], in_=g.own[:, :], compare_op=ALU.is_ge, fill=0.0,
                                   base=DEC_SEQ - 1, pattern=[[DEC_SEQ, DEC_BATCH]], channel_multiplier=-1).then_inc(own_made, 1)
                pool.affine_select(out=wide[:, :, :], in_=wide[:, :, :], compare_op=ALU.is_ge, fill=NEG,
                                   base=0, pattern=[[-DEC_SEQ, DEC_BATCH], [-1, DEC_SEQ]], channel_multiplier=1).then_inc(made, 1)

            @block.scalar
            def _(act):
                log_sigmoid_act(act, u[:, :], (w[:, :], lw[:, :]), (abs_done, 1), exp_done, (sum_done, 1), ln_done)
                for k in range(DEC_BATCH):
                    act.wait_ge(turned, k + 1)
                    act.activation(lall[:, k, 0:PAST], banks[k % 2][0:B_H, :], ACT.Copy).then_inc(copied, 1)

            @block.vector
            def _(dve):
                c = Chain(dve, chain_sem)
                dve.wait_ge(loaded, 16 * (2 + DEC_BATCH))
                c.link(dve.tensor_scalar(lf[:, :], lf[:, :], bias[:, :], None, ALU.add))
                log_sigmoid_dve(dve, c, lf[:, :], u[:, :], w[:, :], lw[:, :], abs_done, exp_done, sum_done, ln_done)
                dve.sem_inc(lf_done, 1)
                dve.wait_ge(filled, 3)
                dve.tensor_tensor_scan(ncp[:, :], ones[:, 0:SEQ], lf[:, 0:SEQ], 0.0, ALU.mult, ALU.subtract).then_inc(cum_done, 1)
                c.link(dve.tensor_copy(lall[:, :, PAST:DK], lf[:, SEQ:T_ALL].rearrange("h (s t) -> h s t", t=DEC_SEQ)))
                for k in range(DEC_BATCH):
                    dve.wait_ge(copied, k + 1)
                    dve.tensor_tensor_scan(ncd[:, k, :], ones[:, 0:DK], lall[:, k, :], 0.0, ALU.mult, ALU.subtract).then_inc(cum_done, 1)
                dve.wait_ge(out_turned, 1)
                dve.tensor_copy(out[:, :, :], outp[:, :, :]).then_inc(out_copied, 1)
                dve.wait_ge(own_made, 2)
                dve.wait_ge(made, 1)
                c.link(dve.tensor_reduce(g.parity[:, :], g.own[:, :].rearrange("p (c e) -> p e c", e=2), axis=AX.X, op=ALU.add))
                c.link(dve.tensor_tensor(wide[:, :, :], wide[:, :, :], spread(g.own[:, :], DEC_SEQ), ALU.mult))
                c.link(dve.tensor_reduce(g.mask_new[:, :], wide[:, :, :].rearrange("p c k -> p k c"), axis=AX.X, op=ALU.add))

            @block.tensor
            def _(pe):
                pe.wait_ge(loaded, 16 * (2 + DEC_BATCH))
                for k in range(DEC_BATCH):
                    if k >= 2:
                        pe.wait_ge(copied, k - 1)
                    for t in range(PAST_T):
                        ins = pe.transpose(banks[k % 2][0:B_H, t * P:(t + 1) * P], cached[:, k, t, :], g.ident[:, :])
                    ins.then_inc(turned, 1)
                pe.wait_ge(lf_done, 1)
                for t in range(NT):
                    ins = pe.transpose(outp[:, t, :], lf[:, t * P:(t + 1) * P], g.ident[0:B_H, 0:B_H])
                ins.then_inc(out_turned, 1)


def fox_prompt(nc, g, q_d, k_prompt, v_prompt, ncp_d, o_d, cache_k):
    UNITS = 2 * NP
    CPP = P
    SLOTS = 2
    AHEAD, PROBS = 2, 4
    kv = k_prompt.rearrange("(t p) d -> p t d", p=P)
    vv = v_prompt.rearrange("(t p) d -> p t d", p=P)
    qv = q_d[0:NP].rearrange("t p d -> p t d")
    ov = o_d[0:NP].rearrange("t p d -> p t d")

    IN = [(part, e, h) for part in range(2) for e in range(2) for h in range(NP // 4)]
    FIRST_IN = 6

    def layout(with_incoming):
        at, freed_at, incoming, groups = 0, [0, 0], {}, {}
        bank = 0
        for u in range(UNITS):
            if with_incoming and FIRST_IN <= u < FIRST_IN + len(IN):
                at, freed_at[0] = at + 1, freed_at[0] + 1
                incoming[u] = (IN[u - FIRST_IN], at, freed_at[0])
                bank = 0
            groups[u] = []
            for a in range(0, u // 2 + 1, 4):
                bank = 1 - bank
                at, freed_at[bank] = at + 1, freed_at[bank] + 1
                groups[u].append((bank, range(a, min(a + 4, u // 2 + 1)), at, freed_at[bank]))
        return groups, incoming, at, freed_at

    every, incoming, PER_PAIR, FREED = layout(True)
    final = layout(False)[0]
    last_in, last_in_freed = incoming[FIRST_IN + len(IN) - 1][1:]

    def groups(j, u):
        return (final if not exists(j + 1) else every)[u]

    def exists(j):
        return not isinstance(j, int) or 0 <= j < B_PAIRS

    def turned_count(j, n):
        return len(IN) + j * PER_PAIR + n

    def freed_count(j, bank, n):
        return (len(IN) if bank == 0 else 0) + j * FREED[bank] + n

    with Scope(nc, "fprompt") as s:
        kq = s.sb("kq", [P, 2, NP, CPP])
        twice = s.sb("twice", [P, 2, NP * 2, 2, B_HD])
        v, ncum = s.sb("v", [P, SLOTS, NP, CPP]), s.sb("ncum", [P, SLOTS, 2, SEQ])
        kk, kl = s.sb("kk", [P, SLOTS, 2, SEQ], fp32r), s.sb("kl", [P, SLOTS, 2, SEQ], fp32r)
        qq = s.sb("qq", [P, SLOTS, 2, SEQ], fp32r)
        ident_r, mask_r = s.sb("ident_r", [P, P], fp32r), s.sb("mask_r", [P, P], fp32r)
        prob, pt = s.sb("prob", [P, PROBS, SEQ]), s.sb("pt", [P, 2, NP, P])
        mx, rs, rinv = s.sb("mx", [P, PROBS]), s.sb("rs", [P, PROBS]), s.sb("rinv", [P, 2])
        o = s.sb("o", [P, SLOTS, NP, CPP])
        (k_loaded, q_loaded, turned, in_high, scores_ready, shifted, max_done, exp_done, pv_ready, o_done, chain_sem, made) = (
            s.sem(n) for n in ("k_loaded", "q_loaded", "turned", "in_high", "scores_ready", "shifted", "max_done",
                               "exp_done", "pv_ready", "o_done", "chain", "made"))
        doubled = s.sem("doubled")
        freed = [s.sem("freed_by_dve"), s.sem("freed_by_act")]
        nc_loaded, v_loaded, stored = ([s.sem(f"{n}{i}") for i in range(SLOTS)] for n in ("nc_loaded", "v_loaded", "stored"))
        settled = s.sem("settled")
        ps = [s.ps(f"scores{e}", [P, SEQ]) for e in range(2)]
        tb = [s.ps(f"turn{i}", [P, 4, P]) for i in range(2)]
        po = [s.ps(f"o_psum{e}", [P, B_HD]) for e in range(2)]

        def pairs(engine, body, chain=None):
            run(engine, B_PAIRS // SLOTS, lambda i: [body(SLOTS * i + slot, slot) for slot in range(SLOTS)],
                chain, peel_last=True, per=SLOTS * UNITS)

        def ahead(j, slot, u):
            return (j, slot, u + AHEAD) if u + AHEAD < UNITS else (j + 1, 1 - slot, u + AHEAD - UNITS)

        def before(j, slot, u):
            return (j, slot, u - 1) if u else (j - 1, 1 - slot, UNITS - 1)

        def copy_probs(engine, copy, bank, j, u):
            for b, tiles, n, _ in groups(j, u):
                if b != bank:
                    continue
                engine.wait_ge(turned, turned_count(j, n))
                if u >= 2 or not below(j, 1):
                    engine.wait_ge(pv_ready, j * UNITS + u - 1)
                copy(pt[:, u % 2, tiles[0]:tiles[-1] + 1, :], tb[bank][:, 0:len(tiles), :]).then_inc(freed[bank], 1)

        with nc.Block() as block:

            @block.sync
            def _(sp):
                def load_kq(j):
                    cols = bass.ds(j * CPP, CPP)
                    sp.dma_start(kq[:, 0], kv[:, :, cols]).then_inc(k_loaded, 16)
                    sp.dma_start(kq[:, 1], qv[:, :, cols]).then_inc(q_loaded, 16)

                def load(j, slot):
                    cols = bass.ds(j * CPP, CPP)
                    if exists(j + 1):
                        wait(sp, doubled, 4 * j + 4)
                        load_kq(j + 1)
                    if not below(j, SLOTS):
                        wait(sp, shifted, (j - 1) * UNITS)
                    for e in range(2):
                        sp.dma_start(ncum[:, slot, e, :], ncp_d[bass.ds(2 * j + e, 1), :].to_broadcast((P, SEQ))).then_inc(nc_loaded[slot], 16)
                    if not below(j, SLOTS):
                        wait(sp, pv_ready, (j - 1) * UNITS)
                    sp.dma_start(v[:, slot], vv[:, :, cols]).then_inc(v_loaded[slot], 16)

                load_kq(0)
                pairs(sp, load)
                for slot in range(SLOTS):
                    sp.wait_ge(v_loaded[slot], 16 * (B_PAIRS // SLOTS))

            @block.gpsimd
            def _(pool):
                def double(j):
                    if not below(j, 1):
                        wait(pool, turned, len(IN) if below(j, 2) else turned_count(j - 2, last_in))
                    for part in range(2):
                        wait(pool, (k_loaded, q_loaded)[part], j * 16 + 16)
                        src = kq[:, part].rearrange("p t (e d) -> p (t e) d", d=B_HD)
                        for r in range(2):
                            pool.tensor_tensor(twice[:, part, :, r, :], src, g.one[:, :].rearrange("p (a b) -> p a b", a=1).to_broadcast(src.shape),
                                               ALU.mult).then_inc(doubled, 1)

                def store(j, slot):
                    if exists(j + 1):
                        double(j + 1)
                    wait(pool, o_done, j * UNITS + UNITS)
                    pool.dma_start(ov[:, :, bass.ds(j * CPP, CPP)], o[:, slot]).then_inc(stored[slot], 16)

                double(0)
                pairs(pool, store)
                for slot in range(SLOTS):
                    pool.wait_ge(stored[slot], 16 * (B_PAIRS // SLOTS))

            @block.tensor
            def _(pe):
                def turn_in(j, slot, item, bank_count):
                    part, e, h = item
                    pe.wait_ge(doubled, 4 * j + 2 * part + 2)
                    if bank_count is not None:
                        pe.wait_ge(freed[0], bank_count)
                    for m in range(4):
                        both = twice[:, part, 2 * (4 * h + m) + e].rearrange("p r d -> p (r d)")
                        ins = pe.transpose(tb[0][:, m, :], both, g.ident[:, :])
                    ins.then_inc(turned, 1)

                def scores(j, slot, u):
                    i, e = u // 2, u % 2
                    if u >= 2 or not below(j, 1):
                        pe.wait_ge(shifted, j * UNITS + u - 1)
                    if u == 0:
                        pe.wait_ge(freed[0], len(IN) if below(j, 1) else freed_count(j - 1, 0, last_in_freed))
                    qs, width = slice(i * P, (i + 1) * P), (i + 1) * P
                    for a in range(0, width, CB):
                        b = min(a + CB, width)
                        pe.matmul(ps[e][:, a:b], qq[:, slot, e, qs], kk[:, slot, e, a:b], start=True, stop=False)
                        pe.matmul(ps[e][:, a:b], qq[0:B_HD, slot, e, qs], kl[0:B_HD, slot, e, a:b], start=False, stop=(b < width))
                    pe.matmul(ps[e][:, width - P:width], ident_r[:, :], mask_r[:, :], start=False, stop=True).then_inc(scores_ready, 1)

                def turn(j, u):
                    pe.wait_ge(exp_done, j * UNITS + u + 1)
                    for bank, tiles, n, freed_n in groups(j, u):
                        if freed_n > 1 or bank == 0 or not below(j, 1):
                            pe.wait_ge(freed[bank], freed_count(j, bank, freed_n - 1))
                        for m, t in enumerate(tiles):
                            ins = pe.transpose(tb[bank][:, m, :], prob[:, u % PROBS, t * P:(t + 1) * P], g.ident[:, :])
                        ins.then_inc(turned, 1)

                def weigh(j, slot, u):
                    i, e = u // 2, u % 2
                    for bank, tiles, n, freed_n in groups(j, u):
                        pe.wait_ge(freed[bank], freed_count(j, bank, freed_n))
                    if u >= 2 or not below(j, 1):
                        pe.wait_ge(o_done, j * UNITS + u - 1)
                    if u == 0:
                        pe.wait_ge(v_loaded[slot], (j - slot) * 8 + 16)
                    for t in range(i + 1):
                        ins = pe.matmul(po[e][:, :], pt[:, u % 2, t, :], v[:, slot, t, e * B_HD:(e + 1) * B_HD], start=(t == 0), stop=(t == i))
                    ins.then_inc(pv_ready, 1)

                def pair(j, slot):
                    for u in range(UNITS):
                        if u in incoming and exists(j + 1):
                            item, n, freed_n = incoming[u]
                            turn_in(j + 1, 1 - slot, item, freed_count(j, 0, freed_n - 1))
                        nj, nslot, nu = ahead(j, slot, u)
                        if exists(nj):
                            scores(nj, nslot, nu)
                        turn(j, u)
                        bj, bslot, bu = before(j, slot, u)
                        if exists(bj):
                            weigh(bj, bslot, bu)

                pe.wait_ge(made, 2)
                for n, item in enumerate(IN):
                    turn_in(0, 0, item, n if n else None)
                for u in range(AHEAD):
                    scores(0, 0, u)
                pairs(pe, pair)
                weigh(B_PAIRS - 1, SLOTS - 1, UNITS - 1)

            @block.vector
            def _(dve):
                c = Chain(dve, chain_sem)

                def low_in(j, slot, item, n):
                    part, e, h = item
                    cols = slice(h * CB, (h + 1) * CB)
                    dve.wait_ge(in_high, n)
                    rows, high, low = ((slice(0, B_HD), kk, kl), (slice(B_HD, P), qq, qq))[part]
                    dve.tensor_tensor(low[rows, slot, e, cols], tb[0][rows, :, :].rearrange("p t n -> p (t n)"),
                                      f32(high[rows, slot, e, cols]), ALU.subtract).then_inc(freed[0], 1)

                def shift(j, slot, u):
                    e, width, k = u % 2, (u // 2 + 1) * P, u % PROBS
                    dve.wait_ge(scores_ready, j * UNITS + u + 1)
                    if u == 0:
                        dve.wait_ge(nc_loaded[slot], (j - slot) * 16 + 32)
                    if u >= PROBS or not below(j, 1):
                        fu, fj = (u - PROBS, j) if u >= PROBS else (u - PROBS + UNITS, j - 1)
                        dve.wait_ge(turned, turned_count(fj, groups(fj, fu)[-1][2]))
                    settle(dve, settled)
                    dve.tensor_tensor_reduce(out=prob[:, k, 0:width], in0=ps[e][:, 0:width], in1=ncum[:, slot, e, 0:width], scale=1.0, scalar=-3e38,
                                             op0=ALU.add, op1=ALU.max, accum_out=mx[:, k:k + 1]).then_inc(shifted, 1)
                    dve.wait_ge(shifted, j * UNITS + u + 1)
                    dve.tensor_scalar(mx[:, k:k + 1], mx[:, k:k + 1], -1.0, None, ALU.mult).then_inc(max_done, 1)

                def invert_sum(u):
                    c.mark(dve.reciprocal(rinv[:, u % 2:u % 2 + 1], rs[:, u % PROBS:u % PROBS + 1]))

                def scale_out(j, slot, u):
                    i, e = u // 2, u % 2
                    c.join()
                    dve.wait_ge(pv_ready, j * UNITS + u + 1)
                    if u == 0 and not below(j, SLOTS):
                        dve.wait_ge(stored[slot], (j - slot) * 8)
                    dve.tensor_scalar(o[:, slot, i, e * B_HD:(e + 1) * B_HD], po[e][:, :], rinv[:, e:e + 1], None, ALU.mult).then_inc(o_done, 1)

                def pair(j, slot):
                    for u in range(UNITS):
                        if u in incoming and exists(j + 1):
                            low_in(j + 1, 1 - slot, incoming[u][0], (j + 1) * len(IN) + u - FIRST_IN + 1)
                        nj, nslot, nu = ahead(j, slot, u)
                        if exists(nj):
                            shift(nj, nslot, nu)
                        bj, bslot, bu = before(j, slot, u)
                        if exists(bj):
                            invert_sum(bu)
                        copy_probs(dve, dve.tensor_copy, 0, j, u)
                        if exists(bj):
                            scale_out(bj, bslot, bu)

                dve.tensor_copy(ident_r[:, :], g.ident[:, :]).then_inc(made, 1)
                dve.tensor_copy(mask_r[:, :], g.mask_qk[:, :]).then_inc(made, 1)
                for n, item in enumerate(IN):
                    low_in(0, 0, item, n + 1)
                for u in range(AHEAD):
                    shift(0, 0, u)
                pairs(dve, pair, c)
                invert_sum(UNITS - 1)
                scale_out(B_PAIRS - 1, SLOTS - 1, UNITS - 1)

            @block.scalar
            def _(act):
                def high_in(j, slot, item, count):
                    part, e, h = item
                    act.wait_ge(turned, count)
                    act.activation((kk, qq)[part][:, slot, e, h * CB:(h + 1) * CB], tb[0][:, :, :].rearrange("p t n -> p (t n)"),
                                   ACT.Copy).then_inc(in_high, 1)

                def exponential(j, u):
                    k, width = u % PROBS, (u // 2 + 1) * P
                    act.wait_ge(max_done, j * UNITS + u + 1)
                    if u >= PROBS or not below(j, 1):
                        act.wait_ge(o_done, j * UNITS + u - PROBS + 1)
                    act.activation(prob[:, k, 0:width], prob[:, k, 0:width], ACT.Exp, bias=mx[:, k:k + 1],
                                   accum_out=rs[:, k:k + 1]).then_inc(exp_done, 1)

                def copy(out, in_):
                    return act.activation(out, in_, ACT.Copy)

                def pair(j, slot):
                    for u in range(UNITS):
                        if u in incoming and exists(j + 1):
                            item, n, _ = incoming[u]
                            high_in(j + 1, 1 - slot, item, turned_count(j, n))
                        copy_probs(act, copy, 1, j, u)
                        nj, _, nu = ahead(j, slot, u)
                        if exists(nj):
                            exponential(nj, nu)
                        if below(j, 1) and u == UNITS // 2:
                            act.dma_start(g.run_k[:, :, :], cache_k[0].rearrange("(t p) h d -> p t (h d)", p=P)).then_inc(g.run_k_loaded, 16)

                for n, item in enumerate(IN):
                    high_in(0, 0, item, n + 1)
                for u in range(AHEAD):
                    exponential(0, u)
                pairs(act, pair)


def fox_running(nc, g, q_d, cache_k, cache_v, k_sample, v_sample, ncd_d, half_d, o_d):
    HALVES = 2
    JH = B_PAIRS // HALVES
    NS = DEC_SEQ
    SLOTS = 2
    kc = cache_k.rearrange("s (t p) h d -> s p t (h d)", p=P)
    vc = cache_v.rearrange("s (t p) h d -> s p t (h d)", p=P)
    kn_d, vn_d = k_sample.rearrange("s t h d -> s t (h d)"), v_sample.rearrange("s t h d -> s t (h d)")
    qn_d = q_d[NT - 1].rearrange("(s t) d -> s t d", t=NS)
    with Scope(nc, "frun") as s:
        k, small = g.run_k, s.sb("small", [NS, 2, D])
        v, vn, ncum = s.sb("v", [P, SLOTS, PAST_T, D]), s.sb("vn", [NS, SLOTS, D]), s.sb("ncum", [P, SLOTS, HALVES, DK])
        kt, ktn, qb = s.sb("kt", [P, SLOTS, B_PAIRS, PAST]), s.sb("ktn", [P, B_PAIRS, NS]), s.sb("qb", [P, B_PAIRS, 2 * NS])
        prob, pt, ptn = s.sb("prob", [P, HALVES, DK]), s.sb("pt", [P, HALVES, PAST_T, P]), s.sb("ptn", [NS, HALVES, P])
        mx, rs, rinv, sel = s.sb("mx", [P, 2]), s.sb("rs", [P, 2]), s.sb("rinv", [P, 2]), s.sb("sel", [P, 2, 2])
        o = s.sb("o", [P, HALVES, B_HD])
        names = ("k_loaded", "kn_loaded", "qn_loaded", "turned", "copied", "small_turned", "kn_copied", "qn_copied", "filled", "scores_ready",
                 "shifted", "max_done", "exp_done", "p_turned", "p_copied", "pv_ready", "o_done", "chain", "moved")
        (k_loaded, kn_loaded, qn_loaded, turned, copied, small_turned, kn_copied, qn_copied, filled, scores_ready,
         shifted, max_done, exp_done, p_turned, p_copied, pv_ready, o_done, chain_sem, moved) = (s.sem(n) for n in names)
        v_loaded, vn_loaded, nc_loaded = ([s.sem(f"{n}{i}") for i in range(SLOTS)] for n in ("v_loaded", "vn_loaded", "nc_loaded"))
        stored = [s.sem(f"stored{i}") for i in range(HALVES)]
        settled, pe_settled = s.sem("settled"), s.sem("pe_settled")
        ps = s.ps("scores", [P, 2 * CB])
        tb = [s.ps(f"turn{i}", [P, 4, P]) for i in range(2)]
        tp = [s.ps(f"pturn{i}", [P, 4, P]) for i in range(2)]
        small_p, po = s.ps("small_p", [P, CB]), s.ps("o_psum", [P, P])

        def streams(engine, body, chain=None):
            run(engine, DEC_BATCH // SLOTS, lambda i: [body(SLOTS * i + slot, slot) for slot in range(SLOTS)], chain, peel_last=True)

        def exists(i):
            return not isinstance(i, int) or i < DEC_BATCH

        with nc.Block() as block:

            @block.sync
            def _(sp):
                def load(i2):
                    for slot in range(SLOTS):
                        i = SLOTS * i2 + slot
                        if not below(i, 1):
                            wait(sp, turned, i * B_PAIRS)
                            sp.dma_start(k[:, :, :], kc[i]).then_inc(k_loaded, 16)
                        if not below(i, 1):
                            wait(sp, small_turned, 2 * i)
                        sp.dma_start(small[:, 0], kn_d[i]).then_inc(kn_loaded, 16)
                        sp.dma_start(small[:, 1], qn_d[i]).then_inc(qn_loaded, 16)
                        if not below(i, SLOTS):
                            wait(sp, pv_ready, (i - 1) * HALVES)
                        sp.dma_start(v[:, slot], vc[i]).then_inc(v_loaded[slot], 16)
                        sp.dma_start(vn[:, slot], vn_d[i]).then_inc(vn_loaded[slot], 16)
                        for e in range(HALVES):
                            sp.dma_start(ncum[:, slot, e, :], ncd_d[i, 8 * e:8 * e + 8].rearrange("h q k -> (h q) k")).then_inc(nc_loaded[slot], 16)

                wait(sp, g.late_stored, 16 * (2 + DEC_BATCH))
                run(sp, DEC_BATCH // SLOTS, load)

            @block.gpsimd
            def _(pool):
                pool.memset(qb[:, :, :], 0.0).then_inc(filled, 1)

                def store(i):
                    for e in range(HALVES):
                        wait(pool, o_done, i * HALVES + e + 1)
                        pool.dma_start(half_d[i, e], o[:, e, :]).then_inc(stored[e], 16)
                    if not below(i, 1):
                        move(i - 1)

                def move(i):
                    for e in range(HALVES):
                        wait(pool, stored[e], i * 16 + 16)
                    pool.dma_start(o_d[NT - 1, bass.ds(i * NS, NS), :].rearrange("q (h d) -> h q d", d=B_HD),
                                   half_d[i].rearrange("e (h q) d -> (e h) q d", q=NS)).then_inc(moved, 16)

                run(pool, DEC_BATCH, store)
                move(DEC_BATCH - 1)
                wait(pool, moved, 16 * DEC_BATCH)

            @block.tensor
            def _(pe):
                def turn_k(i, j0):
                    if j0 == 0:
                        if below(i, 1):
                            pe.wait_ge(g.run_k_loaded, 16)
                        else:
                            pe.wait_ge(k_loaded, i * 16)
                    for j in range(j0, j0 + JH):
                        if j >= 2 or not below(i, 1):
                            pe.wait_ge(copied, i * B_PAIRS + j - 1)
                        for t in range(PAST_T):
                            ins = pe.transpose(tb[j % 2][:, t, :], k[:, t, j * P:(j + 1) * P], g.ident[:, :])
                        ins.then_inc(turned, 1)

                def turn_small(i, part):
                    loaded, used = ((kn_loaded, qn_copied), (qn_loaded, kn_copied))[part]
                    pe.wait_ge(loaded, i * 16 + 16)
                    if part or not below(i, 1):
                        pe.wait_ge(used, i + part)
                    settle(pe, pe_settled)
                    for j in range(B_PAIRS):
                        ins = pe.transpose(small_p[:, j * NS:(j + 1) * NS], small[:, part, j * P:(j + 1) * P], g.ident[0:NS, 0:NS])
                    ins.then_inc(small_turned, 1)

                def scores(i, slot, e):
                    u = i * HALVES + e
                    if e == 0:
                        pe.wait_ge(copied, i * B_PAIRS + B_PAIRS)
                        pe.wait_ge(kn_copied, i + 1)
                        pe.wait_ge(qn_copied, i + 1)
                    if not below(u, 1):
                        pe.wait_ge(shifted, u)
                    for n in range(JH):
                        pe.matmul(ps[32 * n:32 * n + 32, 0:PAST], qb[:, JH * e + n, :], kt[:, slot, JH * e + n, :], start=True, stop=True)
                    for n in range(JH):
                        rows = slice(32 * n, 32 * n + 32)
                        pe.matmul(ps[rows, CB:CB + NS], qb[:, JH * e + n, :], ktn[:, JH * e + n, :], start=True, stop=False)
                        ins = pe.matmul(ps[rows, CB:CB + NS], g.ident[:, rows], g.mask_new[:, :], start=False, stop=True)
                    ins.then_inc(scores_ready, 1)

                def turn(i, e):
                    u = i * HALVES + e
                    pe.wait_ge(exp_done, u + 1)
                    if not below(u, 1):
                        pe.wait_ge(p_copied, 2 * u)
                    for t in range(PAST_T):
                        ins = pe.transpose(tp[0][:, t, :], prob[:, e, t * P:(t + 1) * P], g.ident[:, :])
                    ins.then_inc(p_turned, 1)
                    pe.transpose(tp[1][0:NS, 0, :], prob[:, e, PAST:DK], g.ident[:, :]).then_inc(p_turned, 1)

                def weigh(i, slot, e):
                    u = i * HALVES + e
                    pe.wait_ge(p_copied, 2 * u + 2)
                    if not below(u, 1):
                        pe.wait_ge(o_done, u)
                    if e == 0:
                        pe.wait_ge(v_loaded[slot], (i - slot) * 8 + 16)
                        pe.wait_ge(vn_loaded[slot], (i - slot) * 8 + 16)
                    for n in range(JH):
                        rows, cols = slice(32 * n, 32 * n + 32), slice((JH * e + n) * P, (JH * e + n + 1) * P)
                        for t in range(PAST_T):
                            pe.matmul(po[rows, :], pt[:, e, t, rows], v[:, slot, t, cols], start=(t == 0), stop=False)
                        ins = pe.matmul(po[rows, :], ptn[:, e, rows], vn[:, slot, cols], start=False, stop=True)
                    ins.then_inc(pv_ready, 1)

                def stream(i, slot):
                    more = exists(i + 1)
                    scores(i, slot, 0)
                    if more:
                        turn_k(i + 1, 0)
                    scores(i, slot, 1)
                    if more:
                        turn_k(i + 1, JH)
                    turn(i, 0)
                    if more:
                        turn_small(i + 1, 0)
                    turn(i, 1)
                    weigh(i, slot, 0)
                    if more:
                        turn_small(i + 1, 1)
                    weigh(i, slot, 1)

                turn_k(0, 0)
                turn_k(0, JH)
                turn_small(0, 0)
                turn_small(0, 1)
                streams(pe, stream)

            @block.scalar
            def _(act):
                def copy_k(i, slot, j0):
                    for j in range(j0, j0 + JH):
                        act.wait_ge(turned, i * B_PAIRS + j + 1)
                        if j == 0 and not below(i, SLOTS):
                            act.wait_ge(scores_ready, (i - 1) * HALVES)
                        act.activation(kt[:, slot, j, :], tb[j % 2][:, :, :].rearrange("p t n -> p (t n)"), ACT.Copy).then_inc(copied, 1)

                def copy_new_k(i):
                    act.wait_ge(small_turned, 2 * i + 1)
                    if not below(i, 1):
                        act.wait_ge(scores_ready, i * HALVES)
                    act.activation(ktn[:, :, :], small_p[:, 0:B_PAIRS * NS].rearrange("p (j n) -> p j n", n=NS), ACT.Copy).then_inc(kn_copied, 1)

                def exponential(i, e):
                    u = i * HALVES + e
                    act.wait_ge(max_done, u + 1)
                    if not below(u, HALVES):
                        act.wait_ge(o_done, u - 1)
                    act.activation(prob[:, e, :], prob[:, e, :], ACT.Exp, bias=mx[:, e:e + 1], accum_out=rs[:, e:e + 1]).then_inc(exp_done, 1)

                def stream(i, slot):
                    more = exists(i + 1)
                    if more:
                        copy_k(i + 1, 1 - slot, 0)
                    exponential(i, 0)
                    if more:
                        copy_k(i + 1, 1 - slot, JH)
                    exponential(i, 1)
                    if more:
                        copy_new_k(i + 1)

                copy_k(0, 0, 0)
                copy_k(0, 0, JH)
                copy_new_k(0)
                streams(act, stream)

            @block.vector
            def _(dve):
                c = Chain(dve, chain_sem)

                def copy_new_q(i):
                    dve.wait_ge(small_turned, 2 * i + 2)
                    dve.wait_ge(filled, 1)
                    for half in range(2):
                        rows = slice(half * B_HD, (half + 1) * B_HD)
                        ins = dve.tensor_copy(qb[rows, :, half * NS:(half + 1) * NS], small_p[rows, 0:B_PAIRS * NS].rearrange("p (j n) -> p j n", n=NS))
                        if half == 0:
                            c.link(ins)
                    ins.then_inc(qn_copied, 1)

                def shift(i, slot, e):
                    u = i * HALVES + e
                    dve.wait_ge(scores_ready, u + 1)
                    dve.wait_ge(nc_loaded[slot], (i - slot) * 16 + 32)
                    if not below(u, HALVES):
                        dve.wait_ge(p_turned, 2 * u - 2)
                    settle(dve, settled)
                    dve.tensor_tensor_reduce(out=prob[:, e, :], in0=ps[:, 0:DK], in1=ncum[:, slot, e, :], scale=1.0, scalar=-3e38,
                                             op0=ALU.add, op1=ALU.max, accum_out=mx[:, e:e + 1]).then_inc(shifted, 1)
                    dve.wait_ge(shifted, u + 1)
                    dve.tensor_scalar(mx[:, e:e + 1], mx[:, e:e + 1], -1.0, None, ALU.mult).then_inc(max_done, 1)

                def copy_probs(i, e):
                    u = i * HALVES + e
                    dve.wait_ge(p_turned, 2 * u + 1)
                    dve.tensor_copy(pt[:, e], tp[0][:, :, :]).then_inc(p_copied, 1)
                    dve.wait_ge(p_turned, 2 * u + 2)
                    dve.tensor_copy(ptn[:, e], tp[1][0:NS, 0, :]).then_inc(p_copied, 1)

                def scale_out(i, e):
                    u = i * HALVES + e
                    c.link(dve.reciprocal(rinv[:, e:e + 1], rs[:, e:e + 1]))
                    c.link(dve.tensor_scalar(sel[:, e, :], g.parity[:, :], rinv[:, e:e + 1], None, ALU.mult))
                    dve.wait_ge(pv_ready, u + 1)
                    if not below(i, 1):
                        dve.wait_ge(stored[e], i * 16)
                    c.link(dve.tensor_scalar(o[:, e, :], po[:, 0:B_HD], sel[:, e, 0:1], None, ALU.mult))
                    dve.scalar_tensor_tensor(o[:, e, :], po[:, B_HD:P], sel[:, e, 1:2], o[:, e, :], ALU.mult, ALU.add).then_inc(o_done, 1)

                def stream(i, slot):
                    shift(i, slot, 0)
                    shift(i, slot, 1)
                    copy_probs(i, 0)
                    copy_probs(i, 1)
                    scale_out(i, 0)
                    if exists(i + 1):
                        copy_new_q(i + 1)
                    scale_out(i, 1)

                copy_new_q(0)
                streams(dve, stream, c)


def build(nc, A, O):
    (y_prompt, y_sample, k_prompt, v_prompt, logf_prompt, c_prompt, n_prompt, m_prompt,
     k_sample, v_sample, logf_sample, c_sample, n_sample, m_sample) = O

    def scratch(name, shape):
        return nc.dram_tensor(name, shape, fp32, kind="Internal").ap()

    qkvo = scratch("qkvo", (NT, P, A_O0 + A_H * A_V))
    gates_d = scratch("mlstm_gates_rows", (2 * A_H, T_ALL))
    h_d = scratch("mlstm_h", (NT, P, D))
    fgates_d = scratch("fox_gates_rows", (B_H, T_ALL))
    q_d, sg_d, o_d = scratch("fox_q", (NT, P, D)), scratch("fox_out_gate", (NT, P, D)), scratch("fox_o", (NT, P, D))
    ncp_d = scratch("neg_cum_prompt", (B_H, SEQ))
    ncd_d = scratch("neg_cum_running", (DEC_BATCH, B_H, DEC_SEQ, DK))
    half_d = scratch("fox_o_running", (DEC_BATCH, 2, P, B_HD))

    class Globals:
        pass

    g = Globals()
    with Scope(nc, "g") as top:
        g.x = top.sb("x", [P, NT, D])
        g.ident = top.sb("ident", [P, P])
        g.x_loaded = [top.sem(f"x_loaded{t}") for t in range(NT)]
        g.one = top.sb("one", [P, 1])
        g.mask_kq, g.mask_qk = top.sb("mask_kq", [P, 2, P]), top.sb("mask_qk", [P, P])
        x_sample = A["x_sample"].rearrange("s t d -> (s t) d")
        g.x_tile = lambda t: A["x_prompt"][0, t * P:(t + 1) * P, :] if t < NP else x_sample
        setup(nc, g)
        with Scope(nc, "A1") as s:
            xth, xtl = s.sb("xth", [P, KC, T_ALL], fp32r), s.sb("xtl", [P, KC, T_ALL], fp32r)
            linear(nc, g, xth, xtl, "w_in", A["w_in_a"][0],
                   [(0, 4, "store", lambda b, t: qkvo[t, :, bass.ds(b * CB, CB)]),
                    (A_O0, 2, "sigmoid", lambda b, t: qkvo[t, :, bass.ds(A_O0 + b * CB, CB)])],
                   gates=(A_O0 + A_H * A_V, 2 * A_H, gates_d), kind="norm", gain_row=A["g_mix"][0:1, :], x_arrives=True)
        with Scope(nc, "A2") as s:
            g.sel, g.pair_sel = s.sb("sel", [A_H, A_H, P]), s.sb("pair_sel", [A_H, A_PAIRS, 2, A_QK])
            g.own, g.ones8 = s.sb("own", [P, DEC_BATCH]), s.sb("ones8", [A_H, P])
            g.mask_dec = s.sb("mask_dec", [P, 2, P])
            g.ident_r, g.sel_r = s.sb("ident_r", [P, P], fp32r), s.sb("sel_r", [A_H, A_H, P], fp32r)
            g.Bh, g.Bl = s.sb("B_high", [A_H, T_ALL], fp32r), s.sb("B_low", [A_H, T_ALL], fp32r)
            g.B, g.tok = s.sb("B", [A_H, T_ALL]), s.sb("tok", [P, NT, 4, A_H])
            g.gc_pair, g.gc_dec, g.gc_s = s.sb("gc_pair", [P, A_PAIRS, NP]), s.sb("gc_dec", [P, A_H, DEC_BATCH]), s.sb("gc_s", [DEC_BATCH, A_H])
            g.cold = s.sb("cold", [P, A_H, DEC_BATCH, A_QK])
            g.nload, g.nold = s.sb("nload", [DEC_BATCH // 2 * A_H, P]), s.sb("nold", [DEC_BATCH, A_H * A_QK])
            g.c_loaded, g.n_loaded = s.sem("c_loaded"), s.sem("n_loaded")
            mlstm_gates(nc, g, gates_d, A["b_i_a"], A["b_f_a"], A["state_m"], m_prompt, m_sample)
            mlstm(nc, g, qkvo, h_d, False, c_prompt, n_prompt, A["state_c"], A["state_n"])
            mlstm(nc, g, qkvo, h_d, True, c_sample, n_sample)
        with Scope(nc, "A3") as s:
            xth, xtl = s.sb("xth", [P, KC, T_ALL], fp32r), s.sb("xtl", [P, KC, T_ALL], fp32r)
            linear(nc, g, xth, xtl, "w_out", A["w_out_a"][0], [(0, 2, "residual", None)],
                   kind="mlstm", a=h_d, b=qkvo[:, :, A_O0:A_O0 + D], gain_row=A["g_head_a"])
            ffn(nc, g, xth, xtl, "ffn0", A["w_gu"][0], A["w_down"][0], A["g_ffn"][0:1, :])

            def rows(prompt, sample):
                pv, sv = prompt.rearrange("o (t p) h d -> (o t) p (h d)", p=P), sample.rearrange("s t h d -> (s t) (h d)")
                return lambda b, t: (pv[t] if t < NP else sv)[:, bass.ds(b * CB, CB)]

            linear(nc, g, xth, xtl, "w_kvf", A["w_kvf"],
                   [(0, 2, ("norm", A["g_k"].rearrange("(o d) -> o d", o=1), 1.0), rows(k_prompt, k_sample)),
                    (D, 2, "store", rows(v_prompt, v_sample))], gates=(2 * D, B_H, fgates_d),
                   kind="norm", gain_row=A["g_kv"].rearrange("(o d) -> o d", o=1))
            linear(nc, g, xth, xtl, "w_qg", A["w_qg_b"][0],
                   [(0, 2, ("norm", A["g_q_b"], B_HD ** -0.5), lambda b, t: q_d[t, :, bass.ds(b * CB, CB)]),
                    (D, 2, "sigmoid", lambda b, t: sg_d[t, :, bass.ds(b * CB, CB)])],
                   kind="norm", gain_row=A["g_mix"][1:2, :])
        with Scope(nc, "B1") as s:
            g.own, g.parity, g.mask_new = s.sb("own", [P, DEC_BATCH]), s.sb("parity", [P, 2]), s.sb("mask_new", [P, DEC_SEQ])
            g.ncd, g.logf_out, g.late_stored = s.sb("ncd", [B_H, DEC_BATCH, DK]), s.sb("logf_out", [P, NT, B_H]), s.sem("late_stored")
            g.run_k, g.run_k_loaded = s.sb("run_k", [P, PAST_T, D]), s.sem("run_k_loaded")
            fox_gates(nc, g, fgates_d, A["b_f_b"], A["cache_logf"], logf_prompt, logf_sample, ncp_d, ncd_d)
            fox_prompt(nc, g, q_d, k_prompt.rearrange("o t h d -> (o t) (h d)"), v_prompt.rearrange("o t h d -> (o t) (h d)"), ncp_d, o_d, A["cache_k"])
            fox_running(nc, g, q_d, A["cache_k"], A["cache_v"], k_sample, v_sample, ncd_d, half_d, o_d)
        with Scope(nc, "B2") as s:
            xth, xtl = s.sb("xth", [P, KC, T_ALL], fp32r), s.sb("xtl", [P, KC, T_ALL], fp32r)
            linear(nc, g, xth, xtl, "w_o", A["w_o_b"][0], [(0, 2, "residual", None)], kind="gated", a=o_d, b=sg_d)
            ffn(nc, g, xth, xtl, "ffn1", A["w_gu"][1], A["w_down"][1], A["g_ffn"][1:2, :],
                out=lambda t: y_prompt[0, t * P:(t + 1) * P, :] if t < NP else y_sample.rearrange("s t d -> (s t) d"))


_INS = ['x_prompt', 'x_sample', 'cache_k', 'cache_v', 'cache_logf', 'state_c', 'state_n', 'state_m', 'g_mix', 'g_ffn',
        'w_in_a', 'b_i_a', 'b_f_a', 'g_head_a', 'w_out_a', 'g_kv', 'w_kvf', 'b_f_b', 'g_k', 'w_qg_b', 'g_q_b', 'w_o_b',
        'w_gu', 'w_down']
_OUTS = [(1, SEQ, D), (DEC_BATCH, DEC_SEQ, D), (1, SEQ, B_H, B_HD), (1, SEQ, B_H, B_HD), (1, SEQ, B_H),
         (1, 1, A_H, A_V, A_QK), (1, 1, A_H, A_QK), (1, 1, A_H),
         (DEC_BATCH, DEC_SEQ, B_H, B_HD), (DEC_BATCH, DEC_SEQ, B_H, B_HD), (DEC_BATCH, DEC_SEQ, B_H),
         (DEC_BATCH, 1, A_H, A_V, A_QK), (DEC_BATCH, 1, A_H, A_QK), (DEC_BATCH, 1, A_H)]


def kernel(**inputs):
    import numpy as _np
    import concourse.bacc as _bacc
    from concourse import mybir as _mybir
    from concourse.bass_utils import run_bass_kernel_spmd as _run

    nc = _bacc.Bacc("TRN2", target_bir_lowering=False, num_devices=1)
    arrays, args = {}, {}
    for name in _INS:
        a = _np.ascontiguousarray(inputs[name])
        arrays[f"in_{name}_dram"] = a
        args[name] = nc.dram_tensor(f"in_{name}_dram", a.shape, _mybir.dt.from_np(a.dtype), kind="ExternalInput").ap()
    outs = [nc.dram_tensor(f"out_{i}_dram", shape, _mybir.dt.float32, kind="ExternalOutput").ap() for i, shape in enumerate(_OUTS)]
    build(nc, args, outs)
    r = _run(nc, [arrays], core_ids=[0])
    return tuple(r.results[0][f"out_{i}_dram"] for i in range(len(_OUTS)))
```
